# Optimizing a Trainium2 kernel written in Bass

```python
import functools
import jax, jax.numpy as jnp
from jax import lax
import numpy as np

D_MODEL = 1024
BATCH = 1
SEQ = 1024
DEPTH = 1
DEC_BATCH = 8
DEC_SEQ = 8
PAST_LEN = 256
PAGE_SIZE = 128

BRANCH_W = D_MODEL // 2
GLA_H = 4
GLA_DK = BRANCH_W // (2 * GLA_H)
GLA_DV = BRANCH_W // GLA_H
GLA_LR = 16
GLA_TAU = 16.0
GLA_CHUNK = 64
FOX_HD = 64
FOX_H = BRANCH_W // FOX_HD
FOX_QBLK = 128
CONV_D = BRANCH_W
CONV_W = 3
N_BRANCH = 3
N_EXPERTS = 16
N_GROUPS = 4
EXP_PER_GROUP = N_EXPERTS // N_GROUPS
TOP_K = 2
D_EXPERT = D_MODEL // 4
LN_EPS = 1e-5
DEEPNORM_ALPHA = (2 * DEPTH) ** 0.25
DEEPNORM_BETA = (8 * DEPTH) ** -0.25

IN_SPLITS = (
    ('gla_q', GLA_H * GLA_DK), ('gla_k', GLA_H * GLA_DK), ('gla_v', GLA_H * GLA_DV),
    ('gla_a', GLA_LR), ('gla_r', GLA_H * GLA_DV),
    ('fox_q', FOX_H * FOX_HD), ('fox_k', FOX_H * FOX_HD), ('fox_v', FOX_H * FOX_HD),
    ('fox_f', FOX_H),
    ('conv_b', CONV_D), ('conv_c', CONV_D), ('conv_h', CONV_D),
    ('gate', N_BRANCH * D_MODEL),
)
D_IN = sum(n for _, n in IN_SPLITS)

kernel_name = 'hybrid_gla_fox_conv_moe_step'

def _split_in(proj):
    out = {}
    off = 0
    for name, n in IN_SPLITS:
        out[name] = proj[..., off:off + n]
        off += n
    return out

def _layernorm(x, g, b):
    xf = x.astype(jnp.float32)
    mu = jnp.mean(xf, -1, keepdims=True)
    var = jnp.mean(jnp.square(xf - mu), -1, keepdims=True)
    return ((xf - mu) * lax.rsqrt(var + LN_EPS) * g + b).astype(x.dtype)

def _gla_chunked(q, k, v, log_a, s0):
    B, T, H, DK = q.shape
    DV = v.shape[-1]
    C = GLA_CHUNK if T % GLA_CHUNK == 0 else T
    N = T // C
    f32 = jnp.float32
    qf = q.astype(f32).reshape(B, N, C, H, DK)
    kf = k.astype(f32).reshape(B, N, C, H, DK)
    vf = v.astype(f32).reshape(B, N, C, H, DV)
    b = jnp.cumsum(log_a.astype(f32).reshape(B, N, C, H, DK), axis=2)
    b_last = b[:, :, -1:]
    q_in = qf * jnp.exp(b)
    k_in = kf * jnp.exp(-b)
    k_end = kf * jnp.exp(b_last - b)
    causal = jnp.tril(jnp.ones((C, C), dtype=bool))
    att = jnp.where(causal, jnp.einsum('bnthk,bnshk->bnhts', q_in, k_in), 0.0)
    o_intra = jnp.einsum('bnhts,bnshv->bnthv', att, vf)
    ds = jnp.einsum('bnshk,bnshv->bnhkv', k_end, vf)
    decay = jnp.exp(b_last[:, :, 0])

    def step(S, inp):
        d, dS = inp
        return d[..., None] * S + dS, S

    s_fin, s_start = lax.scan(step, s0.astype(f32),
                              (jnp.moveaxis(decay, 1, 0), jnp.moveaxis(ds, 1, 0)))
    o_inter = jnp.einsum('bnthk,nbhkv->bnthv', q_in, s_start)
    return (o_intra + o_inter).reshape(B, T, H, DV), s_fin

def _fox_block(q_blk, cq_blk, qpos, k, v, ckT, kpos):
    s = jnp.einsum('bqhd,bkhd->bhqk', q_blk, k, preferred_element_type=jnp.float32) * (FOX_HD ** -0.5)
    s = s + (jnp.swapaxes(cq_blk, 1, 2)[..., :, None] - ckT[..., None, :])
    s = jnp.where(kpos[None, :] <= qpos[:, None], s, -jnp.inf)
    p = jax.nn.softmax(s, axis=-1)
    return jnp.einsum('bhqk,bkhd->bqhd', p.astype(v.dtype), v)

def _fox_prompt(q, k, v, logf):
    B, T, H, _ = q.shape
    c = jnp.cumsum(logf, axis=1)
    ckT = jnp.swapaxes(c, 1, 2)
    nb = T // FOX_QBLK
    pos = jnp.arange(T)
    qb = jnp.swapaxes(q.reshape(B, nb, FOX_QBLK, H, FOX_HD), 0, 1)
    cb = jnp.swapaxes(c.reshape(B, nb, FOX_QBLK, H), 0, 1)
    qposb = pos.reshape(nb, FOX_QBLK)
    o = lax.map(lambda a: _fox_block(a[0], a[1], a[2], k, v, ckT, pos), (qb, cb, qposb))
    return jnp.swapaxes(o, 0, 1).reshape(B, T, H, FOX_HD)

def _fox_sample(q, k, v, logf, k_pool, v_pool, logf_pool, page_table):
    DB, T = q.shape[:2]
    past = page_table.shape[1] * PAGE_SIZE
    k_past = jnp.take(k_pool, page_table, axis=0).reshape(DB, past, FOX_H, FOX_HD)
    v_past = jnp.take(v_pool, page_table, axis=0).reshape(DB, past, FOX_H, FOX_HD)
    lf_past = jnp.take(logf_pool, page_table, axis=0).reshape(DB, past, FOX_H)
    k_all = jnp.concatenate([k_past.astype(k.dtype), k], axis=1)
    v_all = jnp.concatenate([v_past.astype(v.dtype), v], axis=1)
    c = jnp.cumsum(jnp.concatenate([lf_past.astype(jnp.float32), logf], axis=1), axis=1)
    kpos = jnp.arange(past + T)
    qpos = past + jnp.arange(T)
    return _fox_block(q, c[:, past:], qpos, k_all, v_all, jnp.swapaxes(c, 1, 2), kpos)

def _short_conv(u, buf, w):
    T = u.shape[1]
    full = jnp.concatenate([buf.astype(u.dtype), u], axis=1)
    y = w[0] * full[:, 0:T]
    for j in range(1, CONV_W):
        y = y + w[j] * full[:, j:j + T]
    return y, full[:, T:]

def _moe(x, w_router, b_router, w_gate, w_up, w_down):
    B, T, D = x.shape
    t = x.reshape(B * T, D)
    logits = jnp.einsum('nd,de->ne', t, w_router, preferred_element_type=jnp.float32) + b_router.astype(jnp.float32)
    probs = jax.nn.softmax(logits, axis=-1)
    grouped = probs.reshape(-1, N_GROUPS, EXP_PER_GROUP)
    gscore = lax.top_k(grouped, TOP_K)[0].sum(-1)
    gsel = jnp.argmax(gscore, axis=-1)
    in_grp = jnp.arange(N_GROUPS)[None, :] == gsel[:, None]
    masked = jnp.where(in_grp[:, :, None], grouped, -1.0).reshape(-1, N_EXPERTS)
    vals, idx = lax.top_k(masked, TOP_K)
    wts = vals / jnp.sum(vals, -1, keepdims=True)
    gate = jnp.einsum('nke,nk->ne', jax.nn.one_hot(idx, N_EXPERTS, dtype=jnp.float32), wts)
    h = jax.nn.silu(jnp.einsum('nd,edf->nef', t, w_gate)) * jnp.einsum('nd,edf->nef', t, w_up)
    h = h * gate[:, :, None].astype(h.dtype)
    return jnp.einsum('nef,efd->nd', h, w_down).reshape(B, T, D)

def _layer(x, w_in, w_gla_a2, b_gla_a, gla_norm_g, b_fox_f, conv_w, w_branch, w_out,
           ln1_g, ln1_b, w_router, b_router, w_e_gate, w_e_up, w_e_down, ln2_g, ln2_b,
           gla_s0, conv_buf, fox_fn):
    B, T, _ = x.shape
    p = _split_in(jnp.einsum('btd,dn->btn', x, w_in))
    gq = p['gla_q'].reshape(B, T, GLA_H, GLA_DK) * (GLA_DK ** -0.5)
    gk = p['gla_k'].reshape(B, T, GLA_H, GLA_DK)
    gv = p['gla_v'].reshape(B, T, GLA_H, GLA_DV)
    a_pre = jnp.einsum('btr,rk->btk', p['gla_a'], w_gla_a2) + b_gla_a
    log_a = (jax.nn.log_sigmoid(a_pre.astype(jnp.float32)) / GLA_TAU).reshape(B, T, GLA_H, GLA_DK)
    o, gla_state = _gla_chunked(gq, gk, gv, log_a, gla_s0)
    o = o * lax.rsqrt(jnp.mean(o * o, -1, keepdims=True) + LN_EPS) * gla_norm_g.reshape(GLA_H, GLA_DV)
    o_gla = (o.reshape(B, T, -1) * jax.nn.silu(p['gla_r'].astype(jnp.float32))).astype(x.dtype)
    fq = p['fox_q'].reshape(B, T, FOX_H, FOX_HD)
    fk = p['fox_k'].reshape(B, T, FOX_H, FOX_HD)
    fv = p['fox_v'].reshape(B, T, FOX_H, FOX_HD)
    logf = jax.nn.log_sigmoid((p['fox_f'] + b_fox_f).astype(jnp.float32))
    o_fox = fox_fn(fq, fk, fv, logf).reshape(B, T, -1).astype(x.dtype)
    u = p['conv_c'] * p['conv_h']
    y, conv_state = _short_conv(u, conv_buf, conv_w)
    o_conv = (p['conv_b'] * y).astype(x.dtype)
    ob = jnp.stack([o_gla, o_fox, o_conv], axis=2)
    br = jnp.einsum('btjc,jcd->btjd', ob, w_branch)
    g = jax.nn.sigmoid(p['gate'].reshape(B, T, N_BRANCH, D_MODEL))
    mix = jnp.einsum('btd,de->bte', jnp.sum(g * br, axis=2), w_out)
    x = _layernorm(DEEPNORM_ALPHA * x + mix, ln1_g, ln1_b)
    x = _layernorm(DEEPNORM_ALPHA * x + _moe(x, w_router, b_router, w_e_gate, w_e_up, w_e_down), ln2_g, ln2_b)
    return x, (fk, fv, logf, gla_state, conv_state)

def setup_inputs(seed: int = 0) -> dict:
    key = jax.random.key(seed)
    ks = jax.random.split(key, 32)
    f32 = jnp.float32
    n_pages = PAST_LEN // PAGE_SIZE
    n_pool = (DEC_BATCH * n_pages * 5 + 3) // 4

    def nrm(k, shape, scale=1.0):
        return jax.random.normal(k, shape, f32) * scale

    page_table = jax.random.permutation(ks[0], n_pool)[:DEC_BATCH * n_pages].reshape(DEC_BATCH, n_pages).astype(jnp.int32)
    return {
        'x_prompt': nrm(ks[1], (BATCH, SEQ, D_MODEL)),
        'x_sample': nrm(ks[2], (DEC_BATCH, DEC_SEQ, D_MODEL)),
        'cache_fox_k': nrm(ks[3], (DEPTH, n_pool, PAGE_SIZE, FOX_H, FOX_HD)),
        'cache_fox_v': nrm(ks[4], (DEPTH, n_pool, PAGE_SIZE, FOX_H, FOX_HD)),
        'cache_fox_logf': jax.nn.log_sigmoid(4.0 + nrm(ks[5], (DEPTH, n_pool, PAGE_SIZE, FOX_H), 1.5)),
        'state_gla': nrm(ks[6], (DEPTH, DEC_BATCH, GLA_H, GLA_DK, GLA_DV)),
        'state_conv': nrm(ks[7], (DEPTH, DEC_BATCH, CONV_W - 1, CONV_D)),
        'page_table': page_table,
        'w_in': nrm(ks[8], (DEPTH, D_MODEL, D_IN), D_MODEL ** -0.5),
        'w_gla_a2': nrm(ks[9], (DEPTH, GLA_LR, GLA_H * GLA_DK), GLA_LR ** -0.5),
        'b_gla_a': nrm(ks[10], (DEPTH, GLA_H * GLA_DK), 0.1),
        'gla_norm_g': 1.0 + nrm(ks[11], (DEPTH, GLA_H * GLA_DV), 0.02),
        'b_fox_f': jax.random.uniform(ks[12], (DEPTH, FOX_H), f32, 1.0, 7.0),
        'conv_w': nrm(ks[13], (DEPTH, CONV_W, CONV_D), CONV_W ** -0.5),
        'w_branch': nrm(ks[14], (DEPTH, N_BRANCH, BRANCH_W, D_MODEL), DEEPNORM_BETA * BRANCH_W ** -0.5),
        'w_out': nrm(ks[15], (DEPTH, D_MODEL, D_MODEL), DEEPNORM_BETA * D_MODEL ** -0.5),
        'ln1_g': 1.0 + nrm(ks[16], (DEPTH, D_MODEL), 0.02),
        'ln1_b': nrm(ks[17], (DEPTH, D_MODEL), 0.02),
        'w_router': nrm(ks[18], (D_MODEL, N_EXPERTS), D_MODEL ** -0.5),
        'b_router': nrm(ks[19], (N_EXPERTS,), 0.01),
        'w_e_gate': nrm(ks[20], (DEPTH, N_EXPERTS, D_MODEL, D_EXPERT), D_MODEL ** -0.5),
        'w_e_up': nrm(ks[21], (DEPTH, N_EXPERTS, D_MODEL, D_EXPERT), D_MODEL ** -0.5),
        'w_e_down': nrm(ks[22], (DEPTH, N_EXPERTS, D_EXPERT, D_MODEL), DEEPNORM_BETA * D_EXPERT ** -0.5),
        'ln2_g': 1.0 + nrm(ks[23], (DEPTH, D_MODEL), 0.02),
        'ln2_b': nrm(ks[24], (DEPTH, D_MODEL), 0.02),
    }

def reference(x_prompt, x_sample, cache_fox_k, cache_fox_v, cache_fox_logf, state_gla, state_conv,
              page_table, w_in, w_gla_a2, b_gla_a, gla_norm_g, b_fox_f, conv_w, w_branch, w_out,
              ln1_g, ln1_b, w_router, b_router, w_e_gate, w_e_up, w_e_down, ln2_g, ln2_b):
    B = x_prompt.shape[0]
    xp, xs = x_prompt, x_sample
    pk, pv, plf, pgla, pconv = [], [], [], [], []
    sk, sv, slf, sgla, sconv = [], [], [], [], []
    for l in range(DEPTH):
        wl = (w_in[l], w_gla_a2[l], b_gla_a[l], gla_norm_g[l], b_fox_f[l], conv_w[l], w_branch[l],
              w_out[l], ln1_g[l], ln1_b[l], w_router, b_router, w_e_gate[l], w_e_up[l], w_e_down[l],
              ln2_g[l], ln2_b[l])
        xp, st_p = _layer(xp, *wl,
                          jnp.zeros((B, GLA_H, GLA_DK, GLA_DV), jnp.float32),
                          jnp.zeros((B, CONV_W - 1, CONV_D), xp.dtype),
                          _fox_prompt)
        fox_s = functools.partial(_fox_sample, k_pool=cache_fox_k[l], v_pool=cache_fox_v[l],
                                  logf_pool=cache_fox_logf[l], page_table=page_table)
        xs, st_s = _layer(xs, *wl, state_gla[l], state_conv[l], fox_s)
        pk.append(st_p[0]); pv.append(st_p[1]); plf.append(st_p[2]); pgla.append(st_p[3]); pconv.append(st_p[4])
        sk.append(st_s[0]); sv.append(st_s[1]); slf.append(st_s[2]); sgla.append(st_s[3]); sconv.append(st_s[4])
    return (xp, xs,
            jnp.stack(pk), jnp.stack(pv), jnp.stack(plf), jnp.stack(pgla), jnp.stack(pconv),
            jnp.stack(sk), jnp.stack(sv), jnp.stack(slf), jnp.stack(sgla), jnp.stack(sconv))


_drawn_inputs = setup_inputs


def setup_inputs(seed=0):
    import zlib

    import numpy as np

    out = dict(_drawn_inputs(seed))
    spreads = {}
    factors = {'cache_fox_logf': 21.074,
     'gla_norm_g': 8.0,
     'ln2_g': 8.45,
     'ln2_b': 8.272,
     'b_router': 3.341}
    for name, (base, spread) in spreads.items():
        noise = np.random.default_rng([zlib.crc32(name.encode()), seed]).standard_normal(out[name].shape)
        drawn = base * np.exp(spread * noise) if base else spread * noise
        out[name] = __import__('jax').numpy.asarray(drawn.astype(out[name].dtype))
    for name, factor in factors.items():
        out[name] = (out[name] * factor).astype(out[name].dtype)
    return out
```

```python
from contextlib import ExitStack

import concourse.bass as bass
import numpy as np
from concourse import mybir

F32 = mybir.dt.float32
F32R = mybir.dt.float32r
I32 = mybir.dt.int32
U32 = mybir.dt.uint32
BF16 = mybir.dt.bfloat16
ALU = mybir.AluOpType
ACT = mybir.ActivationFunctionType
X = mybir.AxisListType.X

D = 1024
KC = D // 128
SEQ = 1024
DB, DT = 8, 8
TOK = SEQ + DB * DT
BW = 512
H_GLA, DK, DV = 4, 64, 128
LR = 16
H_FOX, HD = 8, 64
CHUNK = 64
PAGE = 128
NPAGE = 2
NE, NG, EPG = 16, 4, 4
DE = 256
EPS = 1e-5
ALPHA = 2.0 ** 0.25
NT = 9
GROUPS = [(0, 384), (384, 384), (768, 320)]
GQ, GK, GV, GA, GR = 0, 256, 512, 1024, 1040
FQ, FK, FV, FF = 1552, 2064, 2576, 3088
CB, CC, CH, GATE = 3096, 3608, 4120, 4632
BIG = 1.0e30


class Chain:

    def __init__(self, eng, sem, start=0):
        self.eng, self.sem, self.n = eng, sem, start

    def __call__(self, ins):
        ins.then_inc(self.sem, 1)
        self.n += 1
        self.eng.wait_ge(self.sem, self.n)


def clear(nc, sems):
    nums = sorted(s.num for s in sems)
    first = [n for n in nums if n - 1 not in nums]
    last = [n for n in nums if n + 1 not in nums]
    with nc.Block() as block:
        @block.sync
        def _(eng):
            for a, b in zip(first, last):
                eng.sem_clear(range(a, b + 1))


def f32(ap):
    return ap.bitcast(F32)


SLABS = [[CC + 128 * c, CH + 128 * c, CB + 128 * c] for c in range(4)]
for _p in range(2):
    SLABS += [[GQ + 128 * _p, GK + 128 * _p, GV + 256 * _p],
              [GV + 256 * _p + 128, GR + 256 * _p, GR + 256 * _p + 128]]
SLABS += [[FQ + 128 * p, FK + 128 * p, FV + 128 * p] for p in range(4)]
CONV0, GLA0, FOX0 = 0, 4, 8
N_SLAB = len(SLABS)


class Shared:
    pass


def load_slab(sh, eng, n):
    if n >= N_SLAB:
        return
    if n >= 1:
        eng.wait_ge(sh.w_split, n)
    for b in range(3):
        src = sh.w_in[0, :, SLABS[n][b]:SLABS[n][b] + 128].rearrange("(k p) n -> p k n", p=128)
        eng.dma_start(sh.w_raw[:, b], src).then_inc(sh.w_loaded, 16)


def head_slab(sh, eng, n):
    if n >= N_SLAB:
        return
    eng.wait_ge(sh.w_loaded, 48 * (n + 1))
    if n >= 2:
        eng.wait_ge(sh.fm_ready, 9 * (n - 1))
    eng.activation(sh.w_hi[:, n % 2], sh.w_raw[:], ACT.Copy).then_inc(sh.w_head, 1)


def tail_slab(sh, eng, n):
    if n >= N_SLAB:
        return
    eng.wait_ge(sh.w_head, n + 1)
    eng.tensor_tensor(sh.w_lo[:, n % 2], sh.w_raw[:], f32(sh.w_hi[:, n % 2]),
                      ALU.subtract).then_inc(sh.w_split, 1)


def project_slab(sh, eng, n):
    eng.wait_ge(sh.w_split, n + 1)
    for b in range(3):
        for g, (t0, tn) in enumerate(GROUPS):
            u = 9 * n + 3 * b + g
            if u >= 2:
                eng.wait_ge(sh.fm_free[u % 2], u // 2)
            out = sh.ps[:, u % 2, 0:tn]
            for k in range(KC):
                for j, (w, x) in enumerate(((sh.w_hi, sh.xh), (sh.w_hi, sh.xl), (sh.w_lo, sh.xh))):
                    last = eng.matmul(out, w[:, n % 2, b, k, :], x[:, k, t0:t0 + tn],
                                      start=(k == 0 and j == 0), stop=(k == KC - 1 and j == 2))
            last.then_inc(sh.fm_ready, 1)


def fm_unit(sh, n, b, g):
    u = 9 * n + 3 * b + g
    t0, tn = GROUPS[g]
    return sh.ps[:, u % 2, 0:tn], u + 1, sh.fm_free[u % 2], t0, tn


def stage_x(nc, sh):
    with ExitStack() as ctx:
        x_tm = ctx.enter_context(nc.sbuf_tensor("x_tm", [128, 3, D], F32))
        x_loaded = [sh.front_sem(f"x_loaded{i}") for i in range(3)]
        x_tr = sh.front_sem("x_transposed")
        x_head = sh.front_sem("x_head")
        x_tail = sh.front_sem("x_tail")
        const = sh.front_sem("x_const")
        block = ctx.enter_context(nc.Block())

        @block.sync
        def _(eng):
            for t in range(NT):
                if t >= 3:
                    eng.wait_ge(x_tr, 2 * (t - 2))
                n = 128 if t < 8 else 64
                src = sh.x_prompt[0, 128 * t:128 * t + 128, :] if t < 8 else \
                    sh.x_sample.rearrange("b t d -> (b t) d")
                eng.dma_start(x_tm[0:n, t % 3, :], src).then_inc(x_loaded[t % 3], 16)
                if t == 2:
                    load_slab(sh, eng, 0)

        @block.gpsimd
        def _(eng):
            ch = Chain(eng, const)
            ch(eng.memset(sh.ident[:, :], 0.0))
            ch(eng.affine_select(out=sh.ident[:, :], in_=sh.ident[:, :], compare_op=ALU.not_equal,
                                 fill=1.0, base=0, pattern=[[-1, 128]], channel_multiplier=1))

        @block.tensor
        def _(eng):
            eng.wait_ge(const, 2)
            for t in range(NT):
                n = 128 if t < 8 else 64
                eng.wait_ge(x_loaded[t % 3], 16 * (t // 3 + 1))
                for half in range(2):
                    u = 2 * t + half
                    if u >= 4:
                        eng.wait_ge(x_tail, u - 3)
                    for k in range(4):
                        last = eng.transpose(sh.ps[:, u % 4, 128 * k:128 * k + n],
                                             x_tm[0:n, t % 3, 128 * (4 * half + k):128 * (4 * half + k) + 128],
                                             sh.ident[0:n, 0:n])
                    last.then_inc(x_tr, 1)

        def unit(u):
            t, half = divmod(u, 2)
            n = 128 if t < 8 else 64
            bank = sh.ps[:, u % 4, :].rearrange("p (k n) -> p k n", k=4)[:, :, 0:n]
            return bank, (slice(None), slice(4 * half, 4 * half + 4), slice(128 * t, 128 * t + n))

        @block.scalar
        def _(eng):
            for u in range(2 * NT):
                eng.wait_ge(x_tr, u + 1)
                bank, at = unit(u)
                eng.activation(sh.xh[at], bank, ACT.Copy).then_inc(x_head, 1)
            head_slab(sh, eng, 0)

        @block.vector
        def _(eng):
            for u in range(2 * NT):
                eng.wait_ge(x_head, u + 1)
                bank, at = unit(u)
                eng.tensor_tensor(sh.xl[at], bank, f32(sh.xh[at]), ALU.subtract).then_inc(x_tail, 1)
            tail_slab(sh, eng, 0)


def store_branch(sh, eng, j, rows, cols, hi, lo, sem):
    eng.dma_start(sh.oT_hi[j, rows, cols], f32(hi)).then_inc(sem, 16)
    eng.dma_start(sh.oT_lo[j, rows, cols], f32(lo)).then_inc(sem, 16)


def wait_freed(sh, eng, n, b, g):
    u = 9 * n + 3 * b + g
    eng.wait_ge(sh.fm_free[u % 2], u // 2 + 1)


def wait_block_freed(sh, eng, n, b):
    for g in (1, 2):
        wait_freed(sh, eng, n, b, g)


def stage_conv(nc, sh):
    U = SEQ + 2 + DB * (DT + 2)
    NS = 2 + 2 * DB
    with ExitStack() as ctx:
        def sb(name, shape, dt=F32):
            return ctx.enter_context(nc.sbuf_tensor("cv_" + name, shape, dt))

        def sem(name):
            return sh.front_sem("cv_" + name)
        rows = sb("rows", [19, BW])
        cols = sb("cols", [128, 4, 19])
        c_sb = sb("c", [128, TOK])
        u = sb("u", [128, U])
        y = sb("y", [128, TOK])
        o = sb("o", [128, TOK])
        o_hi = sb("o_hi", [128, 2, TOK], F32R)
        o_lo = sb("o_lo", [128, 2, TOK], F32R)
        st = sb("st", [128, 2, NS])
        st_tm = sb("st_tm", [NS, BW])
        loaded, rows_tr, oh_ready, ol_ready = sem("loaded"), sem("rows_tr"), sem("oh_ready"), sem("ol_ready")
        stored, st_ready, st_tr, st_out = sem("stored"), sem("st_ready"), sem("st_tr"), sem("st_out")
        dve_step, u_zero = sem("dve_step"), sem("u_zero")
        u_s = u[:, SEQ + 2:U].rearrange("p (b s) -> p b s", b=DB)
        y_s = y[:, SEQ:TOK].rearrange("p (b s) -> p b s", b=DB)
        block = ctx.enter_context(nc.Block())

        @block.sync
        def _(eng):
            eng.dma_start(rows[0:16, :], sh.state_conv[0].rearrange("b j c -> (b j) c")).then_inc(loaded, 16)
            eng.dma_start(rows[16:19, :], sh.conv_w[0]).then_inc(loaded, 16)
            for c in range(4):
                load_slab(sh, eng, CONV0 + c + 1)
                eng.wait_ge(ol_ready, c + 1)
                store_branch(sh, eng, 2, slice(128 * c, 128 * c + 128), slice(0, TOK),
                             o_hi[:, c % 2, :], o_lo[:, c % 2, :], stored)
            eng.wait_ge(st_out, 4)
            eng.dma_start(sh.prompt_conv[0, 0], st_tm[0:2, :]).then_inc(stored, 16)
            eng.dma_start(sh.sample_conv[0].rearrange("b j c -> (b j) c"), st_tm[2:NS, :]).then_inc(stored, 16)
            eng.wait_ge(stored, 16 * 10)

        @block.gpsimd
        def _(eng):
            eng.memset(u[:, 0:2], 0.0).then_inc(u_zero, 1)

        @block.tensor
        def _(eng):
            eng.wait_ge(loaded, 32)
            for c in range(4):
                last = eng.transpose(sh.ps[:, 7, 32 * c:32 * c + 19], rows[:, 128 * c:128 * c + 128],
                                     sh.ident[0:19, 0:19])
            last.then_inc(rows_tr, 1)
            for c in range(4):
                project_slab(sh, eng, CONV0 + c)
                eng.wait_ge(st_ready, c + 1)
                if c >= 1:
                    eng.wait_ge(st_out, c)
                eng.transpose(sh.ps[0:NS, 6, 0:128], st[:, c % 2, :], sh.ident[:, :]).then_inc(st_tr, 1)

        @block.scalar
        def _(eng):
            for c in range(4):
                head_slab(sh, eng, CONV0 + c + 1)
                for g in range(3):
                    bank, n, free, t0, tn = fm_unit(sh, CONV0 + c, 0, g)
                    eng.wait_ge(sh.fm_ready, n)
                    eng.activation(c_sb[:, t0:t0 + tn], bank, ACT.Copy).then_inc(free, 1)
                eng.wait_ge(st_tr, c + 1)
                eng.activation(st_tm[:, 128 * c:128 * c + 128], sh.ps[0:NS, 6, 0:128], ACT.Copy).then_inc(st_out, 1)
                wait_block_freed(sh, eng, CONV0 + c, 2)
                if c >= 2:
                    eng.wait_ge(stored, 32 * (c - 1))
                eng.activation(o_hi[:, c % 2, :], o[:, :], ACT.Copy).then_inc(oh_ready, 1)

        @block.vector
        def _(eng):
            ch = Chain(eng, dve_step)
            eng.wait_ge(rows_tr, 1)
            ch(eng.tensor_copy(cols[:, :, :], sh.ps[:, 7, 0:128].rearrange("p (c n) -> p c n", c=4)[:, :, 0:19]))
            eng.wait_ge(u_zero, 1)
            for c in range(4):
                tail_slab(sh, eng, CONV0 + c + 1)
                ch(eng.tensor_copy(u_s[:, :, 0:2], cols[:, c, 0:16].rearrange("p (b j) -> p b j", b=DB)))
                for g in range(3):
                    bank, n, free, t0, tn = fm_unit(sh, CONV0 + c, 1, g)
                    wait_freed(sh, eng, CONV0 + c, 0, g)
                    eng.wait_ge(sh.fm_ready, n)
                    pn = min(tn, SEQ - t0)
                    if pn < tn:
                        ch(eng.tensor_tensor(u_s[:, :, 2:], bank[:, pn:tn].rearrange("p (b t) -> p b t", b=DB),
                                             c_sb[:, SEQ:TOK].rearrange("p (b t) -> p b t", b=DB), ALU.mult))
                    eng.tensor_tensor(u[:, 2 + t0:2 + t0 + pn], bank[:, 0:pn], c_sb[:, t0:t0 + pn],
                                      ALU.mult).then_inc(free, 1)
                wait_block_freed(sh, eng, CONV0 + c, 1)
                tap = [cols[:, c, 16 + j:17 + j] for j in range(3)]
                eng.tensor_scalar(y[:, 0:SEQ], u[:, 0:SEQ], tap[0], None, ALU.mult)
                ch(eng.tensor_scalar(y_s, u_s[:, :, 0:DT], tap[0], None, ALU.mult))
                for j in (1, 2):
                    eng.scalar_tensor_tensor(out=y[:, 0:SEQ], in0=u[:, j:j + SEQ], scalar=tap[j], in1=y[:, 0:SEQ],
                                             op0=ALU.mult, op1=ALU.add)
                    ch(eng.scalar_tensor_tensor(out=y_s, in0=u_s[:, :, j:j + DT], scalar=tap[j], in1=y_s,
                                                op0=ALU.mult, op1=ALU.add))
                if c >= 2:
                    eng.wait_ge(st_tr, c - 1)
                ch(eng.tensor_copy(st[:, c % 2, 0:2], u[:, SEQ:SEQ + 2]))
                eng.tensor_copy(st[:, c % 2, 2:NS].rearrange("p (b j) -> p b j", b=DB),
                                u_s[:, :, DT:DT + 2]).then_inc(st_ready, 1)
                for g in range(3):
                    bank, n, free, t0, tn = fm_unit(sh, CONV0 + c, 2, g)
                    eng.wait_ge(sh.fm_ready, n)
                    eng.tensor_tensor(o[:, t0:t0 + tn], bank, y[:, t0:t0 + tn], ALU.mult).then_inc(free, 1)
                eng.wait_ge(oh_ready, c + 1)
                eng.tensor_tensor(o_lo[:, c % 2, :], o[:, :], f32(o_hi[:, c % 2, :]),
                                  ALU.subtract).then_inc(ol_ready, 1)


def stage_small(nc, sh):
    with ExitStack() as ctx:
        def sb(name, shape, dt=F32):
            return ctx.enter_context(nc.sbuf_tensor("sm_" + name, shape, dt))

        def sem(name):
            return sh.front_sem("sm_" + name)
        w = sb("w", [128, KC, 128])
        wh, wl = sb("wh", [128, KC, 128], F32R), sb("wl", [128, KC, 128], F32R)
        bf = sb("bf", [H_FOX, 1])
        z, a, logf, c, nc_ = (sb(n, [H_FOX, TOK]) for n in ("z", "a", "logf", "c", "nc"))
        restart = sb("restart", [H_FOX, TOK])
        lf_tm = sb("lf_tm", [128, NT, H_FOX])
        zero, loaded, head, tail, ready = (sem(n) for n in ("zero", "loaded", "head", "tail", "ready"))
        act_s, dve_s, lf_ready, lf_tr, stored, c_ready, pool_s, lf_out = (
            sem(n) for n in ("act", "dve", "lf_ready", "lf_tr", "stored", "c_ready", "pool", "lf_out"))
        block = ctx.enter_context(nc.Block())

        @block.gpsimd
        def _(eng):
            eng.memset(w[:, :, :], 0.0).then_inc(zero, 1)
            ch = Chain(eng, pool_s)
            ch(eng.memset(sh.restart[:, :], 1.0))
            ch(eng.memset(sh.restart[:, 0:SEQ:CHUNK], 0.0))
            ch(eng.memset(sh.restart[:, SEQ:TOK:DT], 0.0))
            ch(eng.memset(restart[:, :], 1.0))
            ch(eng.memset(restart[:, SEQ:TOK:DT], 0.0))

        @block.sync
        def _(eng):
            eng.wait_ge(zero, 1)
            for col, at, n in ((FF, 0, H_FOX), (GA, 32, LR)):
                eng.dma_start(w[:, :, at:at + n], sh.w_in[0, :, col:col + n].rearrange("(k p) n -> p k n", p=128)
                              ).then_inc(loaded, 16)
            eng.dma_start(bf[:, :], sh.b_fox_f.rearrange("a h -> h a"), allow_slow_non_contiguous=True).then_inc(loaded, 16)
            eng.dma_start(sh.wa2[:, :], sh.w_gla_a2[0]).then_inc(loaded, 16)
            eng.dma_start(sh.bga[:, :], sh.b_gla_a[0].rearrange("(c p) -> p c", p=128), allow_slow_non_contiguous=True).then_inc(loaded, 16)
            eng.dma_start(sh.gnorm[:, :], sh.gla_norm_g[0].rearrange("(c p) -> p c", p=128), allow_slow_non_contiguous=True).then_inc(loaded, 16)
            eng.wait_ge(c_ready, 2)
            eng.dma_start(sh.c_dram[0], c[:, :]).then_inc(stored, 16)
            eng.dma_start(sh.c_dram[1], nc_[:, :]).then_inc(stored, 16)
            eng.wait_ge(lf_out, 1)
            eng.dma_start(sh.prompt_fox_logf[0, 0].rearrange("(t p) h -> p t h", p=128), lf_tm[:, 0:8, :]).then_inc(stored, 16)
            eng.dma_start(sh.sample_fox_logf[0].rearrange("b t h -> (b t) h"), lf_tm[0:64, 8, :]).then_inc(stored, 16)
            eng.wait_ge(stored, 64)

        @block.tensor
        def _(eng):
            eng.wait_ge(tail, 1)
            for g, (t0, tn) in enumerate(GROUPS):
                for k in range(KC):
                    for j, (ww, x) in enumerate(((wh, sh.xh), (wh, sh.xl), (wl, sh.xh))):
                        last = eng.matmul(sh.ps[:, 2 + g, 0:tn], ww[:, k, :], x[:, k, t0:t0 + tn],
                                          start=(k == 0 and j == 0), stop=(k == KC - 1 and j == 2))
                last.then_inc(ready, 1)
            eng.wait_ge(lf_ready, 1)
            for t in range(NT):
                n = 128 if t < 8 else 64
                last = eng.transpose(sh.ps[0:n, 7, 8 * t:8 * t + 8], logf[:, 128 * t:128 * t + n],
                                     sh.ident[0:8, 0:8])
            last.then_inc(lf_tr, 1)

        @block.scalar
        def _(eng):
            ch = Chain(eng, act_s)
            eng.wait_ge(loaded, 96)
            eng.activation(wh[:, :, :], w[:, :, :], ACT.Copy).then_inc(head, 1)
            for g, (t0, tn) in enumerate(GROUPS):
                eng.wait_ge(ready, g + 1)
                eng.activation(sh.gaT[:, t0:t0 + tn], sh.ps[32:48, 2 + g, 0:tn], ACT.Copy)
                ch(eng.activation(z[:, t0:t0 + tn], sh.ps[0:8, 2 + g, 0:tn], ACT.Identity, bias=bf[:, :]))
            ch(eng.activation(a[:, :], z[:, :], ACT.Abs))
            ch(eng.activation(a[:, :], a[:, :], ACT.Exp, scale=-1.0))
            ch(eng.activation(a[:, :], a[:, :], ACT.Ln, bias=1.0))

        @block.vector
        def _(eng):
            ch = Chain(eng, dve_s)
            eng.wait_ge(head, 1)
            eng.tensor_tensor(wl[:, :, :], w[:, :, :], f32(wh[:, :, :]), ALU.subtract).then_inc(tail, 1)
            eng.wait_ge(act_s, 6)
            eng.scalar_tensor_tensor(out=logf[:, :], in0=z[:, :], scalar=0.0, in1=a[:, :],
                                     op0=ALU.min, op1=ALU.subtract).then_inc(lf_ready, 1)
            eng.wait_ge(lf_ready, 1)
            eng.wait_ge(pool_s, 5)
            eng.tensor_tensor_scan(c[:, :], restart[:, :], logf[:, :], 0.0, ALU.mult, ALU.add).then_inc(c_ready, 1)
            eng.wait_ge(c_ready, 1)
            eng.tensor_scalar(nc_[:, :], c[:, :], -1.0, None, ALU.mult).then_inc(c_ready, 1)
            eng.wait_ge(lf_tr, 1)
            ch(eng.tensor_copy(lf_tm[:, 0:8, :], sh.ps[:, 7, 0:64].rearrange("p (t h) -> p t h", h=8)))
            eng.tensor_copy(lf_tm[0:64, 8, :], sh.ps[0:64, 7, 64:72]).then_inc(lf_out, 1)


def stage_gla(nc, sh):
    NCH = SEQ // CHUNK
    with ExitStack() as ctx:
        def sb(name, shape, dt=F32):
            return ctx.enter_context(nc.sbuf_tensor("gl_" + name, shape, dt))

        def sem(name):
            return sh.front_sem("gl_" + name)
        q = sb("q", [128, TOK])
        k = sb("k", [128, TOK])
        kz = sb("kz", [128, 2, TOK])
        T = sb("T", [128, 3, TOK])
        v = sb("v", [128, NT, 2 * DV])
        rs = sb("rs", [128, 2, TOK])
        kez = sb("kez", [128, 2, 2, 128])
        att = sb("att", [128, 2, 2, 128])
        att_s = sb("att_s", [64, 2, 64])
        mask, mask_s = sb("mask", [128, 2, 128], I32), sb("mask_s", [64, 2, 64], I32)
        S = sb("S", [128, 4, 2 * DV])
        S0 = sb("S0", [128, DB, 2 * DV])
        qz = sb("qz", [128, 9 * 64])
        decay = sb("decay", [128, NCH + DB])
        row_b = sb("row_b", [64, DB])
        ss, rstd = sb("ss", [128, 2 * NT]), sb("rstd", [128, 2 * NT])
        kez_s = k[0:64, 0:DB * 128].rearrange("p (b n) -> p b n", b=DB)
        (pool_s, act_s, dve_s, la_mm, la_free, e1, e2, e3, kend_ready, tr, tr_free, state_in,
         att_mm, att_ready, ds_mm, s_ready, o_mm, o_out, r_exp, ss_ready, sq_ready, on_ready, oT_tr, oT_ready, oh_ready,
         ol_ready, stored, kes_ready, dss_mm, s0_new, kz_ready, k_in, qin_ready, vk_ready, sq_in, z_ready, b_ready) = (
             sem(n) for n in (
             "pool", "act", "dve", "la_mm", "la_free", "e1", "e2", "e3", "kend_ready", "tr",
             "tr_free", "state_in", "att_mm", "att_ready", "ds_mm", "s_ready", "o_mm", "o_out", "r_exp", "ss_ready",
             "sq_ready", "on_ready", "oT_tr", "oT_ready", "oh_ready", "ol_ready", "stored", "kes_ready", "dss_mm",
             "s0_new", "kz_ready", "k_in", "qin_ready", "vk_ready", "sq_in", "z_ready", "b_ready"))
        block = ctx.enter_context(nc.Block())
        NOT = 6

        @block.gpsimd
        def _(eng):
            ch = Chain(eng, pool_s)
            for m, n in ((mask, 128), (mask_s, 64)):
                f = T[0:n, 0, 0:2 * n].rearrange("p (h t) -> p h t", h=2)
                ch(eng.memset(f, 1.0))
                ch(eng.affine_select(out=f, in_=f, compare_op=ALU.is_ge, fill=0.0, base=0,
                                     pattern=[[0, 2], [1, n]], channel_multiplier=-1))
                if n == 128:
                    g = f[:, :, 64:128]
                    ch(eng.affine_select(out=g, in_=g, compare_op=ALU.is_ge, fill=0.0, base=-64,
                                         pattern=[[0, 2], [0, 64]], channel_multiplier=1))
                else:
                    g = f.rearrange("p h (b t) -> p h b t", b=DB)
                    ch(eng.affine_select(out=g, in_=g, compare_op=ALU.is_ge, fill=0.0, base=0,
                                         pattern=[[0, 2], [-DT, DB], [0, DT]], channel_multiplier=1))
                ch(eng.tensor_copy(m[:, :, :], f))
            ch(eng.memset(row_b[:, :], 1.0))
            ch(eng.affine_select(out=row_b[:, :], in_=row_b[:, :], compare_op=ALU.is_ge, fill=0.0, base=0,
                                 pattern=[[-DT, DB]], channel_multiplier=1))
            ch(eng.affine_select(out=row_b[:, :], in_=row_b[:, :], compare_op=ALU.is_ge, fill=0.0, base=DT - 1,
                                 pattern=[[DT, DB]], channel_multiplier=-1))
            for buf in (kz[:, :, :], att[:, :, :, :], att_s[:, :, :], kez[:, :, :, :], S0[:, :, :], qz[:, :],
                        v[64:128, NT - 1, :]):
                ch(eng.memset(buf, 0.0))
        POOL_DONE = 8 + 3 + 7

        @block.sync
        def _(eng):
            for p in range(2):
                if p == 0:
                    eng.wait_ge(pool_s, POOL_DONE)
                else:
                    eng.wait_ge(stored, 16 * 4)
                for h in range(2):
                    eng.dma_start(S0[64 * h:64 * h + 64, :, 128 * h:128 * h + 128],
                                  sh.state_gla[0, :, 2 * p + h].rearrange("b k v -> k b v")).then_inc(state_in, 16)
                load_slab(sh, eng, GLA0 + 2 * p + 1)
                load_slab(sh, eng, GLA0 + 2 * p + 2)
                eng.wait_ge(s_ready, (NCH + 1) * (p + 1))
                for h in range(2):
                    eng.dma_start(sh.prompt_gla[0, 0, 2 * p + h],
                                  S[64 * h:64 * h + 64, NCH % 4, 128 * h:128 * h + 128]).then_inc(stored, 16)
                eng.wait_ge(s0_new, 4 * (p + 1))
                for h in range(2):
                    eng.dma_start(sh.sample_gla[0, :, 2 * p + h].rearrange("b k v -> k b v"),
                                  S0[64 * h:64 * h + 64, :, 128 * h:128 * h + 128]).then_inc(stored, 16)
                for h in range(2):
                    eng.wait_ge(ol_ready, 2 * p + h + 1)
                    r0 = 128 * (2 * p + h)
                    store_branch(sh, eng, 0, slice(r0, r0 + 128), slice(0, TOK), T[:, 1, :], T[:, 2, :], stored)
                    eng.wait_ge(stored, 128 * p + 64 + 32 * (h + 1))

        def transpose_tile(eng, p, t):
            n = 128 if t < 8 else 64
            if t >= 2:
                eng.wait_ge(tr_free, NT * p + t - 1)
            for j, src in enumerate((T[:, 1, :], T[:, 2, :], k[:, :])):
                last = eng.transpose(sh.ps[0:n, 2 + t % 2, 128 * j:128 * j + 128],
                                     src[:, 128 * t:128 * t + n], sh.ident[:, :])
            last.then_inc(tr, 1)

        def place_tile(eng, p, t):
            n = 128 if t < 8 else 64
            eng.wait_ge(tr, NT * p + t + 1)
            bank = sh.ps[0:n, 2 + t % 2, :]
            if t < 8:
                if t >= 2:
                    eng.wait_ge(ds_mm, 8 * p + t - 1)
                eng.tensor_copy(kez[0:64, t % 2, 0, :], bank[0:64, 256:384])
                eng.tensor_copy(kez[64:128, t % 2, 1, :], bank[64:128, 256:384])
            else:
                for b in range(DB):
                    last = eng.tensor_scalar(kez_s[:, b, :], bank[:, 256:384], row_b[:, b:b + 1], None, ALU.mult)
                last.then_inc(kes_ready, 1)
            eng.tensor_copy(v[0:n, t, :], bank[:, 0:256]).then_inc(tr_free, 1)

        @block.tensor
        def _(eng):
            for p in range(2):
                if p == 1:
                    eng.wait_ge(oT_ready, NOT)
                for g, (t0, tn) in enumerate(GROUPS):
                    eng.matmul(sh.ps[:, 2 + g, 0:tn], sh.wa2[:, 128 * p:128 * p + 128], sh.gaT[:, t0:t0 + tn],
                               start=True, stop=True).then_inc(la_mm, 1)
                project_slab(sh, eng, GLA0 + 2 * p)
                project_slab(sh, eng, GLA0 + 2 * p + 1)
                eng.wait_ge(la_free, 3 * (p + 1))
                wait_block_freed(sh, eng, GLA0 + 2 * p, 2)
                wait_block_freed(sh, eng, GLA0 + 2 * p + 1, 0)
                eng.wait_ge(kend_ready, p + 1)
                transpose_tile(eng, p, 0)
                eng.wait_ge(qin_ready, p + 1)
                eng.wait_ge(kz_ready, p + 1)
                eng.wait_ge(state_in, 32 * (p + 1))
                for t in range(NT):
                    if t < 8:
                        transpose_tile(eng, p, t + 1)
                    eng.wait_ge(tr_free, NT * p + t + 1)
                    n = 128 if t < 8 else 64
                    i = NT * p + t
                    tok = slice(128 * t, 128 * t + n)
                    if i >= 1:
                        eng.wait_ge(att_ready, i)
                    for h in range(2):
                        last = eng.matmul(sh.ps[0:n, 4, 128 * h:128 * h + n], kz[:, h, tok], q[:, tok],
                                          start=(h == 0), stop=(h == 1), skip_group_check=True)
                    last.then_inc(att_mm, 1)
                    if t < 8:
                        if t >= 1:
                            eng.wait_ge(s_ready, (NCH + 1) * p + 2 * t + 1)
                        elif p == 1:
                            eng.wait_ge(s0_new, 4)
                        for c in range(2):
                            last = eng.matmul(sh.ps[:, 7, 256 * c:256 * c + 256], kez[:, t % 2, c, :], v[:, t, :],
                                              start=True, stop=True, skip_group_check=True)
                        last.then_inc(ds_mm, 1)
                    out = sh.ps[0:n, 5 + t % 2, 0:256]
                    if i >= 2:
                        eng.wait_ge(o_out, i - 1)
                    eng.wait_ge(att_ready, i + 1)
                    for h in range(2):
                        a = att[:, t % 2, h, :] if t < 8 else att_s[:, h, :]
                        eng.matmul(out[:, 128 * h:128 * h + 128], a, v[0:n, t, 128 * h:128 * h + 128],
                                   start=(h == 0), stop=False, skip_group_check=True)
                    if t < 8:
                        for c in range(2):
                            eng.wait_ge(s_ready, (NCH + 1) * p + 2 * t + c + 1)
                            last = eng.matmul(out[64 * c:64 * c + 64, :],
                                              q[:, 128 * t + 64 * c:128 * t + 64 * c + 64],
                                              S[:, (2 * t + c) % 4, :], start=False, stop=True, skip_group_check=True)
                    else:
                        for b in range(DB):
                            last = eng.matmul(out, qz[:, 64 * b:64 * b + 64], S0[:, b, :],
                                              start=False, stop=(b == DB - 1), skip_group_check=True)
                    last.then_inc(o_mm, 1)
                eng.wait_ge(kes_ready, p + 1)
                for b2 in range(4):
                    if b2 == 0:
                        eng.wait_ge(s_ready, (NCH + 1) * (p + 1))
                    else:
                        eng.wait_ge(s0_new, 4 * p + b2)
                    for e in range(2):
                        last = eng.matmul(sh.ps[:, 7, 256 * e:256 * e + 256], kez_s[:, 2 * b2 + e, :],
                                          v[0:64, NT - 1, :], start=True, stop=True, skip_group_check=True)
                    last.then_inc(dss_mm, 1)
                eng.wait_ge(on_ready, p + 1)
                for h in range(2):
                    for w in range(3):
                        i = NOT * p + 3 * h + w
                        if i % NOT >= 2:
                            eng.wait_ge(oT_ready, i - 1)
                        for t in range(4 * w, min(4 * w + 4, NT)):
                            n = 128 if t < 8 else 64
                            last = eng.transpose(sh.ps[:, 2 + i % 2, 128 * (t % 4):128 * (t % 4) + n],
                                                 v[0:n, t, 128 * h:128 * h + 128], sh.ident[0:n, 0:n])
                        last.then_inc(oT_tr, 1)

        @block.scalar
        def _(eng):
            ch = Chain(eng, act_s)
            for p in range(2):
                s0, s1 = GLA0 + 2 * p, GLA0 + 2 * p + 1
                if p == 0:
                    eng.wait_ge(pool_s, POOL_DONE)
                else:
                    eng.wait_ge(stored, 128)
                for g, (t0, tn) in enumerate(GROUPS):
                    eng.wait_ge(la_mm, 3 * p + g + 1)
                    eng.activation(T[:, 0, t0:t0 + tn], sh.ps[:, 2 + g, 0:tn], ACT.Identity,
                                   bias=sh.bga[:, p:p + 1]).then_inc(la_free, 1)
                eng.wait_ge(la_free, 3 * (p + 1))
                ch(eng.activation(T[:, 1, :], T[:, 0, :], ACT.Abs))
                ch(eng.activation(T[:, 1, :], T[:, 1, :], ACT.Exp, scale=-1.0))
                eng.activation(T[:, 1, :], T[:, 1, :], ACT.Ln, bias=1.0).then_inc(z_ready, 1)
                for g in range(3):
                    bank, n, free, t0, tn = fm_unit(sh, s0, 0, g)
                    eng.wait_ge(sh.fm_ready, n)
                    eng.activation(q[:, t0:t0 + tn], bank, ACT.Copy, scale=DK ** -0.5).then_inc(free, 1)
                eng.wait_ge(b_ready, p + 1)
                eng.activation(T[:, 1, :], T[:, 0, :], ACT.Exp).then_inc(e1, 1)
                eng.activation(T[:, 2, :], T[:, 0, :], ACT.Exp, scale=-1.0).then_inc(e2, 1)
                for g in range(3):
                    bank, n, free, t0, tn = fm_unit(sh, s0, 1, g)
                    eng.wait_ge(sh.fm_ready, n)
                    eng.activation(k[:, t0:t0 + tn], bank, ACT.Copy).then_inc(free, 1)
                head_slab(sh, eng, s1)
                eng.wait_ge(e3, p + 1)
                ch(eng.activation(T[:, 0, :], T[:, 0, :], ACT.Exp, scale=-1.0))
                eng.wait_ge(kz_ready, p + 1)
                eng.wait_ge(qin_ready, p + 1)
                for n0, b, dst in ((s0, 2, 1), (s1, 0, 2)):
                    for g in range(3):
                        bank, n, free, t0, tn = fm_unit(sh, n0, b, g)
                        eng.wait_ge(sh.fm_ready, n)
                        eng.activation(T[:, dst, t0:t0 + tn], bank, ACT.Copy).then_inc(free, 1)
                    if b == 2:
                        head_slab(sh, eng, s1 + 1)
                eng.wait_ge(kend_ready, p + 1)
                for b in (1, 2):
                    for g in range(3):
                        bank, n, free, t0, tn = fm_unit(sh, s1, b, g)
                        eng.wait_ge(sh.fm_ready, n)
                        if b == 2:
                            wait_freed(sh, eng, s1, 1, g)
                        eng.activation(T[:, 0, t0:t0 + tn], bank, ACT.Exp, scale=-1.0).then_inc(r_exp, 1)
                for t in range(NT):
                    n = 128 if t < 8 else 64
                    eng.wait_ge(o_mm, NT * p + t + 1)
                    if t == NT - 1:
                        eng.wait_ge(dss_mm, 4 * (p + 1))
                    eng.activation(v[0:n, t, :], sh.ps[0:n, 5 + t % 2, 0:256], ACT.Copy).then_inc(o_out, 1)
                eng.wait_ge(ss_ready, p + 1)
                eng.activation(ss[:, :], ss[:, :], ACT.Sqrt).then_inc(sq_ready, 1)
                for h in range(2):
                    eng.wait_ge(oT_ready, NOT * p + 3 * h + 3)
                    if h == 1:
                        eng.wait_ge(stored, 128 * p + 64 + 32)
                    eng.activation(T[:, 1, :].bitcast(F32R), T[:, 0, :], ACT.Copy).then_inc(oh_ready, 1)

        @block.vector
        def _(eng):
            ch = Chain(eng, dve_s)
            eng.wait_ge(pool_s, POOL_DONE)
            for p in range(2):
                s0, s1 = GLA0 + 2 * p, GLA0 + 2 * p + 1
                eng.wait_ge(z_ready, p + 1)
                ch(eng.scalar_tensor_tensor(out=T[:, 2, :], in0=T[:, 0, :], scalar=0.0, in1=T[:, 1, :],
                                            op0=ALU.min, op1=ALU.subtract))
                ch(eng.tensor_scalar(T[:, 2, :], T[:, 2, :], 1.0 / 16.0, None, ALU.mult))
                eng.tensor_tensor_scan(T[:, 0, :], sh.restart[:, :], T[:, 2, :], 0.0, ALU.mult,
                                       ALU.add).then_inc(b_ready, 1)
                tail_slab(sh, eng, s1)
                eng.wait_ge(e1, p + 1)
                wait_block_freed(sh, eng, s0, 0)
                ch(eng.tensor_copy(decay[:, 0:NCH], T[:, 1, CHUNK - 1:SEQ:CHUNK]))
                ch(eng.tensor_copy(decay[:, NCH:], T[:, 1, SEQ + DT - 1:TOK:DT]))
                eng.tensor_tensor(q[:, :], q[:, :], T[:, 1, :], ALU.mult).then_inc(qin_ready, 1)
                eng.wait_ge(qin_ready, p + 1)
                ch(eng.tensor_copy(qz[:, :].rearrange("p (b s) -> p b s", s=72)[:, :, 0:DT],
                                   q[:, SEQ:TOK].rearrange("p (b t) -> p b t", b=DB)))
                eng.wait_ge(e2, p + 1)
                wait_block_freed(sh, eng, s0, 1)
                ch(eng.tensor_tensor(kz[0:64, 0, :], k[0:64, :], T[0:64, 2, :], ALU.mult))
                eng.tensor_tensor(kz[64:128, 1, :], k[64:128, :], T[64:128, 2, :], ALU.mult).then_inc(kz_ready, 1)
                bp = T[:, 0, 0:SEQ].rearrange("p (c s) -> p c s", s=CHUNK)
                bs = T[:, 0, SEQ:TOK].rearrange("p (c s) -> p c s", s=DT)
                ch(eng.tensor_copy(ss[:, 0:NCH], T[:, 0, CHUNK - 1:SEQ:CHUNK]))
                ch(eng.tensor_copy(rstd[:, 0:DB], T[:, 0, SEQ + DT - 1:TOK:DT]))
                ch(eng.tensor_tensor(bp, bp, ss[:, 0:NCH].unsqueeze(2).broadcast_to([128, NCH, CHUNK]), ALU.subtract))
                eng.tensor_tensor(bs, bs, rstd[:, 0:DB].unsqueeze(2).broadcast_to([128, DB, DT]),
                                  ALU.subtract).then_inc(e3, 1)
                eng.wait_ge(act_s, 3 * (p + 1))
                eng.tensor_tensor(k[:, :], k[:, :], T[:, 0, :], ALU.mult).then_inc(kend_ready, 1)
                tail_slab(sh, eng, s1 + 1)
                for b in (1, 2):
                    for g in range(3):
                        bank, n, free, t0, tn = fm_unit(sh, s1, b, g)
                        out = rs[:, b - 1, t0:t0 + tn]
                        eng.wait_ge(r_exp, 6 * p + 3 * (b - 1) + g + 1)
                        ch(eng.tensor_scalar(out, T[:, 0, t0:t0 + tn], 1.0, None, ALU.add))
                        ch(eng.reciprocal(out, out))
                        eng.tensor_tensor(out, bank, out, ALU.mult).then_inc(free, 1)
                if p == 1:
                    eng.wait_ge(stored, 32)
                eng.memset(S[:, :, :], 0.0).then_inc(s_ready, 1)
                place_tile(eng, p, 0)
                for t in range(NT):
                    if t < 8:
                        place_tile(eng, p, t + 1)
                    n = 128 if t < 8 else 64
                    i = NT * p + t
                    eng.wait_ge(att_mm, i + 1)
                    if t < 8:
                        if t >= 2:
                            eng.wait_ge(o_mm, i - 1)
                        eng.copy_predicated(att[:, t % 2, :, :], mask[:, :, :],
                                            sh.ps[:, 4, 0:256].rearrange("p (h t) -> p h t", h=2)).then_inc(att_ready, 1)
                        for c in range(2):
                            m = 2 * t + c
                            eng.wait_ge(ds_mm, 8 * p + t + 1)
                            eng.wait_ge(s_ready, (NCH + 1) * p + m + 1)
                            if m >= 3 and c == 1:
                                eng.wait_ge(o_mm, i)
                            new, old = S[:, (m + 1) % 4], S[:, m % 4]
                            ds = sh.ps[:, 7, 256 * c:256 * c + 256]
                            d = decay[:, m:m + 1]
                            eng.scalar_tensor_tensor(out=new[0:64, 0:128], in0=old[0:64, 0:128], scalar=d[0:64],
                                                     in1=ds[0:64, 0:128], op0=ALU.mult, op1=ALU.add)
                            eng.scalar_tensor_tensor(out=new[64:128, 128:256], in0=old[64:128, 128:256],
                                                     scalar=d[64:128], in1=ds[64:128, 128:256], op0=ALU.mult,
                                                     op1=ALU.add).then_inc(s_ready, 1)
                    else:
                        eng.copy_predicated(att_s[:, :, :], mask_s[:, :, :],
                                            sh.ps[0:64, 4, 0:256].rearrange("p (h t) -> p h t", h=2)[:, :, 0:64]
                                            ).then_inc(att_ready, 1)
                eng.wait_ge(o_mm, NT * (p + 1))
                for b2 in range(4):
                    eng.wait_ge(dss_mm, 4 * p + b2 + 1)
                    for e in range(2):
                        b = 2 * b2 + e
                        ds = sh.ps[:, 7, 256 * e:256 * e + 256]
                        d = decay[:, NCH + b:NCH + b + 1]
                        for h in range(2):
                            r, cc = slice(64 * h, 64 * h + 64), slice(128 * h, 128 * h + 128)
                            last = eng.scalar_tensor_tensor(out=S0[r, b, cc], in0=S0[r, b, cc], scalar=d[r],
                                                            in1=ds[r, cc], op0=ALU.mult, op1=ALU.add)
                    last.then_inc(s0_new, 1)
                eng.wait_ge(o_out, NT * (p + 1))
                ov = v[:, :, :].rearrange("p t (h n) -> p (t h) n", h=2)
                sq = T[:, :, :].rearrange("p a n -> p (a n)")[:, 0:NT * 256].rearrange("p (i n) -> p i n", n=DV)
                ch(eng.tensor_tensor(sq, ov, ov, ALU.mult))
                ch(eng.reduce_sum(ss[:, :], sq, axis=X))
                eng.tensor_scalar(ss[:, :], ss[:, :], 1.0 / DV, EPS, ALU.mult, ALU.add).then_inc(ss_ready, 1)
                eng.wait_ge(sq_ready, p + 1)
                ch(eng.reciprocal(rstd[:, :], ss[:, :]))
                eng.tensor_tensor(ov, ov, rstd[:, :].unsqueeze(2).broadcast_to([128, 2 * NT, DV]),
                                  ALU.mult).then_inc(on_ready, 1)
                for h in range(2):
                    if 2 * p + h:
                        eng.wait_ge(ol_ready, 2 * p + h)
                    for w in range(3):
                        i = NOT * p + 3 * h + w
                        t0, tn = 512 * w, min(512, TOK - 512 * w)
                        eng.wait_ge(oT_tr, i + 1)
                        eng.scalar_tensor_tensor(out=T[:, 0, t0:t0 + tn], in0=sh.ps[:, 2 + i % 2, 0:tn],
                                                 scalar=sh.gnorm[:, 2 * p + h:2 * p + h + 1],
                                                 in1=rs[:, h, t0:t0 + tn], op0=ALU.mult, op1=ALU.mult).then_inc(oT_ready, 1)
                    eng.wait_ge(oh_ready, 2 * p + h + 1)
                    eng.tensor_tensor(T[:, 2, :].bitcast(F32R), T[:, 0, :], T[:, 1, :], ALU.subtract).then_inc(ol_ready, 1)



def stage_fox(nc, sh):
    UN = 16
    chunks = [i // 2 // 4 + 1 for i in range(UN)]
    NCHK = sum(chunks)
    with ExitStack() as ctx:
        def sb(name, shape, dt=F32):
            return ctx.enter_context(nc.sbuf_tensor("fx_" + name, shape, dt))

        def sem(name):
            return sh.front_sem("fx_" + name)
        qa, ka = sb("qa", [HD + 2, 2, TOK]), sb("ka", [HD + 2, 2, TOK])
        vT = sb("vT", [128, TOK])
        kv = sb("kv", [128, NT, 2 * 128])
        P = sb("P", [128, 2, SEQ])
        PT = sb("PT", [128, 2, 8, 128])
        o_tm = sb("o_tm", [128, 2, 2, HD])
        oh, ol = sb("oh", [128, SEQ], F32R), sb("ol", [128, SEQ], F32R)
        mx, nm, rsum = sb("mx", [128, UN]), sb("nm", [128, UN]), sb("rsum", [128, UN])
        rinv = sb("rinv", [128, 2, 2])
        mneg, ident16 = sb("mneg", [128, 128], BF16), sb("ident16", [128, 128], BF16)
        mf = sb("mf", [128, 128])
        (pool_s, dve_s, c_in, kv_tr, kv_out, kv_stored, s_ready, nm_ready, exp_done, p_tr, pt_out, pv_done,
         o_out, oT_tr, oT_hi, oT_lo, stored) = (sem(n) for n in (
             "pool", "dve", "c_in", "kv_tr", "kv_out", "kv_stored", "s_ready", "nm_ready", "exp_done", "p_tr",
             "pt_out", "pv_done", "o_out", "oT_tr", "oT_hi", "oT_lo", "stored"))
        block = ctx.enter_context(nc.Block())

        def first_chunk(p, i):
            return NCHK * p + sum(chunks[:i])

        @block.gpsimd
        def _(eng):
            ch = Chain(eng, pool_s)
            ch(eng.memset(qa[HD:HD + 2, :, :], 1.0))
            ch(eng.memset(ka[HD:HD + 2, :, :], 1.0))
            ch(eng.memset(mf[:, :], 0.0))
            ch(eng.affine_select(out=mf[:, :], in_=mf[:, :], compare_op=ALU.is_ge, fill=-BIG, base=0,
                                 pattern=[[-1, 128]], channel_multiplier=1))
            ch(eng.tensor_copy(mneg[:, :], mf[:, :]))
            ch(eng.tensor_copy(ident16[:, :], sh.ident[:, :]))
            ch(eng.memset(sh.qbd[:, :, :, :], 0.0))

        @block.sync
        def _(eng):
            eng.wait_ge(pool_s, 2)
            for p in range(4):
                load_slab(sh, eng, FOX0 + p + 1)
                if p >= 1:
                    eng.wait_ge(s_ready, UN * p)
                eng.dma_start(qa[HD:HD + 1, :, :], sh.c_dram[0, 2 * p:2 * p + 2, :].unsqueeze(0)).then_inc(c_in, 16)
                eng.dma_start(ka[HD + 1:HD + 2, :, :], sh.c_dram[1, 2 * p:2 * p + 2, :].unsqueeze(0)).then_inc(c_in, 16)
                eng.wait_ge(kv_out, NT * (p + 1))
                cols = slice(128 * p, 128 * p + 128)
                for j, (po, so) in enumerate(((sh.prompt_fox_k, sh.sample_fox_k), (sh.prompt_fox_v, sh.sample_fox_v))):
                    part = slice(128 * j, 128 * j + 128)
                    eng.dma_start(po[0, 0].rearrange("(t p) h d -> p t (h d)", p=128)[:, :, cols],
                                  kv[:, 0:8, part]).then_inc(kv_stored, 16)
                    eng.dma_start(so[0].rearrange("b t h d -> (b t) (h d)")[:, cols],
                                  kv[0:64, 8, part]).then_inc(kv_stored, 16)
                eng.wait_ge(oT_lo, 8 * (p + 1))
                store_branch(sh, eng, 1, cols, slice(0, SEQ), oh[:, :], ol[:, :], stored)
            eng.wait_ge(kv_stored, 64 * 4)
            eng.wait_ge(stored, 32 * 4)

        @block.tensor
        def _(eng):
            eng.wait_ge(pool_s, 7)

            def scores(p, i):
                qt, h = divmod(i, 2)
                I, kn = UN * p + i, 128 * (qt + 1)
                if I >= 2:
                    eng.wait_ge(exp_done, I - 1)
                bank0 = 2 + 2 * (i % 2)
                for k0 in range(0, kn, 512):
                    n = min(512, kn - k0)
                    out = sh.ps[:, bank0 + k0 // 512, 0:n]
                    diag = k0 + n == kn
                    last = eng.matmul(out, qa[:, h, 128 * qt:128 * qt + 128], ka[:, h, k0:k0 + n],
                                      start=True, stop=not diag, skip_group_check=True)
                    if diag:
                        last = eng.matmul(out[:, n - 128:n], ident16[:, :], mneg[:, :], start=False, stop=True,
                                          skip_group_check=True)
                last.then_inc(s_ready, 1)

            def transpose_probs(p, i):
                qt = i // 2
                eng.wait_ge(exp_done, UN * p + i + 1)
                for c in range(chunks[i]):
                    C = first_chunk(p, i) + c
                    if C >= 2:
                        eng.wait_ge(pt_out, C - 1)
                    for t in range(4 * c, min(4 * c + 4, qt + 1)):
                        last = eng.transpose(sh.ps[:, 6 + C % 2, 128 * (t % 4):128 * (t % 4) + 128],
                                             P[:, i % 2, 128 * t:128 * t + 128], sh.ident[:, :])
                    last.then_inc(p_tr, 1)

            def weigh_values(p, i):
                qt, h = divmod(i, 2)
                eng.wait_ge(pt_out, first_chunk(p, i) + chunks[i])
                if h == 0 and qt >= 2:
                    eng.wait_ge(oT_lo, 8 * p + qt - 1)
                for t in range(qt + 1):
                    last = eng.matmul(sh.ps[:, qt % 2, 64 * h:64 * h + 64], PT[:, i % 2, t, :],
                                      kv[:, t, 128 + 64 * h:128 + 64 * h + 64],
                                      start=(h == 0 and t == 0), stop=(t == qt), skip_group_check=True)
                last.then_inc(pv_done, 1)

            def transpose_out(p, qt):
                eng.wait_ge(o_out, 8 * p + qt + 1)
                eng.transpose(sh.ps[:, qt % 2, 128:256], o_tm[:, qt % 2, :, :].rearrange("p h d -> p (h d)"),
                              sh.ident[:, :]).then_inc(oT_tr, 1)

            for p in range(4):
                n = FOX0 + p
                if p >= 1:
                    eng.wait_ge(oT_lo, 8 * p)
                project_slab(sh, eng, n)
                wait_block_freed(sh, eng, n, 1)
                wait_block_freed(sh, eng, n, 2)
                eng.wait_ge(c_in, 32 * (p + 1))
                if p == 0:
                    pass
                for t in range(NT):
                    m = 128 if t < 8 else 64
                    if t >= 2:
                        eng.wait_ge(kv_out, NT * p + t - 1)
                    else:
                        eng.wait_ge(pt_out, NCHK * p)
                    tok = slice(128 * t, 128 * t + m)
                    bank = sh.ps[0:m, 6 + t % 2, :]
                    for h in range(2):
                        eng.transpose(bank[:, 64 * h:64 * h + 64], ka[0:HD, h, tok], sh.ident[0:HD, 0:HD])
                    eng.transpose(bank[:, 128:256], vT[:, tok], sh.ident[:, :]).then_inc(kv_tr, 1)
                eng.wait_ge(kv_out, NT * (p + 1))
                scores(p, 0)
                for i in range(UN + 2):
                    if i + 1 < UN:
                        scores(p, i + 1)
                    if i < UN:
                        transpose_probs(p, i)
                    if 1 <= i <= UN:
                        weigh_values(p, i - 1)
                    if i >= 3 and i % 2:
                        transpose_out(p, (i - 3) // 2)

        @block.scalar
        def _(eng):
            eng.wait_ge(pool_s, 7)
            for p in range(4):
                n0 = FOX0 + p
                head_slab(sh, eng, n0 + 1)
                for g in range(3):
                    bank, n, free, t0, tn = fm_unit(sh, n0, 0, g)
                    eng.wait_ge(sh.fm_ready, n)
                    if g == 2:
                        for h in range(2):
                            at = 16 * p + 8 * h
                            eng.activation(sh.qbd[64 * h:64 * h + 64, p, :, at:at + 8],
                                           bank[64 * h:64 * h + 64, SEQ - t0:].rearrange("p (b t) -> p b t", b=DB),
                                           ACT.Copy, scale=HD ** -0.5)
                    eng.activation(qa[0:HD, 0, t0:t0 + tn], bank[0:64, :], ACT.Copy, scale=HD ** -0.5)
                    eng.activation(qa[0:HD, 1, t0:t0 + tn], bank[64:128, :], ACT.Copy,
                                   scale=HD ** -0.5).then_inc(free, 1)
                for g in range(3):
                    bank, n, free, t0, tn = fm_unit(sh, n0, 2, g)
                    eng.wait_ge(sh.fm_ready, n)
                    eng.activation(vT[:, t0:t0 + tn], bank, ACT.Copy).then_inc(free, 1)
                for i in range(-1, UN + 2):
                    if i + 1 < UN:
                        I = UN * p + i + 1
                        eng.wait_ge(nm_ready, I + 1)
                        if i + 1 >= 2:
                            eng.wait_ge(p_tr, first_chunk(p, i - 1) + chunks[i - 1])
                        kn = 128 * ((i + 1) // 2 + 1)
                        s = sh.ps[:, 2 + 2 * ((i + 1) % 2):4 + 2 * ((i + 1) % 2), :].rearrange("p a n -> p (a n)")
                        eng.activation(P[:, (i + 1) % 2, 0:kn], s[:, 0:kn], ACT.Exp, bias=nm[:, i + 1:i + 2],
                                       accum_out=rsum[:, i + 1:i + 2]).then_inc(exp_done, 1)
                    if i >= 3 and i % 2:
                        qt = (i - 3) // 2
                        eng.wait_ge(oT_tr, 8 * p + qt + 1)
                        if p >= 1 and qt == 0:
                            eng.wait_ge(stored, 32 * p)
                        eng.activation(oh[:, 128 * qt:128 * qt + 128], sh.ps[:, qt % 2, 128:256],
                                       ACT.Copy).then_inc(oT_hi, 1)

        @block.vector
        def _(eng):
            ch = Chain(eng, dve_s)
            for p in range(4):
                n0 = FOX0 + p
                tail_slab(sh, eng, n0 + 1)
                for g in range(3):
                    bank, n, free, t0, tn = fm_unit(sh, n0, 1, g)
                    eng.wait_ge(sh.fm_ready, n)
                    if g == 2:
                        eng.tensor_copy(sh.kTs[:, p, :], bank[:, SEQ - t0:])
                    eng.tensor_copy(ka[0:HD, 0, t0:t0 + tn], bank[0:64, :])
                    eng.tensor_copy(ka[0:HD, 1, t0:t0 + tn], bank[64:128, :]).then_inc(free, 1)
                if p >= 1:
                    eng.wait_ge(kv_stored, 64 * p)
                    eng.wait_ge(pv_done, UN * p)
                for t in range(NT):
                    m = 128 if t < 8 else 64
                    eng.wait_ge(kv_tr, NT * p + t + 1)
                    if t == 8:
                        ch(eng.tensor_copy(sh.vs[:, 128 * p:128 * p + 128], sh.ps[0:m, 6 + t % 2, 128:256]))
                    eng.tensor_copy(kv[0:m, t, :], sh.ps[0:m, 6 + t % 2, 0:256]).then_inc(kv_out, 1)
                for i in range(-1, UN + 2):
                    if i + 1 < UN:
                        I = UN * p + i + 1
                        eng.wait_ge(s_ready, I + 1)
                        kn = 128 * ((i + 1) // 2 + 1)
                        s = sh.ps[:, 2 + 2 * ((i + 1) % 2):4 + 2 * ((i + 1) % 2), :].rearrange("p a n -> p (a n)")
                        if I >= UN:
                            eng.wait_ge(exp_done, I + 1 - UN)
                        ch(eng.reduce_max(mx[:, i + 1:i + 2], s[:, 0:kn], axis=X))
                        eng.tensor_scalar(nm[:, i + 1:i + 2], mx[:, i + 1:i + 2], -1.0, None,
                                          ALU.mult).then_inc(nm_ready, 1)
                    if 0 <= i < UN:
                        qt = i // 2
                        if UN * p + i >= 2:
                            eng.wait_ge(pv_done, UN * p + i - 1)
                        for c in range(chunks[i]):
                            C = first_chunk(p, i) + c
                            eng.wait_ge(p_tr, C + 1)
                            nt = min(4, qt + 1 - 4 * c)
                            eng.tensor_copy(PT[:, i % 2, 4 * c:4 * c + nt, :].rearrange("p t n -> p (t n)"),
                                            sh.ps[:, 6 + C % 2, 0:128 * nt]).then_inc(pt_out, 1)
                    if i >= 2 and i % 2 == 0:
                        qt = (i - 2) // 2
                        eng.wait_ge(pv_done, UN * p + i)
                        if 8 * p + qt >= 2:
                            eng.wait_ge(oT_tr, 8 * p + qt - 1)
                        ch(eng.reciprocal(rinv[:, qt % 2, :], rsum[:, 2 * qt:2 * qt + 2]))
                        eng.tensor_tensor(o_tm[:, qt % 2, :, :],
                                          sh.ps[:, qt % 2, 0:128].rearrange("p (h d) -> p h d", h=2),
                                          rinv[:, qt % 2, :].unsqueeze(2).broadcast_to([128, 2, HD]),
                                          ALU.mult).then_inc(o_out, 1)
                    if i >= 3 and i % 2:
                        qt = (i - 3) // 2
                        eng.wait_ge(oT_hi, 8 * p + qt + 1)
                        eng.tensor_tensor(ol[:, 128 * qt:128 * qt + 128], sh.ps[:, qt % 2, 128:256],
                                          f32(oh[:, 128 * qt:128 * qt + 128]), ALU.subtract).then_inc(oT_lo, 1)


def stage_fox_sample(nc, sh):
    R = H_FOX * DT
    KN = NPAGE * PAGE + DB * DT
    PAST = NPAGE * PAGE
    with ExitStack() as ctx:
        def sb(name, shape, dt=F32):
            return ctx.enter_context(nc.sbuf_tensor("fs_" + name, shape, dt))

        def sem(name):
            return sh.front_sem("fs_" + name)
        pages = sb("pages", [1, DB * NPAGE], I32)
        kp, vp = sb("kp", [128, 2, NPAGE, BW]), sb("vp", [128, 2, NPAGE, BW])
        lf = sb("lf", [128, 2, NPAGE, H_FOX])
        KT = sb("KT", [128, 2, 4, PAST])
        bias = sb("bias", [H_FOX, 2, KN])
        cs, cneg = sb("cs", [H_FOX, DB * DT]), sb("cneg", [H_FOX, DB * DT])
        head = sb("head", [H_FOX, R])
        headc = sb("headc", [H_FOX, 2, R])
        tsel = sb("tsel", [DT, R])
        base, window = sb("base", [DT, 128]), sb("window", [R, 128])
        after, ones = sb("after", [128, 128]), sb("ones", [128, KN])
        P, PT = sb("P", [R, 2, KN]), sb("PT", [128, 2, 3, R])
        mx, nm, rsum, rinv = (sb(n, [R, DB]) for n in ("mx", "nm", "rsum", "rinv"))
        oT = sb("oT", [128, 4, DB * DT])
        oh, ol = sb("oh", [128, 4, DB * DT], F32R), sb("ol", [128, 4, DB * DT], F32R)
        (pool_s, dve_s, small_in, page_in0, page_in1, k_tr, k_out, b_mm, b_out, w_mm, w_out, s_mm, nm_ready, exp_done, p_ready,
         p_tr, pt_out, pv_mm, o_out, oT_hi, oT_lo, stored) = (sem(n) for n in (
             "pool", "dve", "small_in", "page_in0", "page_in1", "k_tr", "k_out", "b_mm", "b_out", "w_mm", "w_out", "s_mm",
             "nm_ready", "exp_done", "p_ready", "p_tr", "pt_out", "pv_mm", "o_out", "oT_hi", "oT_lo", "stored"))
        page_in = [page_in0, page_in1]
        block = ctx.enter_context(nc.Block())

        @block.gpsimd
        def _(eng):
            ch = Chain(eng, pool_s)
            for m in (head, tsel):
                ch(eng.memset(m[:, :], 0.0))
            hv = head[:, :].rearrange("p (h t) -> p h t", h=H_FOX)
            tv = tsel[:, :].rearrange("p (h t) -> p h t", h=H_FOX)
            ch(eng.affine_select(out=hv, in_=hv, compare_op=ALU.not_equal, fill=1.0, base=0,
                                 pattern=[[-1, H_FOX], [0, DT]], channel_multiplier=1))
            ch(eng.affine_select(out=tv, in_=tv, compare_op=ALU.not_equal, fill=1.0, base=0,
                                 pattern=[[0, H_FOX], [-1, DT]], channel_multiplier=1))
            off = (DB - 1) * DT
            ch(eng.memset(base[:, :], 0.0))
            ch(eng.affine_select(out=base[:, :], in_=base[:, :], compare_op=ALU.is_ge, fill=-BIG, base=-off,
                                 pattern=[[1, 128]], channel_multiplier=0))
            ch(eng.affine_select(out=base[:, :], in_=base[:, :], compare_op=ALU.is_ge, fill=-BIG, base=off,
                                 pattern=[[-1, 128]], channel_multiplier=1))
            ch(eng.memset(after[:, :], 1.0))
            ch(eng.affine_select(out=after[:, :], in_=after[:, :], compare_op=ALU.is_gt, fill=0.0, base=0,
                                 pattern=[[-1, 128]], channel_multiplier=1))
            ch(eng.memset(ones[:, :], 1.0))
        POOL_DONE = 10

        @block.sync
        def _(eng):
            eng.dma_start(pages[:, :], sh.page_table.rearrange("b p -> (b p)").unsqueeze(0)).then_inc(small_in, 16)
            eng.wait_ge(small_in, 16)
            for b in range(DB):
                if b >= 2:
                    eng.wait_ge(pv_mm, b - 1)
                for g in range(NPAGE):
                    page = eng.value_load(pages[0:1, NPAGE * b + g:NPAGE * b + g + 1], min_val=0,
                                          max_val=sh.cache_fox_k.shape[1] - 1)
                    for pool, buf in ((sh.cache_fox_k, kp[:, b % 2, g, :]), (sh.cache_fox_v, vp[:, b % 2, g, :])):
                        eng.dma_start(buf, pool[0, bass.ds(page, 1)].rearrange("o s h d -> (o s) (h d)")
                                      ).then_inc(page_in[b % 2], 16)
                    eng.dma_start(lf[:, b % 2, g, :], sh.cache_fox_logf[0, bass.ds(page, 1)].rearrange("o s h -> (o s) h")
                                  ).then_inc(page_in[b % 2], 16)
                if b == 0:
                    eng.dma_start(cs[:, :], sh.c_dram[0, :, SEQ:TOK]).then_inc(small_in, 16)
                    eng.dma_start(cneg[:, :], sh.c_dram[1, :, SEQ:TOK]).then_inc(small_in, 16)
            eng.wait_ge(oT_lo, 1)
            for dst, src in ((sh.oT_hi, oh), (sh.oT_lo, ol)):
                eng.dma_start(dst[1, :, SEQ:TOK].rearrange("(c p) n -> p c n", p=128), f32(src[:, :, :])).then_inc(stored, 16)
            eng.wait_ge(stored, 32)

        @block.tensor
        def _(eng):
            eng.wait_ge(pool_s, POOL_DONE)
            eng.matmul(sh.ps[0:R, 7, 0:128], tsel[:, :], base[:, :], start=True, stop=True).then_inc(w_mm, 1)
            eng.wait_ge(w_out, 1)

            def scores(b):
                r = b % 2
                eng.wait_ge(page_in[r], 96 * (b // 2 + 1))
                if b >= 1:
                    eng.wait_ge(k_out, 2 * b)
                for g in range(NPAGE):
                    for c in range(4):
                        last = eng.transpose(sh.ps[:, g, 128 * c:128 * c + 128], kp[:, r, g, 128 * c:128 * c + 128],
                                             sh.ident[:, :])
                    last.then_inc(k_tr, 1)
                if b >= 1:
                    eng.wait_ge(b_out, b)
                eng.matmul(sh.ps[0:H_FOX, 2, 0:128], lf[:, r, 0, :], after[:, :], start=True, stop=False)
                eng.matmul(sh.ps[0:H_FOX, 2, 0:128], lf[:, r, 1, :], ones[:, 0:128], start=False, stop=True)
                eng.matmul(sh.ps[0:H_FOX, 2, 128:256], lf[:, r, 1, :], after[:, :], start=True,
                           stop=True, skip_group_check=True).then_inc(b_mm, 1)
                eng.wait_ge(b_out, b + 1)
                eng.wait_ge(k_out, 2 * b + 2)
                if b >= 2:
                    eng.wait_ge(exp_done, b - 1)
                out = sh.ps[0:R, 3 + r, 0:KN]
                eng.matmul(out, head[:, :], bias[:, r, :], start=True, stop=False, skip_group_check=True)
                eng.matmul(out, headc[:, r, :], ones[0:H_FOX, :], start=False, stop=False, skip_group_check=True)
                for c in range(4):
                    eng.matmul(out[:, 0:PAST], sh.qbd[:, c, b, :], KT[:, r, c, :], start=False, stop=False,
                               skip_group_check=True)
                    eng.matmul(out[:, PAST:], sh.qbd[:, c, b, :], sh.kTs[:, c, :], start=False, stop=False,
                               skip_group_check=True)
                w0 = (DB - 1 - b) * DT
                eng.matmul(out[:, PAST:], sh.ident[0:R, 0:R], window[:, w0:w0 + DB * DT], start=False, stop=True,
                           skip_group_check=True).then_inc(s_mm, 1)

            def values(b):
                r = b % 2
                eng.wait_ge(p_ready, b + 1)
                if b >= 1:
                    eng.wait_ge(pt_out, b)
                for g, n in enumerate((128, 128, 64)):
                    last = eng.transpose(sh.ps[0:n, 5, R * g:R * g + R], P[:, r, 128 * g:128 * g + n],
                                         sh.ident[0:R, 0:R])
                last.then_inc(p_tr, 1)
                eng.wait_ge(pt_out, b + 1)
                if b >= 1:
                    eng.wait_ge(o_out, b)
                for c in range(4):
                    out, cc = sh.ps[:, 6, R * c:R * c + R], slice(128 * c, 128 * c + 128)
                    eng.matmul(out, vp[:, r, 0, cc], PT[:, r, 0, :], start=(c == 0), stop=False, skip_group_check=True)
                    eng.matmul(out, vp[:, r, 1, cc], PT[:, r, 1, :], start=False, stop=False, skip_group_check=True)
                    last = eng.matmul(out, sh.vs[:, cc], PT[0:64, r, 2, :], start=False, stop=True, skip_group_check=True)
                last.then_inc(pv_mm, 1)

            scores(0)
            for b in range(DB):
                if b + 1 < DB:
                    scores(b + 1)
                values(b)

        @block.scalar
        def _(eng):
            for b in range(DB):
                r = b % 2
                eng.wait_ge(nm_ready, b + 1)
                if b >= 2:
                    eng.wait_ge(p_tr, b - 1)
                eng.activation(P[:, r, :], sh.ps[0:R, 3 + r, 0:KN], ACT.Exp, bias=nm[:, b:b + 1],
                               accum_out=rsum[:, b:b + 1]).then_inc(exp_done, 1)
            eng.wait_ge(o_out, DB)
            eng.activation(oh[:, :, :], oT[:, :, :], ACT.Copy).then_inc(oT_hi, 1)

        @block.vector
        def _(eng):
            ch = Chain(eng, dve_s)
            eng.wait_ge(w_mm, 1)
            eng.tensor_copy(window[:, :], sh.ps[0:R, 7, 0:128]).then_inc(w_out, 1)
            eng.wait_ge(small_in, 48)
            eng.wait_ge(pool_s, POOL_DONE)

            def prepare(b):
                r = b % 2
                for g in range(NPAGE):
                    eng.wait_ge(k_tr, 2 * b + g + 1)
                    if b >= 2:
                        eng.wait_ge(s_mm, b - 1)
                    eng.tensor_copy(KT[:, r, :, 128 * g:128 * g + 128],
                                    sh.ps[:, g, :].rearrange("p (c n) -> p c n", c=4)).then_inc(k_out, 1)
                ch(eng.tensor_tensor(headc[:, r, :].rearrange("p (h t) -> p h t", h=H_FOX),
                                     head[:, :].rearrange("p (h t) -> p h t", h=H_FOX),
                                     cs[:, DT * b:DT * b + DT].unsqueeze(1).broadcast_to([H_FOX, H_FOX, DT]), ALU.mult))
                ch(eng.tensor_copy(bias[:, r, PAST:], cneg[:, :]))
                eng.wait_ge(b_mm, b + 1)
                eng.tensor_copy(bias[:, r, 0:PAST], sh.ps[0:H_FOX, 2, 0:PAST]).then_inc(b_out, 1)
                eng.wait_ge(s_mm, b + 1)
                ch(eng.reduce_max(mx[:, b:b + 1], sh.ps[0:R, 3 + r, 0:KN], axis=X))
                eng.tensor_scalar(nm[:, b:b + 1], mx[:, b:b + 1], -1.0, None, ALU.mult).then_inc(nm_ready, 1)

            prepare(0)
            for b in range(DB):
                r = b % 2
                if b + 1 < DB:
                    prepare(b + 1)
                eng.wait_ge(exp_done, b + 1)
                ch(eng.reciprocal(rinv[:, b:b + 1], rsum[:, b:b + 1]))
                eng.tensor_scalar(P[:, r, :], P[:, r, :], rinv[:, b:b + 1], None, ALU.mult).then_inc(p_ready, 1)
                eng.wait_ge(p_tr, b + 1)
                if b >= 2:
                    eng.wait_ge(pv_mm, b - 1)
                ch(eng.tensor_copy(PT[0:64, r, 2, :], sh.ps[0:64, 5, 2 * R:3 * R]))
                eng.tensor_copy(PT[:, r, 0:2, :], sh.ps[:, 5, 0:2 * R].rearrange("p (g n) -> p g n", g=2)).then_inc(pt_out, 1)
                eng.wait_ge(pv_mm, b + 1)
                o = sh.ps[:, 6, 0:4 * 80].rearrange("p (c n) -> p c n", c=4)
                eng.tensor_copy(oT[0:64, :, DT * b:DT * b + DT], o[0:64, :, 0:DT])
                eng.tensor_copy(oT[64:128, :, DT * b:DT * b + DT], o[64:128, :, DT:2 * DT]).then_inc(o_out, 1)
            eng.wait_ge(oT_hi, 1)
            eng.tensor_tensor(ol[:, :, :], oT[:, :, :], f32(oh[:, :, :]), ALU.subtract).then_inc(oT_lo, 1)


def stage_gates(nc, sh):
    UJ = 24
    with ExitStack() as ctx:
        def sb(name, shape, dt=F32):
            return ctx.enter_context(nc.sbuf_tensor("gt_" + name, shape, dt))

        def sem(name):
            return sh.front_sem("gt_" + name)
        w_raw = sb("w_raw", [128, 2, 12, 128])
        w_hi, w_lo = sb("w_hi", [128, 2, 2, 12, 128], F32R), sb("w_lo", [128, 2, 2, 12, 128], F32R)
        oh, ol = sb("oh", [128, 4, TOK], F32R), sb("ol", [128, 4, TOK], F32R)
        sg = sb("sg", [128, 4, 384])
        (loaded, head, split, o_in, gate_mm, br_mm, sg_ready, mul_done, m_done) = (sem(n) for n in (
            "loaded", "head", "split", "o_in", "gate_mm", "br_mm", "sg_ready", "mul_done", "m_done"))
        block = ctx.enter_context(nc.Block())

        def load(eng, j, cp, n):
            if not isinstance(n, int) or n > 0:
                eng.wait_ge(split, n)
            for c in range(2):
                col = (2 * cp + c) * 128
                eng.dma_start(w_raw[:, c, 0:8, :],
                              sh.w_in[0, :, bass.ds(GATE + col + j * D, 128)].rearrange("(k p) n -> p k n", p=128)
                              ).then_inc(loaded, 16)
                eng.dma_start(w_raw[:, c, 8:12, :],
                              sh.w_branch[0, bass.ds(j, 1), :, col:col + 128].rearrange("o (k p) n -> p (o k) n", p=128)
                              ).then_inc(loaded, 16)

        def take_head(eng, n, s):
            eng.wait_ge(loaded, 64 * (n + 1))
            eng.activation(w_hi[:, s % 2], w_raw[:], ACT.Copy).then_inc(head, 1)

        def take_tail(eng, n, s):
            eng.wait_ge(head, n + 1)
            eng.tensor_tensor(w_lo[:, s % 2], w_raw[:], f32(w_hi[:, s % 2]), ALU.subtract).then_inc(split, 1)

        @block.gpsimd
        def _(eng):
            eng.memset(sh.m[:, :, :], 0.0).then_inc(m_done, 1)

        @block.sync
        def _(eng):
            load(eng, 0, 0, 0)
            load(eng, 0, 1, 1)

            def branch(j, last):
                eng.wait_ge(m_done, UJ * j + 1)
                for dst, src in ((oh, sh.oT_hi), (ol, sh.oT_lo)):
                    eng.dma_start(f32(dst[:, :, :]), src[bass.ds(j, 1)].rearrange("o (k p) n -> p (o k) n", p=128)
                                  ).then_inc(o_in, 16)
                for s in range(2 if last else 4):
                    load(eng, j if s < 2 else j + 1, (s + 2) % 4, 4 * j + s + 2)
            with eng.Fori(0, 2) as j:
                branch(j, False)
            branch(2, True)

        @block.tensor
        def _(eng):
            def branch(j):
                eng.wait_ge(m_done, UJ * j + 1)
                for s in range(4):
                    eng.wait_ge(split, 4 * j + s + 1)
                    for c in range(2):
                        for kind, bank0, ks, hi, lo, done in (("gate", 0, range(8), sh.xh, sh.xl, gate_mm),
                                                              ("branch", 4, range(4), oh, ol, br_mm)):
                            if kind == "branch" and s == 0 and c == 0:
                                eng.wait_ge(o_in, 32 * j + 32)
                            for g, (t0, tn) in enumerate(GROUPS):
                                v = 3 * (2 * s + c) + g
                                if v >= 4:
                                    eng.wait_ge(m_done, UJ * j + v - 2)
                                out = sh.ps[:, bank0 + v % 4, 0:tn]
                                for k in ks:
                                    wk = k + (8 if bank0 else 0)
                                    for i, (w, x) in enumerate(((w_hi, hi), (w_hi, lo), (w_lo, hi))):
                                        last = eng.matmul(out, w[:, s % 2, c, wk, :], x[:, k, t0:t0 + tn],
                                                          start=(k == 0 and i == 0), stop=(k == ks[-1] and i == 2))
                                last.then_inc(done, 1)
            with eng.Fori(0, 2) as j:
                branch(j)
            branch(2)

        @block.scalar
        def _(eng):
            take_head(eng, 0, 0)
            take_head(eng, 1, 1)

            def branch(j, last):
                for s in range(4):
                    for u in range(6):
                        v = 6 * s + u
                        t0, tn = GROUPS[u % 3]
                        eng.wait_ge(gate_mm, UJ * j + v + 1)
                        eng.activation(sg[:, v % 4, 0:tn], sh.ps[:, v % 4, 0:tn], ACT.Sigmoid).then_inc(sg_ready, 1)
                    if not last or s < 2:
                        eng.wait_ge(br_mm, UJ * j + 6 * s + 6)
                        take_head(eng, 4 * j + s + 2, s)
            with eng.Fori(0, 2) as j:
                branch(j, False)
            branch(2, True)

        @block.vector
        def _(eng):
            take_tail(eng, 0, 0)
            take_tail(eng, 1, 1)
            eng.wait_ge(m_done, 1)

            def branch(j, last):
                for s in range(4):
                    for u in range(6):
                        v = 6 * s + u
                        t0, tn = GROUPS[u % 3]
                        fb = 2 * s + u // 3
                        eng.wait_ge(sg_ready, UJ * j + v + 1)
                        eng.wait_ge(br_mm, UJ * j + v + 1)
                        eng.tensor_tensor(sg[:, v % 4, 0:tn], sh.ps[:, 4 + v % 4, 0:tn], sg[:, v % 4, 0:tn],
                                          ALU.mult).then_inc(mul_done, 1)
                        eng.wait_ge(mul_done, UJ * j + v + 1)
                        eng.tensor_tensor(sh.m[:, fb, t0:t0 + tn], sh.m[:, fb, t0:t0 + tn], sg[:, v % 4, 0:tn],
                                          ALU.add).then_inc(m_done, 1)
                    if not last or s < 2:
                        take_tail(eng, 4 * j + s + 2, s)
            with eng.Fori(0, 2) as j:
                branch(j, False)
            branch(2, True)


def tile_rows(t):
    return (128 * t, 0) if t < 8 else (TOK - 128, 64)


def stage_out(nc, sh):
    with ExitStack() as ctx:
        def sb(name, shape, dt=F32):
            return ctx.enter_context(nc.sbuf_tensor("wo_" + name, shape, dt))

        def sem(name):
            return sh.front_sem("wo_" + name)
        w_raw = sb("w_raw", [128, 2, D])
        w_hi, w_lo = sb("w_hi", [128, KC, D], F32R), sb("w_lo", [128, KC, D], F32R)
        x = w_raw
        r = sb("r", [128, D])
        x1 = sb("x1", [128, 2, D])
        x1T = sb("x1T", [128, KC, 128])
        gb, bb = sb("gb", [128, D]), sb("bb", [128, D])
        wr, brb = sb("wr", [128, KC, NE]), sb("brb", [128, NE])
        st, mv = sb("st", [128, 2, 6]), sb("mv", [128, 2])
        std, rstd = sb("std", [128, 1]), sb("rstd", [128, 1])
        (c_in, w_in0, w_in1, w_head, w_tail, m_head, m_tail, x_in0, x_in1, mix_mm, dve_s, var_ready, std_ready, x1_ready, x1_tr,
         x1T_out, lg_mm, lg_out, r_ready) = (sem(n) for n in (
             "c_in", "w_in0", "w_in1", "w_head", "w_tail", "m_head", "m_tail", "x_in0", "x_in1", "mix_mm", "dve", "var_ready",
             "std_ready", "x1_ready", "x1_tr", "x1T_out", "lg_mm", "lg_out", "r_ready"))
        x_in, w_in = [x_in0, x_in1], [w_in0, w_in1]
        stored0, stored1 = stored = [sh.dma_sem(f"wo_stored{i}") for i in range(2)]
        block = ctx.enter_context(nc.Block())

        @block.sync
        def _(eng):
            for k in range(KC):
                if k >= 2:
                    eng.wait_ge(w_tail, k - 1)
                eng.dma_start(w_raw[:, k % 2, :], sh.w_out[0, 128 * k:128 * k + 128, :]).then_inc(w_in[k % 2], 16)
                if k == 1:
                    for dst, src in ((gb, sh.ln1_g), (bb, sh.ln1_b)):
                        eng.dma_start(dst[:, :], src.broadcast_to([128, D])).then_inc(c_in, 16)
                    eng.dma_start(brb[:, :], sh.b_router.unsqueeze(0).broadcast_to([128, NE])).then_inc(c_in, 16)
                    eng.dma_start(wr[:, :, :], sh.w_router.rearrange("(k p) n -> p k n", p=128)).then_inc(c_in, 16)
            for t in range(NT):
                if t >= 2:
                    eng.wait_ge(r_ready, t - 1)
                else:
                    eng.wait_ge(w_tail, KC - 1 + t)
                if t < 8:
                    eng.dma_start(x[:, t % 2, :], sh.x_prompt[0, 128 * t:128 * t + 128, :]).then_inc(x_in[t % 2], 16)
                else:
                    eng.dma_start(x[0:64, t % 2, :], sh.x_prompt[0, SEQ - 64:SEQ, :]).then_inc(x_in[t % 2], 16)
                    eng.dma_start(x[64:128, t % 2, :], sh.x_sample.rearrange("b t d -> (b t) d")).then_inc(x_in[t % 2], 16)

        @block.gpsimd
        def _(eng):
            for t in range(NT):
                t0, p0 = tile_rows(t)
                eng.wait_ge(x1_ready, t + 1)
                eng.dma_start(sh.x1_dram[t0 + p0:t0 + 128, :], x1[p0:128, t % 2, :]).then_inc(stored[t % 2], 16)
            eng.wait_ge(stored0, 16 * 5)
            eng.wait_ge(stored1, 16 * 4)

        @block.tensor
        def _(eng):
            def router(t):
                eng.wait_ge(x1_ready, t + 1)
                for half in range(2):
                    u = 2 * t + half
                    if u >= 2:
                        eng.wait_ge(x1T_out, u - 1)
                    for k in range(4):
                        c0 = 128 * (4 * half + k)
                        last = eng.transpose(sh.ps[:, 4 + half, 128 * k:128 * k + 128], x1[:, t % 2, c0:c0 + 128],
                                             sh.ident[:, :])
                    last.then_inc(x1_tr, 1)
                eng.wait_ge(x1T_out, 2 * t + 2)
                if t >= 1:
                    eng.wait_ge(lg_out, t)
                for k in range(KC):
                    last = eng.matmul(sh.ps[:, 6, 0:NE], x1T[:, k, :], wr[:, k, :], start=(k == 0), stop=(k == KC - 1))
                last.then_inc(lg_mm, 1)

            eng.wait_ge(c_in, 64)
            eng.wait_ge(w_tail, KC)
            eng.wait_ge(m_tail, KC)
            for t in range(NT):
                t0, _p0 = tile_rows(t)
                if t >= 2:
                    eng.wait_ge(r_ready, t - 1)
                for half in range(2):
                    out = sh.ps[:, 2 * (t % 2) + half, :]
                    for k in range(KC):
                        for i, (m, w) in enumerate(((sh.xh, w_hi), (sh.xl, w_hi), (sh.xh, w_lo))):
                            last = eng.matmul(out, m[:, k, t0:t0 + 128], w[:, k, 512 * half:512 * half + 512],
                                              start=(k == 0 and i == 0), stop=(k == KC - 1 and i == 2))
                last.then_inc(mix_mm, 1)
                if t >= 1:
                    router(t - 1)
            router(NT - 1)

        @block.scalar
        def _(eng):
            for k in range(KC):
                eng.wait_ge(w_in[k % 2], 16 * (k // 2 + 1))
                eng.activation(w_hi[:, k, :], w_raw[:, k % 2, :], ACT.Copy).then_inc(w_head, 1)
                eng.activation(sh.xh[:, k, :], sh.m[:, k, :], ACT.Copy).then_inc(m_head, 1)
            for t in range(NT + 1):
                if t < NT:
                    eng.wait_ge(var_ready, t + 1)
                    eng.activation(std[:, :], mv[:, 1:2], ACT.Sqrt).then_inc(std_ready, 1)
                if t >= 1:
                    for half in range(2):
                        eng.wait_ge(x1_tr, 2 * (t - 1) + half + 1)
                        if t >= 2 and half == 0:
                            eng.wait_ge(lg_mm, t - 1)
                        eng.activation(x1T[:, 4 * half:4 * half + 4, :],
                                       sh.ps[:, 4 + half, :].rearrange("p (k n) -> p k n", k=4), ACT.Copy).then_inc(x1T_out, 1)

        @block.vector
        def _(eng):
            for k in range(KC):
                eng.wait_ge(w_head, k + 1)
                eng.tensor_tensor(w_lo[:, k, :], w_raw[:, k % 2, :], f32(w_hi[:, k, :]), ALU.subtract).then_inc(w_tail, 1)
                eng.wait_ge(m_head, k + 1)
                eng.tensor_tensor(sh.xl[:, k, :], sh.m[:, k, :], f32(sh.xh[:, k, :]), ALU.subtract).then_inc(m_tail, 1)
            eng.wait_ge(c_in, 64)
            ch = Chain(eng, dve_s)
            for t in range(NT + 1):
                if t < NT:
                    eng.wait_ge(mix_mm, t + 1)
                    eng.wait_ge(x_in[t % 2], 16 * (t // 2 + 1) if t < 8 else 16 * 6)
                    eng.scalar_tensor_tensor(out=r[:, :], in0=x[:, t % 2, :], scalar=ALPHA,
                                             in1=sh.ps[:, 2 * (t % 2):2 * (t % 2) + 2, :].rearrange("p a n -> p (a n)"),
                                             op0=ALU.mult, op1=ALU.add).then_inc(r_ready, 1)
                    eng.wait_ge(r_ready, t + 1)
                    for half in range(2):
                        ch(eng.bn_stats(st[:, half, :], r[:, 512 * half:512 * half + 512]))
                    ch(eng.bn_aggr(mv[:, :], st[:, :, :].rearrange("p a n -> p (a n)")))
                    eng.tensor_scalar(mv[:, 1:2], mv[:, 1:2], EPS, None, ALU.add).then_inc(var_ready, 1)
                if t >= 1:
                    eng.wait_ge(lg_mm, t)
                    eng.tensor_tensor(sh.lg[:, t - 1, :], sh.ps[:, 6, 0:NE], brb[:, :], ALU.add).then_inc(lg_out, 1)
                if t < NT:
                    eng.wait_ge(std_ready, t + 1)
                    ch(eng.reciprocal(rstd[:, :], std[:, :]))
                    ch(eng.tensor_scalar(r[:, :], r[:, :], mv[:, 0:1], rstd[:, :], ALU.subtract, ALU.mult))
                    ch(eng.tensor_tensor(r[:, :], r[:, :], gb[:, :], ALU.mult))
                    if t >= 2:
                        eng.wait_ge(stored[t % 2], 16 * (t // 2))
                        eng.wait_ge(x1_tr, 2 * (t - 1))
                    eng.tensor_tensor(x1[:, t % 2, :], r[:, :], bb[:, :], ALU.add).then_inc(x1_ready, 1)
                    eng.wait_ge(x1_ready, t + 1)


TILE = 256
NTILE = (2 * TOK - NE) // TILE + NE
NSLOT = NTILE * TILE
NB = NSLOT // 128


def stage_route(nc, sh):
    with ExitStack() as ctx:
        def sb(name, shape, dt=F32):
            return ctx.enter_context(nc.sbuf_tensor("rt_" + name, shape, dt))

        def sem(name):
            return ctx.enter_context(nc.semaphore("rt_" + name))
        N4 = NT * NG
        e, p, pm, eq, oh1, oh2, ohc, rank, slot = (sb(n, [128, NT, NE]) for n in (
            "e", "p", "pm", "eq", "oh1", "oh2", "ohc", "rank", "slot"))
        s6, gs, geq, gsel = sb("s6", [128, N4, 6]), sb("gs", [128, NT, NG]), sb("geq", [128, NT, NG]), sb("gsel", [128, NT, NG])
        a, b, v1, v2 = (sb(n, [128, NT]) for n in ("a", "b", "v1", "v2"))
        desc = sb("desc", [128, NE])
        cnt, nt, incl, off, one16 = (sb(n, [128, NE]) for n in ("cnt", "nt", "incl", "off", "one16"))
        tot = sb("tot", [128, NT, NE])
        before_, ones = sb("before", [128, 128]), sb("ones", [128, 128])
        sloti, blk, pos = (sb(n, [128, 2, NT], I32) for n in ("sloti", "blk", "pos"))
        addr = sb("addr", [128, 2, NT], U32)
        dummy = sb("dummy", [64, 2], I32)
        tokid = sb("tokid", [128, NT], U32)
        tokf = sb("tokf", [128, NT], I32)
        zeros = sb("zeros", [128, NB + 1], U32)
        ti = sb("ti", [1, NTILE])
        tcmp, tsum = sb("tcmp", [1, NTILE, NE]), sb("tsum", [1, NTILE])
        (pool_s, dve_s, act_s, exp_in, oh_ready, r_mm, a_ready, cleared, scattered, idx_in) = (sem(n) for n in (
            "pool", "dve", "act", "exp_in", "oh_ready", "r_mm", "a_ready", "cleared", "scattered", "idx_in"))
        block = ctx.enter_context(nc.Block())

        @block.gpsimd
        def _(eng):
            ch = Chain(eng, pool_s)
            ch(eng.memset(zeros[:, :], 0))
            eng.dma_start(sh.slot_tok[0:128 * (NB + 1), :].rearrange("(p b) o -> p (b o)", p=128), zeros[:, :]
                          ).then_inc(cleared, 16)
            ch(eng.iota(desc[:, :], pattern=[[-1, NE]], base=NE, channel_multiplier=0,
                        allow_small_or_imprecise_dtypes=True))
            ch(eng.iota(ti[:, :], pattern=[[1, NTILE]], base=0, channel_multiplier=0,
                        allow_small_or_imprecise_dtypes=True))
            ch(eng.memset(ones[:, :], 1.0))
            ch(eng.memset(one16[:, :], 1.0))
            ch(eng.memset(before_[:, :], 1.0))
            ch(eng.affine_select(out=before_[:, :], in_=before_[:, :], compare_op=ALU.is_gt, fill=0.0, base=0,
                                 pattern=[[1, 128]], channel_multiplier=-1))
            ch(eng.iota(tokf[:, 0:8], pattern=[[128, 8]], base=0, channel_multiplier=1))
            ch(eng.iota(tokf[:, 8:9], pattern=[[0, 1]], base=TOK - 128, channel_multiplier=1))
            ch(eng.tensor_copy(tokid[:, :], tokf[:, :]))
            ch(eng.iota(dummy[:, :], pattern=[[64, 2]], base=NSLOT, channel_multiplier=1))
            eng.wait_ge(a_ready, 1)
            eng.wait_ge(cleared, 16)
            for c in range(2):
                for t in range(NT):
                    eng.indirect_dma_start(out=sh.slot_tok[:, :],
                                           out_offset=bass.IndirectOffsetOnAxis(ap=addr[:, c, t:t + 1], axis=0),
                                           in_=tokid[:, t:t + 1], in_offset=None).then_inc(scattered, 16)
            eng.wait_ge(scattered, 16 * 2 * NT)
            eng.dma_start(sh.slot_idx[:, :], sh.slot_tok[0:NSLOT, :].rearrange("(p b) o -> p (b o)", p=128)
                          ).then_inc(idx_in, 16)
            eng.wait_ge(idx_in, 16)
        POOL_DONE = 11

        @block.scalar
        def _(eng):
            eng.wait_ge(exp_in, 1)
            eng.activation(e[:, :, :], e[:, :, :], ACT.Exp).then_inc(act_s, 1)

        @block.tensor
        def _(eng):
            eng.wait_ge(pool_s, POOL_DONE)
            eng.wait_ge(oh_ready, 1)
            rhs = ohc[:, :, :].rearrange("p t e -> p (t e)")
            eng.matmul(sh.ps[:, 0, 0:NT * NE], before_[:, :], rhs, start=True, stop=True)
            eng.matmul(sh.ps[:, 1, 0:NT * NE], ones[:, :], rhs, start=True, stop=True).then_inc(r_mm, 1)

        @block.vector
        def _(eng):
            ch = Chain(eng, dve_s)
            tt, ts = eng.tensor_tensor, eng.tensor_scalar

            def wide(ap, n=NE):
                return ap.unsqueeze(2).broadcast_to([128, ap.shape[1], n])

            def first_max(value, best, out, k):
                ch(eng.reduce_max(best, value, axis=X))
                ch(tt(out, value, wide(best, k), ALU.is_equal))
                ch(tt(out, out, desc[:, NE - k:].unsqueeze(1).broadcast_to([128, NT, k]), ALU.mult))
                ch(eng.reduce_max(b[:, :], out, axis=X))
                ch(tt(out, out, wide(b[:, :], k), ALU.is_equal))

            eng.wait_ge(pool_s, POOL_DONE)
            ch(eng.reduce_max(a[:, :], sh.lg[:, :, :], axis=X))
            tt(e[:, :, :], sh.lg[:, :, :], wide(a[:, :]), ALU.subtract).then_inc(exp_in, 1)
            eng.wait_ge(act_s, 1)
            ch(eng.reduce_sum(a[:, :], e[:, :, :], axis=X))
            ch(eng.reciprocal(a[:, :], a[:, :]))
            ch(tt(p[:, :, :], e[:, :, :], wide(a[:, :]), ALU.mult))
            pg = p[:, :, :].rearrange("p t (g n) -> p (t g) n", g=NG)
            at = 0
            for d in (1, 2, 3):
                ch(tt(s6[:, :, at:at + 4 - d], pg[:, :, 0:4 - d], pg[:, :, d:4], ALU.add))
                at += 4 - d
            ch(eng.reduce_max(gs[:, :, :].rearrange("p t g -> p (t g)"), s6[:, :, :], axis=X))
            first_max(gs[:, :, :], a[:, :], gsel[:, :, :], NG)
            ch(ts(geq[:, :, :], gsel[:, :, :], -1.0, None, ALU.add))
            g4 = lambda ap: ap.rearrange("p t g -> p (t g)").unsqueeze(2).broadcast_to([128, N4, EPG])
            pmg = pm[:, :, :].rearrange("p t (g n) -> p (t g) n", g=NG)
            ch(tt(pmg, pg, g4(gsel[:, :, :]), ALU.mult))
            ch(tt(pmg, pmg, g4(geq[:, :, :]), ALU.add))
            first_max(pm[:, :, :], v1[:, :], oh1[:, :, :], NE)
            ch(eng.scalar_tensor_tensor(out=pm[:, :, :], in0=oh1[:, :, :], scalar=-4.0, in1=pm[:, :, :],
                                        op0=ALU.mult, op1=ALU.add))
            first_max(pm[:, :, :], v2[:, :], oh2[:, :, :], NE)
            ch(tt(a[:, :], v1[:, :], v2[:, :], ALU.add))
            ch(eng.reciprocal(a[:, :], a[:, :]))
            ch(tt(sh.wt[:, 0, :], v1[:, :], a[:, :], ALU.mult))
            ch(tt(sh.wt[:, 1, :], v2[:, :], a[:, :], ALU.mult))
            ch(tt(ohc[:, :, :], oh1[:, :, :], oh2[:, :, :], ALU.add))
            eng.memset(ohc[0:64, NT - 1, :], 0.0).then_inc(oh_ready, 1)
            eng.wait_ge(r_mm, 1)
            ch(eng.tensor_copy(rank[:, :, :], sh.ps[:, 0, 0:NT * NE].rearrange("p (t e) -> p t e", t=NT)))
            ch(eng.tensor_copy(tot[:, :, :], sh.ps[:, 1, 0:NT * NE].rearrange("p (t e) -> p t e", t=NT)))
            ch(eng.tensor_copy(cnt[:, :], tot[:, 0, :]))
            for t in range(1, NT):
                ch(tt(rank[:, t, :], rank[:, t, :], cnt[:, :], ALU.add))
                ch(tt(cnt[:, :], cnt[:, :], tot[:, t, :], ALU.add))
            ch(ts(nt[:, :], cnt[:, :], 0.0, None, ALU.is_gt))
            for k in range(1, -(-TOK // TILE)):
                ch(eng.scalar_tensor_tensor(out=nt[:, :], in0=cnt[:, :], scalar=float(TILE * k), in1=nt[:, :],
                                            op0=ALU.is_gt, op1=ALU.add))
            ch(eng.tensor_tensor_scan(incl[:, :], one16[:, :], nt[:, :], 0.0, ALU.mult, ALU.add))
            ch(tt(off[:, :], incl[:, :], nt[:, :], ALU.subtract))
            ch(ts(off[:, :], off[:, :], float(TILE), None, ALU.mult))
            ch(tt(rank[:, :, :], rank[:, :, :], off[:, :].unsqueeze(1).broadcast_to([128, NT, NE]), ALU.add))
            for c, oh in enumerate((oh1, oh2)):
                ch(tt(slot[:, :, :], rank[:, :, :], oh[:, :, :], ALU.mult))
                ch(eng.reduce_sum(a[:, :], slot[:, :, :], axis=X))
                ch(eng.memset(a[0:64, NT - 1:NT], 0.0))
                ch(eng.tensor_copy(sloti[:, c, :], a[:, :]))
            ch(eng.tensor_copy(sh.slots[:, :, :], sloti[:, :, :]))
            ch(ts(blk[:, :, :], sloti[:, :, :], 7, None, ALU.arith_shift_right))
            ch(ts(pos[:, :, :], sloti[:, :, :], 127, None, ALU.bitwise_and))
            ch(eng.scalar_tensor_tensor(out=pos[:, :, :], in0=pos[:, :, :], scalar=float(NB), in1=blk[:, :, :],
                                        op0=ALU.mult, op1=ALU.add))
            ch(eng.tensor_copy(pos[0:64, :, NT - 1], dummy[:, :]))
            eng.tensor_copy(addr[:, :, :], pos[:, :, :]).then_inc(a_ready, 1)
            ch(tt(tcmp[:, :, :], incl[0:1, :].unsqueeze(1).broadcast_to([1, NTILE, NE]),
                  ti[:, :].unsqueeze(2).broadcast_to([1, NTILE, NE]), ALU.is_le))
            ch(eng.reduce_sum(tsum[:, :], tcmp[:, :, :], axis=X))
            ch(ts(tsum[:, :], tsum[:, :], float(NE - 1), None, ALU.min))
            ch(eng.tensor_copy(sh.eid[:, :], tsum[:, :]))


def stage_moe(nc, sh):
    with ExitStack() as ctx:
        def sb(name, shape, dt=F32):
            return ctx.enter_context(nc.sbuf_tensor("mo_" + name, shape, dt))

        def sem(name):
            return ctx.enter_context(nc.semaphore("mo_" + name))
        raw = [sb(f"raw{m}", [128, 2048]) for m in "gud"]
        hi = [sb(f"hi{m}", [128, 2, 2048], F32R) for m in "gud"]
        lo = [sb(f"lo{m}", [128, 2, 2048], F32R) for m in "gud"]
        idx = sb("idx", [128, 2, 2], U32)
        probe = sb("probe", [128, 2])
        xg = sb("xg", [128, 2, 2, D])
        xh, xl = sb("xh", [128, 2, KC, TILE], F32R), sb("xl", [128, 2, KC, TILE], F32R)
        sg, t_, h = (sb(n, [128, 2 * TILE]) for n in ("sg", "t", "h"))
        hh, hl = sb("hh", [128, 2, 2, TILE], F32R), sb("hl", [128, 2, 2, TILE], F32R)
        y = sb("y", [128, 2, D])
        w_in = [sem(f"w_in{m}") for m in "gud"]
        w_head = [sem(f"w_head{m}") for m in "gud"]
        w_tail = [sem(f"w_tail{m}") for m in "gud"]
        (idx_ready, x_in0, x_in1, x_tr, x_head, x_tail, g_mm, u_mm, sg_ready, t_ready, h_ready, hh_ready, hl_ready, y_mm,
         y_out, y_st0, y_st1) = (sem(n) for n in (
             "idx_ready", "x_in0", "x_in1", "x_tr", "x_head", "x_tail", "g_mm", "u_mm", "sg_ready", "t_ready", "h_ready",
             "hh_ready", "hl_ready", "y_mm", "y_out", "y_st0", "y_st1"))
        x_in, y_st = [x_in0, x_in1], [y_st0, y_st1]
        y_rows = sh.y_dram.rearrange("(i j p) n -> i j p n", j=2, p=128)
        LAST = NTILE // 2 - 1
        block = ctx.enter_context(nc.Block())

        def wait(eng, sem, value):
            if not isinstance(value, int) or value > 0:
                eng.wait_ge(sem, value)

        @block.sync
        def _(eng):
            def load(i, r):
                ex = eng.value_load(sh.eid[0:1, bass.ds(i, 1)], min_val=0, max_val=NE - 1)
                for m, w in enumerate((sh.w_e_gate, sh.w_e_up, sh.w_e_down)):
                    wait(eng, w_tail[m], i)
                    k = w.shape[2] // 128
                    eng.dma_start(raw[m][:, :].rearrange("p (k n) -> p k n", k=k),
                                  w[0, bass.ds(ex, 1)].rearrange("o (k p) n -> p (o k) n", p=128)).then_inc(w_in[m], 16)

            def body(i, r, more):
                if more:
                    load(i + 2, r)
                for j in range(2):
                    eng.wait_ge(y_out, 4 * i + 2 * j + 2)
                    eng.dma_start(y_rows[bass.ds(i, 1), j].rearrange("o p n -> (o p) n"), y[:, j, :]).then_inc(y_st[j], 16)
            load(0, 0)
            load(1, 1)
            body(0, 0, True)
            body(1, 1, True)
            with eng.Fori(1, LAST) as q:
                body(2 * q, 0, True)
                body(2 * q + 1, 1, True)
            body(NTILE - 2, 0, False)
            body(NTILE - 1, 1, False)
            for j in range(2):
                eng.wait_ge(y_st[j], 16 * NTILE)

        @block.gpsimd
        def _(eng):
            def gather(i, r, tiles_done):
                if tiles_done is not None:
                    eng.wait_ge(x_tr, tiles_done)
                eng.tensor_copy(idx[:, r, :], sh.slot_idx[:, bass.ds(2 * i, 2)]).then_inc(idx_ready, 1)
                eng.wait_ge(idx_ready, i + 1)
                eng.tensor_tensor(probe[:, 1:2], probe[:, 0:1], probe[:, 0:1], ALU.add)
                for j in range(2):
                    eng.indirect_dma_start(out=xg[:, r, j, :], out_offset=None, in_=sh.x1_dram[:, :],
                                           in_offset=bass.IndirectOffsetOnAxis(ap=idx[:, r, j:j + 1], axis=0)
                                           ).then_inc(x_in[r], 16)
            eng.memset(probe[:, :], 0.0)
            gather(0, 0, None)
            gather(1, 1, None)
            with eng.Fori(0, LAST) as q:
                for r in range(2):
                    i = 2 * q + r
                    gather(i + 2, r, 4 * i + 4)

        @block.tensor
        def _(eng):
            def transpose(i, r, pair, quarters, first=False):
                if quarters[0] == 0:
                    eng.wait_ge(x_in[r], 32 * pair + 32)
                for q in quarters:
                    if not (first and q < 2):
                        eng.wait_ge(x_tail, 4 * i + q - 1)
                    for k in range(2):
                        for j in range(2):
                            c0 = 128 * (2 * q + k)
                            last = eng.transpose(sh.ps[:, q % 2, TILE * k + 128 * j:TILE * k + 128 * j + 128],
                                                 xg[:, r, j, c0:c0 + 128], sh.ident[:, :])
                    last.then_inc(x_tr, 1)

            def in_product(i, r, m, done):
                eng.wait_ge(w_tail[m], i + 1)
                if m == 0:
                    eng.wait_ge(x_tail, 4 * i + 4)
                    wait(eng, h_ready, i - 1)
                for f in range(2):
                    out = sh.ps[:, 2 + 2 * r + m, TILE * f:TILE * f + TILE]
                    for k in range(KC):
                        w0 = DE * k + 128 * f
                        for a, (w, x) in enumerate(((hi, xh), (hi, xl), (lo, xh))):
                            last = eng.matmul(out, w[m][:, r, w0:w0 + 128], x[:, r, k, :],
                                              start=(k == 0 and a == 0), stop=(k == KC - 1 and a == 2),
                                              skip_group_check=True)
                last.then_inc(done, 1)

            def down(i, r):
                eng.wait_ge(hl_ready, i + 1)
                eng.wait_ge(w_tail[2], i + 1)
                for j in range(2):
                    for half in range(2):
                        u = 2 * j + half
                        wait(eng, y_out, 4 * i + (u - 1 if u >= 2 else 0))
                        for f in range(2):
                            w0 = D * f + 512 * half
                            for a, (hx, w) in enumerate(((hh, hi), (hl, hi), (hh, lo))):
                                last = eng.matmul(sh.ps[:, 6 + half, :], hx[:, r, f, 128 * j:128 * j + 128],
                                                  w[2][:, r, w0:w0 + 512],
                                                  start=(f == 0 and a == 0), stop=(f == 1 and a == 2))
                        last.then_inc(y_mm, 1)

            def body(i, r, pair, more, most):
                if most:
                    transpose(i + 2, r, pair + 1, (0, 1))
                if more:
                    in_product(i + 1, 1 - r, 0, g_mm)
                if most:
                    transpose(i + 2, r, pair + 1, (2, 3))
                if more:
                    in_product(i + 1, 1 - r, 1, u_mm)
                down(i, r)

            transpose(0, 0, 0, (0, 1, 2, 3), True)
            transpose(1, 1, 0, (0, 1))
            in_product(0, 0, 0, g_mm)
            transpose(1, 1, 0, (2, 3))
            in_product(0, 0, 1, u_mm)
            body(0, 0, 0, True, True)
            body(1, 1, 0, True, True)
            with eng.Fori(1, LAST) as q:
                body(2 * q, 0, q, True, True)
                body(2 * q + 1, 1, q, True, True)
            body(NTILE - 2, 0, LAST, True, False)
            body(NTILE - 1, 1, LAST, False, False)

        @block.scalar
        def _(eng):
            def head(i, r, m):
                eng.wait_ge(w_in[m], 16 * i + 16)
                eng.activation(hi[m][:, r, :], raw[m][:, :], ACT.Copy).then_inc(w_head[m], 1)

            def x_heads(i, r, quarters):
                for q in quarters:
                    eng.wait_ge(x_tr, 4 * i + q + 1)
                    eng.activation(xh[:, r, 2 * q:2 * q + 2, :],
                                   sh.ps[:, q % 2, :].rearrange("p (k n) -> p k n", k=2), ACT.Copy).then_inc(x_head, 1)

            def sigmoid(i, r):
                eng.wait_ge(g_mm, i + 1)
                wait(eng, t_ready, i)
                eng.activation(sg[:, :], sh.ps[:, 2 + 2 * r, :], ACT.Sigmoid).then_inc(sg_ready, 1)

            def h_head(i, r):
                eng.wait_ge(h_ready, i + 1)
                eng.activation(hh[:, r].rearrange("p f n -> p (f n)"), h[:, :], ACT.Copy).then_inc(hh_ready, 1)

            def body(i, r, more, most):
                if most:
                    x_heads(i + 2, r, (0, 1))
                    eng.wait_ge(g_mm, i + 1)
                    head(i + 2, r, 0)
                if more:
                    sigmoid(i + 1, 1 - r)
                if most:
                    x_heads(i + 2, r, (2, 3))
                    eng.wait_ge(u_mm, i + 1)
                    head(i + 2, r, 1)
                if more:
                    wait(eng, y_mm, 4 * i)
                    h_head(i + 1, 1 - r)
                for u in range(4):
                    j, half = divmod(u, 2)
                    eng.wait_ge(y_mm, 4 * i + u + 1)
                    if half == 0:
                        wait(eng, y_st[j], 16 * i)
                    eng.activation(y[:, j, 512 * half:512 * half + 512], sh.ps[:, 6 + half, :], ACT.Copy).then_inc(y_out, 1)
                if most:
                    head(i + 2, r, 2)

            for i in range(2):
                for m in range(3):
                    head(i, i, m)
                x_heads(i, i, (0, 1, 2, 3))
            sigmoid(0, 0)
            h_head(0, 0)
            body(0, 0, True, True)
            body(1, 1, True, True)
            with eng.Fori(1, LAST) as q:
                body(2 * q, 0, True, True)
                body(2 * q + 1, 1, True, True)
            body(NTILE - 2, 0, True, False)
            body(NTILE - 1, 1, False, False)

        @block.vector
        def _(eng):
            def tail(i, r, m):
                eng.wait_ge(w_head[m], i + 1)
                eng.tensor_tensor(lo[m][:, r, :], raw[m][:, :], f32(hi[m][:, r, :]), ALU.subtract).then_inc(w_tail[m], 1)

            def x_tails(i, r, quarters):
                for q in quarters:
                    eng.wait_ge(x_head, 4 * i + q + 1)
                    eng.tensor_tensor(xl[:, r, 2 * q:2 * q + 2, :], sh.ps[:, q % 2, :].rearrange("p (k n) -> p k n", k=2),
                                      f32(xh[:, r, 2 * q:2 * q + 2, :]), ALU.subtract).then_inc(x_tail, 1)

            def gate(i, r):
                eng.wait_ge(sg_ready, i + 1)
                wait(eng, h_ready, i)
                eng.tensor_tensor(t_[:, :], sh.ps[:, 2 + 2 * r, :], sg[:, :], ALU.mult).then_inc(t_ready, 1)

            def hidden(i, r):
                eng.wait_ge(u_mm, i + 1)
                eng.wait_ge(t_ready, i + 1)
                wait(eng, hl_ready, i)
                eng.tensor_tensor(h[:, :], sh.ps[:, 3 + 2 * r, :], t_[:, :], ALU.mult).then_inc(h_ready, 1)
                eng.wait_ge(hh_ready, i + 1)
                eng.tensor_tensor(hl[:, r].rearrange("p f n -> p (f n)"), h[:, :],
                                  f32(hh[:, r]).rearrange("p f n -> p (f n)"), ALU.subtract).then_inc(hl_ready, 1)

            def body(i, r, more, most):
                if most:
                    x_tails(i + 2, r, (0, 1))
                    tail(i + 2, r, 0)
                if more:
                    gate(i + 1, 1 - r)
                if most:
                    x_tails(i + 2, r, (2, 3))
                    tail(i + 2, r, 1)
                if more:
                    hidden(i + 1, 1 - r)
                if most:
                    tail(i + 2, r, 2)

            for i in range(2):
                for m in range(3):
                    tail(i, i, m)
                x_tails(i, i, (0, 1, 2, 3))
            gate(0, 0)
            hidden(0, 0)
            body(0, 0, True, True)
            body(1, 1, True, True)
            with eng.Fori(1, LAST) as q:
                body(2 * q, 0, True, True)
                body(2 * q + 1, 1, True, True)
            body(NTILE - 2, 0, True, False)


def stage_combine(nc, sh):
    with ExitStack() as ctx:
        def sb(name, shape, dt=F32):
            return ctx.enter_context(nc.sbuf_tensor("co_" + name, shape, dt))

        def sem(name):
            return ctx.enter_context(nc.semaphore("co_" + name))
        RB = 3
        x1, y1, y2, a, r, o = (sb(n, [128, RB, D]) for n in ("x1", "y1", "y2", "a", "r", "o"))
        gb, bb = sb("gb", [128, D]), sb("bb", [128, D])
        st, mv = sb("st", [128, RB, 2, 6]), sb("mv", [128, RB, 2])
        std, rstd, nmr = sb("std", [128, RB]), sb("rstd", [128, RB]), sb("nmr", [128, RB])
        (c_in, a_ready, dve_s, var_ready, std_ready, rstd_ready, n_ready, g_ready, o_ready, r_ready) = (sem(n) for n in (
            "c_in", "a_ready", "dve", "var_ready", "std_ready", "rstd_ready", "n_ready", "g_ready", "o_ready", "r_ready"))
        t_in = [sem(f"t_in{i}") for i in range(RB)]
        x_in = [sem(f"x_in{i}") for i in range(RB)]
        stored = [sem(f"stored{i}") for i in range(RB)]
        block = ctx.enter_context(nc.Block())

        @block.sync
        def _(eng):
            for t in range(NT + 2):
                if t < NT:
                    if t >= RB:
                        eng.wait_ge(r_ready, t - RB + 1)
                    eng.dma_start(x1[:, t % RB, :], sh.x1_dram[tile_rows(t)[0]:tile_rows(t)[0] + 128, :]).then_inc(x_in[t % RB], 16)
                if t == 0:
                    for dst, src in ((gb, sh.ln2_g), (bb, sh.ln2_b)):
                        eng.dma_start(dst[:, :], src.broadcast_to([128, D])).then_inc(c_in, 16)
                u = t - 2
                if u >= 0:
                    eng.wait_ge(o_ready, u + 1)
                    if u < 8:
                        eng.dma_start(sh.y_prompt[0, 128 * u:128 * u + 128, :], o[:, u % RB, :]).then_inc(stored[u % RB], 16)
                    else:
                        eng.dma_start(sh.y_sample.rearrange("b t d -> (b t) d"), o[64:128, u % RB, :]).then_inc(stored[u % RB], 16)
            for i in range(RB):
                eng.wait_ge(stored[i], 16 * 3)

        @block.gpsimd
        def _(eng):
            def fetch(t):
                if t >= RB:
                    eng.wait_ge(r_ready, t - RB + 1)
                for c, dst in enumerate((y1, y2)):
                    eng.indirect_dma_start(out=dst[:, t % RB, :], out_offset=None, in_=sh.y_dram[:, :],
                                           in_offset=bass.IndirectOffsetOnAxis(ap=sh.slots[:, c, t:t + 1], axis=0)
                                           ).then_inc(t_in[t % RB], 16)
            fetch(0)
            fetch(1)
            eng.wait_ge(c_in, 32)
            for t in range(NT):
                if t + 2 < NT:
                    fetch(t + 2)
                eng.wait_ge(g_ready, t + 1)
                if t >= RB:
                    eng.wait_ge(stored[t % RB], 16 * (t // RB))
                eng.tensor_tensor(o[:, t % RB, :], r[:, t % RB, :], bb[:, :], ALU.add).then_inc(o_ready, 1)

        @block.scalar
        def _(eng):
            for t in range(NT + 1):
                if t < NT:
                    b = t % RB
                    eng.wait_ge(t_in[b], 32 * (t // RB + 1))
                    if t >= RB:
                        eng.wait_ge(r_ready, t - RB + 1)
                    eng.activation(a[:, b, :], y1[:, b, :], ACT.Copy, scale=sh.wt[:, 0, t:t + 1]).then_inc(a_ready, 1)
                    eng.wait_ge(var_ready, t + 1)
                    eng.activation(std[:, b:b + 1], mv[:, b, 1:2], ACT.Sqrt).then_inc(std_ready, 1)
                    eng.wait_ge(rstd_ready, t + 1)
                    eng.activation(r[:, b, :], r[:, b, :], ACT.Identity, scale=rstd[:, b:b + 1],
                                   bias=nmr[:, b:b + 1]).then_inc(n_ready, 1)

        @block.vector
        def _(eng):
            ch = Chain(eng, dve_s)
            eng.wait_ge(c_in, 32)
            for t in range(NT):
                b = t % RB
                eng.wait_ge(a_ready, t + 1)
                eng.wait_ge(x_in[b], 16 * (t // RB + 1))
                ch(eng.scalar_tensor_tensor(out=a[:, b, :], in0=y2[:, b, :], scalar=sh.wt[:, 1, t:t + 1], in1=a[:, b, :],
                                            op0=ALU.mult, op1=ALU.add))
                if t >= RB:
                    eng.wait_ge(o_ready, t - RB + 1)
                eng.scalar_tensor_tensor(out=r[:, b, :], in0=x1[:, b, :], scalar=ALPHA, in1=a[:, b, :],
                                         op0=ALU.mult, op1=ALU.add).then_inc(r_ready, 1)
                eng.wait_ge(r_ready, t + 1)
                for half in range(2):
                    ch(eng.bn_stats(st[:, b, half, :], r[:, b, 512 * half:512 * half + 512]))
                ch(eng.bn_aggr(mv[:, b, :], st[:, b, :, :].rearrange("p a n -> p (a n)")))
                eng.tensor_scalar(mv[:, b, 1:2], mv[:, b, 1:2], EPS, None, ALU.add).then_inc(var_ready, 1)
                eng.wait_ge(std_ready, t + 1)
                ch(eng.reciprocal(rstd[:, b:b + 1], std[:, b:b + 1]))
                eng.scalar_tensor_tensor(out=nmr[:, b:b + 1], in0=mv[:, b, 0:1], scalar=-1.0, in1=rstd[:, b:b + 1],
                                         op0=ALU.mult, op1=ALU.mult).then_inc(rstd_ready, 1)
                eng.wait_ge(n_ready, t + 1)
                eng.tensor_tensor(r[:, b, :], r[:, b, :], gb[:, :], ALU.mult).then_inc(g_ready, 1)




def build(nc, ins, outs, upto=99):
    sh = Shared()
    sh.x_prompt = ins["x_prompt"]
    sh.x_sample = ins["x_sample"]
    sh.cache_fox_k = ins["cache_fox_k"]
    sh.cache_fox_v = ins["cache_fox_v"]
    sh.cache_fox_logf = ins["cache_fox_logf"]
    sh.state_gla = ins["state_gla"]
    sh.state_conv = ins["state_conv"]
    sh.page_table = ins["page_table"]
    sh.w_in = ins["w_in"]
    sh.w_gla_a2 = ins["w_gla_a2"]
    sh.b_gla_a = ins["b_gla_a"]
    sh.gla_norm_g = ins["gla_norm_g"]
    sh.b_fox_f = ins["b_fox_f"]
    sh.conv_w = ins["conv_w"]
    sh.w_branch = ins["w_branch"]
    sh.w_out = ins["w_out"]
    sh.ln1_g = ins["ln1_g"]
    sh.ln1_b = ins["ln1_b"]
    sh.w_router = ins["w_router"]
    sh.b_router = ins["b_router"]
    sh.w_e_gate = ins["w_e_gate"]
    sh.w_e_up = ins["w_e_up"]
    sh.w_e_down = ins["w_e_down"]
    sh.ln2_g = ins["ln2_g"]
    sh.ln2_b = ins["ln2_b"]
    sh.y_prompt = outs["y_prompt"]
    sh.y_sample = outs["y_sample"]
    sh.prompt_fox_k = outs["prompt_fox_k"]
    sh.prompt_fox_v = outs["prompt_fox_v"]
    sh.prompt_fox_logf = outs["prompt_fox_logf"]
    sh.prompt_gla = outs["prompt_gla"]
    sh.prompt_conv = outs["prompt_conv"]
    sh.sample_fox_k = outs["sample_fox_k"]
    sh.sample_fox_v = outs["sample_fox_v"]
    sh.sample_fox_logf = outs["sample_fox_logf"]
    sh.sample_gla = outs["sample_gla"]
    sh.sample_conv = outs["sample_conv"]
    sh.oT_hi = nc.dram_tensor("oT_hi", [3, BW, TOK], F32, kind="Internal").ap()
    sh.oT_lo = nc.dram_tensor("oT_lo", [3, BW, TOK], F32, kind="Internal").ap()
    sh.slot_tok = nc.dram_tensor("slot_tok", [NSLOT + 128, 1], U32, kind="Internal").ap()
    sh.y_dram = nc.dram_tensor("y_dram", [NSLOT, D], F32, kind="Internal").ap()
    sh.x1_dram = nc.dram_tensor("x1_dram", [TOK, D], F32, kind="Internal").ap()
    sh.c_dram = nc.dram_tensor("c_dram", [2, H_FOX, TOK], F32, kind="Internal").ap()
    with ExitStack() as ctx:
        def sb(name, shape, dt=F32):
            return ctx.enter_context(nc.sbuf_tensor(name, shape, dt))

        sems, used = ctx.enter_context(ExitStack()), []

        def sem(name):
            used.append(sems.enter_context(nc.semaphore(name)))
            return used[-1]
        sh.front_sem = sem
        sh.dma_sem = lambda name: ctx.enter_context(nc.semaphore(name))
        sh.ps = ctx.enter_context(nc.psum_tensor("ps", [128, 8, 512], F32))
        sh.ident = sb("ident", [128, 128])
        sh.w_loaded, sh.w_head, sh.w_split = sem("w_loaded"), sem("w_head"), sem("w_split")
        sh.fm_ready = sem("fm_ready")
        sh.fm_free = [sem("fm_free0"), sem("fm_free1")]
        sh.lg = sb("lg", [128, NT, NE])
        sh.wt = sb("wt", [128, 2, NT])
        sh.slots = sb("slots", [128, 2, NT], U32)
        sh.slot_idx = sb("slot_idx", [128, NB], U32)
        sh.eid = sb("eid", [1, NTILE], I32)
        with ExitStack() as dense:
            sh.xh = dense.enter_context(nc.sbuf_tensor("xh", [128, KC, TOK], F32R))
            sh.xl = dense.enter_context(nc.sbuf_tensor("xl", [128, KC, TOK], F32R))
            with ExitStack() as front:
                def fsb(name, shape, dt=F32):
                    return front.enter_context(nc.sbuf_tensor(name, shape, dt))
                sh.w_raw = fsb("w_raw", [128, 3, KC, 128])
                sh.w_hi = fsb("w_hi", [128, 2, 3, KC, 128], F32R)
                sh.w_lo = fsb("w_lo", [128, 2, 3, KC, 128], F32R)
                stage_x(nc, sh)
                stage_conv(nc, sh)
                with ExitStack() as gla:
                    def gsb(name, shape, dt=F32):
                        return gla.enter_context(nc.sbuf_tensor(name, shape, dt))
                    sh.gaT = gsb("gaT", [LR, TOK])
                    sh.wa2 = gsb("wa2", [LR, 256])
                    sh.bga = gsb("bga", [128, 2])
                    sh.gnorm = gsb("gnorm", [128, 4])
                    sh.restart = gsb("restart", [128, TOK], BF16)
                    stage_small(nc, sh)
                    stage_gla(nc, sh)
                sh.qbd = fsb("qbd", [128, 4, DB, H_FOX * DT])
                sh.kTs = fsb("kTs", [128, 4, DB * DT])
                sh.vs = fsb("vs", [DB * DT, BW])
                stage_fox(nc, sh)
                stage_fox_sample(nc, sh)
            if upto < 1:
                return
            sh.m = dense.enter_context(nc.sbuf_tensor("m", [128, KC, TOK], F32))
            stage_gates(nc, sh)
            stage_out(nc, sh)
        if upto < 2:
            return
        clear(nc, used)
        sems.close()
        stage_route(nc, sh)
        stage_moe(nc, sh)
        stage_combine(nc, sh)


_INS = ['x_prompt', 'x_sample', 'cache_fox_k', 'cache_fox_v', 'cache_fox_logf', 'state_gla', 'state_conv',
        'page_table', 'w_in', 'w_gla_a2', 'b_gla_a', 'gla_norm_g', 'b_fox_f', 'conv_w', 'w_branch', 'w_out',
        'ln1_g', 'ln1_b', 'w_router', 'b_router', 'w_e_gate', 'w_e_up', 'w_e_down', 'ln2_g', 'ln2_b']
_OUTS = [('y_prompt', (1, 1024, 1024)), ('y_sample', (8, 8, 1024)),
         ('prompt_fox_k', (1, 1, 1024, 8, 64)), ('prompt_fox_v', (1, 1, 1024, 8, 64)),
         ('prompt_fox_logf', (1, 1, 1024, 8)), ('prompt_gla', (1, 1, 4, 64, 128)), ('prompt_conv', (1, 1, 2, 512)),
         ('sample_fox_k', (1, 8, 8, 8, 64)), ('sample_fox_v', (1, 8, 8, 8, 64)), ('sample_fox_logf', (1, 8, 8, 8)),
         ('sample_gla', (1, 8, 4, 64, 128)), ('sample_conv', (1, 8, 2, 512))]


def kernel(**inputs):
    import numpy as _np
    import concourse.bacc as _bacc
    from concourse import mybir as _mybir
    from concourse.bass_utils import run_bass_kernel_spmd as _run

    nc = _bacc.Bacc("TRN2", target_bir_lowering=False, num_devices=1)
    arrays, ins, outs = {}, {}, {}
    for name in _INS:
        a = _np.ascontiguousarray(inputs[name])
        arrays[f"in_{name}"] = a
        ins[name] = nc.dram_tensor(f"in_{name}", a.shape, _mybir.dt.from_np(a.dtype), kind="ExternalInput").ap()
    for name, shape in _OUTS:
        outs[name] = nc.dram_tensor(f"out_{name}", shape, _mybir.dt.float32, kind="ExternalOutput").ap()
    build(nc, ins, outs)
    r = _run(nc, [arrays], core_ids=[0])
    return tuple(r.results[0][f"out_{name}"] for name, _ in _OUTS)
```

```python
from contextlib import ExitStack

import concourse.bass as bass
import numpy as np
from concourse import mybir

F32 = mybir.dt.float32
F32R = mybir.dt.float32r
I32 = mybir.dt.int32
U32 = mybir.dt.uint32
BF16 = mybir.dt.bfloat16
ALU = mybir.AluOpType
ACT = mybir.ActivationFunctionType
X = mybir.AxisListType.X

D = 1024
KC = D // 128
SEQ = 1024
DB, DT = 8, 8
TOK = SEQ + DB * DT
BW = 512
H_GLA, DK, DV = 4, 64, 128
LR = 16
H_FOX, HD = 8, 64
CHUNK = 64
PAGE = 128
NPAGE = 2
NE, NG, EPG = 16, 4, 4
DE = 256
EPS = 1e-5
ALPHA = 2.0 ** 0.25
NT = 9
GROUPS = [(0, 384), (384, 384), (768, 320)]
GQ, GK, GV, GA, GR = 0, 256, 512, 1024, 1040
FQ, FK, FV, FF = 1552, 2064, 2576, 3088
CB, CC, CH, GATE = 3096, 3608, 4120, 4632
BIG = 1.0e30


class Chain:

    def __init__(self, eng, sem, start=0):
        self.eng, self.sem, self.n = eng, sem, start

    def __call__(self, ins):
        ins.then_inc(self.sem, 1)
        self.n += 1
        self.eng.wait_ge(self.sem, self.n)


def clear(nc, sems):
    nums = sorted(s.num for s in sems)
    first = [n for n in nums if n - 1 not in nums]
    last = [n for n in nums if n + 1 not in nums]
    with nc.Block() as block:
        @block.sync
        def _(eng):
            for a, b in zip(first, last):
                eng.sem_clear(range(a, b + 1))


def f32(ap):
    return ap.bitcast(F32)


SLABS = [[CC + 128 * c, CH + 128 * c, CB + 128 * c] for c in range(4)]
for _p in range(2):
    SLABS += [[GQ + 128 * _p, GK + 128 * _p, GV + 256 * _p],
              [GV + 256 * _p + 128, GR + 256 * _p, GR + 256 * _p + 128]]
SLABS += [[FQ + 128 * p, FK + 128 * p, FV + 128 * p] for p in range(4)]
CONV0, GLA0, FOX0 = 0, 4, 8
N_SLAB = len(SLABS)


class Shared:
    pass


SLAB = 3 * KC * 128


def weight_views(sh, blocks, chunks):
    two = [part[:, :].rearrange("p (r b k n) -> p r b k n", r=2, b=blocks, k=chunks) for part in (sh.slab_hi, sh.slab_lo)]
    return sh.slab_raw[:, :].rearrange("p (b k n) -> p b k n", b=blocks, k=chunks), two[0], two[1]


def load_slab(sh, eng, n):
    if n >= N_SLAB:
        return
    if n >= 1:
        eng.wait_ge(sh.w_split, n)
    for b in range(3):
        src = sh.w_in[0, :, SLABS[n][b]:SLABS[n][b] + 128].rearrange("(k p) n -> p k n", p=128)
        eng.dma_start(sh.w_raw[:, b], src).then_inc(sh.w_loaded, 16)


def head_slab(sh, eng, n):
    if n >= N_SLAB:
        return
    eng.wait_ge(sh.w_loaded, 48 * (n + 1))
    if n >= 2:
        eng.wait_ge(sh.fm_ready, 9 * (n - 1))
    eng.activation(sh.w_hi[:, n % 2], sh.w_raw[:], ACT.Copy).then_inc(sh.w_head, 1)


def tail_slab(sh, eng, n):
    if n >= N_SLAB:
        return
    eng.wait_ge(sh.w_head, n + 1)
    eng.tensor_tensor(sh.w_lo[:, n % 2], sh.w_raw[:], f32(sh.w_hi[:, n % 2]),
                      ALU.subtract).then_inc(sh.w_split, 1)


def project_slab(sh, eng, n, first=0, last_unit=9):
    eng.wait_ge(sh.w_split, n + 1)
    for b in range(3):
        for g, (t0, tn) in enumerate(GROUPS):
            if not first <= 3 * b + g < last_unit:
                continue
            u = 9 * n + 3 * b + g
            if u >= 2:
                eng.wait_ge(sh.fm_free[u % 2], u // 2)
            out = sh.ps[:, u % 2, 0:tn]
            for k in range(KC):
                for j, (w, x) in enumerate(((sh.w_hi, sh.xh), (sh.w_hi, sh.xl), (sh.w_lo, sh.xh))):
                    last = eng.matmul(out, w[:, n % 2, b, k, :], x[:, k, t0:t0 + tn],
                                      start=(k == 0 and j == 0), stop=(k == KC - 1 and j == 2))
            last.then_inc(sh.fm_ready, 1)


def fm_unit(sh, n, b, g):
    u = 9 * n + 3 * b + g
    t0, tn = GROUPS[g]
    return sh.ps[:, u % 2, 0:tn], u + 1, sh.fm_free[u % 2], t0, tn


def stage_x(nc, sh):
    with ExitStack() as ctx:
        x_tm = ctx.enter_context(nc.sbuf_tensor("x_tm", [128, 3, D], F32))
        x_loaded = [sh.front_sem(f"x_loaded{i}") for i in range(3)]
        x_tr = sh.front_sem("x_transposed")
        x_head = sh.front_sem("x_head")
        x_tail = sh.front_sem("x_tail")
        const = sh.front_sem("x_const")
        block = ctx.enter_context(nc.Block())

        @block.sync
        def _(eng):
            for t in range(NT):
                if t >= 3:
                    eng.wait_ge(x_tr, 2 * (t - 2))
                n = 128 if t < 8 else 64
                src = sh.x_prompt[0, 128 * t:128 * t + 128, :] if t < 8 else \
                    sh.x_sample.rearrange("b t d -> (b t) d")
                eng.dma_start(x_tm[0:n, t % 3, :], src).then_inc(x_loaded[t % 3], 16)
                if t == 2:
                    load_slab(sh, eng, 0)
            load_slab(sh, eng, 1)

        @block.gpsimd
        def _(eng):
            ch = Chain(eng, const)
            ch(eng.memset(sh.ident[:, :], 0.0))
            ch(eng.affine_select(out=sh.ident[:, :], in_=sh.ident[:, :], compare_op=ALU.not_equal,
                                 fill=1.0, base=0, pattern=[[-1, 128]], channel_multiplier=1))

        @block.tensor
        def _(eng):
            eng.wait_ge(const, 2)
            for t in range(NT):
                n = 128 if t < 8 else 64
                eng.wait_ge(x_loaded[t % 3], 16 * (t // 3 + 1))
                for half in range(2):
                    u = 2 * t + half
                    if u >= 4:
                        eng.wait_ge(x_tail, u - 3)
                    for k in range(4):
                        last = eng.transpose(sh.ps[:, u % 4, 128 * k:128 * k + n],
                                             x_tm[0:n, t % 3, 128 * (4 * half + k):128 * (4 * half + k) + 128],
                                             sh.ident[0:n, 0:n])
                    last.then_inc(x_tr, 1)

        def unit(u):
            t, half = divmod(u, 2)
            n = 128 if t < 8 else 64
            bank = sh.ps[:, u % 4, :].rearrange("p (k n) -> p k n", k=4)[:, :, 0:n]
            return bank, (slice(None), slice(4 * half, 4 * half + 4), slice(128 * t, 128 * t + n))

        @block.scalar
        def _(eng):
            for u in range(2 * NT):
                eng.wait_ge(x_tr, u + 1)
                bank, at = unit(u)
                eng.activation(sh.xh[at], bank, ACT.Copy).then_inc(x_head, 1)
                if u == 9:
                    head_slab(sh, eng, 0)

        @block.vector
        def _(eng):
            for u in range(2 * NT):
                eng.wait_ge(x_head, u + 1)
                bank, at = unit(u)
                eng.tensor_tensor(sh.xl[at], bank, f32(sh.xh[at]), ALU.subtract).then_inc(x_tail, 1)
                if u == 9:
                    tail_slab(sh, eng, 0)


def store_branch(sh, eng, j, rows, cols, hi, lo, sem):
    eng.dma_start(sh.oT_hi[j, rows, cols], f32(hi)).then_inc(sem, 16)
    eng.dma_start(sh.oT_lo[j, rows, cols], f32(lo)).then_inc(sem, 16)


def wait_freed(sh, eng, n, b, g):
    u = 9 * n + 3 * b + g
    eng.wait_ge(sh.fm_free[u % 2], u // 2 + 1)


def wait_block_freed(sh, eng, n, b):
    for g in (1, 2):
        wait_freed(sh, eng, n, b, g)


def small_projections(nc, sh, ctx):
    def sb(name, shape, dt=F32):
        return ctx.enter_context(nc.sbuf_tensor("sm_" + name, shape, dt))

    def sem(name):
        return sh.front_sem("sm_" + name)
    w = sb("w", [128, KC, 128])
    wh, wl = sb("wh", [128, KC, 128], F32R), sb("wl", [128, KC, 128], F32R)
    bf = sb("bf", [H_FOX, 1])
    z, a, logf = (sb(n, [H_FOX, TOK]) for n in ("z", "a", "logf"))
    c, nc_ = z, a
    restart = sb("restart", [H_FOX, TOK], BF16)
    lf_tm = sb("lf_tm", [128, NT, H_FOX])
    zero, loaded, head, tail, ready = (sem(n) for n in ("zero", "loaded", "head", "tail", "ready"))
    act_s, dve_s, lf_ready, lf_tr, stored, c_ready, pool_s, lf_out = (
        sem(n) for n in ("act", "dve", "lf_ready", "lf_tr", "stored", "c_ready", "pool", "lf_out"))

    class Parts:
        def clear_masks(eng):
            eng.memset(w[:, :, :], 0.0).then_inc(zero, 1)
            ch = Chain(eng, pool_s)
            ch(eng.memset(sh.restart[:, :], 1.0))
            ch(eng.memset(sh.restart[:, 0:SEQ:CHUNK], 0.0))
            ch(eng.memset(sh.restart[:, SEQ:TOK:DT], 0.0))
            ch(eng.memset(restart[:, :], 1.0))
            ch(eng.memset(restart[:, SEQ:TOK:DT], 0.0))

        def load(eng):
            eng.wait_ge(zero, 1)
            for col, at, n in ((FF, 0, H_FOX), (GA, 32, LR)):
                eng.dma_start(w[:, :, at:at + n], sh.w_in[0, :, col:col + n].rearrange("(k p) n -> p k n", p=128)
                              ).then_inc(loaded, 16)
            eng.dma_start(bf[:, :], sh.b_fox_f.rearrange("a h -> h a"), allow_slow_non_contiguous=True).then_inc(loaded, 16)
            eng.dma_start(sh.wa2[:, :], sh.w_gla_a2[0]).then_inc(loaded, 16)
            eng.dma_start(sh.bga[:, :], sh.b_gla_a[0].rearrange("(c p) -> p c", p=128), allow_slow_non_contiguous=True).then_inc(loaded, 16)
            eng.dma_start(sh.gnorm[:, :], sh.gla_norm_g[0].rearrange("(c p) -> p c", p=128), allow_slow_non_contiguous=True).then_inc(loaded, 16)

        def store(eng):
            eng.wait_ge(c_ready, 2)
            eng.dma_start(sh.c_dram[0], c[:, :]).then_inc(stored, 16)
            eng.dma_start(sh.c_dram[1], nc_[:, :]).then_inc(stored, 16)
            eng.wait_ge(lf_out, 1)
            eng.dma_start(sh.prompt_fox_logf[0, 0].rearrange("(t p) h -> p t h", p=128), lf_tm[:, 0:8, :]).then_inc(stored, 16)
            eng.dma_start(sh.sample_fox_logf[0].rearrange("b t h -> (b t) h"), lf_tm[0:64, 8, :]).then_inc(stored, 16)
            eng.wait_ge(stored, 64)

        def project(eng):
            eng.wait_ge(tail, 1)
            for g, (t0, tn) in enumerate(GROUPS):
                for k in range(KC):
                    for j, (ww, x) in enumerate(((wh, sh.xh), (wh, sh.xl), (wl, sh.xh))):
                        last = eng.matmul(sh.ps[:, 2 + g, 0:tn], ww[:, k, :], x[:, k, t0:t0 + tn],
                                          start=(k == 0 and j == 0), stop=(k == KC - 1 and j == 2))
                last.then_inc(ready, 1)

        def transpose_logf(eng):
            eng.wait_ge(lf_ready, 1)
            for t in range(NT):
                n = 128 if t < 8 else 64
                last = eng.transpose(sh.ps[0:n, 5, 8 * t:8 * t + 8], logf[:, 128 * t:128 * t + n],
                                     sh.ident[0:8, 0:8])
            last.then_inc(lf_tr, 1)

        def w_heads(eng):
            eng.wait_ge(loaded, 96)
            eng.activation(wh[:, :, :], w[:, :, :], ACT.Copy).then_inc(head, 1)

        def place(eng):
            for g, (t0, tn) in enumerate(GROUPS):
                eng.wait_ge(ready, g + 1)
                eng.activation(sh.gaT[:, t0:t0 + tn], sh.ps[32:48, 2 + g, 0:tn], ACT.Copy)
                eng.activation(z[:, t0:t0 + tn], sh.ps[0:8, 2 + g, 0:tn], ACT.Identity, bias=bf[:, :]).then_inc(act_s, 1)

        def softplus(eng):
            eng.wait_ge(act_s, 3)
            ch = Chain(eng, act_s, 3)
            ch(eng.activation(a[:, :], z[:, :], ACT.Abs))
            ch(eng.activation(a[:, :], a[:, :], ACT.Exp, scale=-1.0))
            ch(eng.activation(a[:, :], a[:, :], ACT.Ln, bias=1.0))

        def w_tails(eng):
            eng.wait_ge(head, 1)
            eng.tensor_tensor(wl[:, :, :], w[:, :, :], f32(wh[:, :, :]), ALU.subtract).then_inc(tail, 1)

        def running_sums(eng):
            eng.wait_ge(act_s, 6)
            eng.scalar_tensor_tensor(out=logf[:, :], in0=z[:, :], scalar=0.0, in1=a[:, :],
                                     op0=ALU.min, op1=ALU.subtract).then_inc(lf_ready, 1)
            eng.wait_ge(lf_ready, 1)
            eng.wait_ge(pool_s, 5)
            eng.tensor_tensor_scan(c[:, :], restart[:, :], logf[:, :], 0.0, ALU.mult, ALU.add).then_inc(c_ready, 1)
            eng.wait_ge(c_ready, 1)
            eng.tensor_scalar(nc_[:, :], c[:, :], -1.0, None, ALU.mult).then_inc(c_ready, 1)

        def place_logf(eng):
            eng.wait_ge(lf_tr, 1)
            ch = Chain(eng, dve_s)
            ch(eng.tensor_copy(lf_tm[:, 0:8, :], sh.ps[:, 5, 0:64].rearrange("p (t h) -> p t h", h=8)))
            eng.tensor_copy(lf_tm[0:64, 8, :], sh.ps[0:64, 5, 64:72]).then_inc(lf_out, 1)
    return Parts


def stage_conv(nc, sh):
    U = SEQ + 2 + DB * (DT + 2)
    NS = 2 + 2 * DB
    with ExitStack() as ctx:
        def sb(name, shape, dt=F32):
            return ctx.enter_context(nc.sbuf_tensor("cv_" + name, shape, dt))

        def sem(name):
            return sh.front_sem("cv_" + name)
        rows = sb("rows", [19, BW])
        cols = sb("cols", [128, 4, 19])
        c_sb = sb("c", [128, TOK])
        u = sb("u", [128, U])
        y, b_sb = sb("y", [128, TOK]), sb("b", [128, TOK])
        o = sb("o", [128, TOK])
        o_hi = sb("o_hi", [128, 2, TOK], F32R)
        o_lo = sb("o_lo", [128, 2, TOK], F32R)
        st = sb("st", [128, 2, NS])
        st_tm = sb("st_tm", [NS, BW])
        loaded, rows_tr, oh_ready, ol_ready = sem("loaded"), sem("rows_tr"), sem("oh_ready"), sem("ol_ready")
        stored, st_ready, st_tr, st_out = sem("stored"), sem("st_ready"), sem("st_tr"), sem("st_out")
        dve_step, u_zero, o_whole = sem("dve_step"), sem("u_zero"), sem("o_whole")
        u_s = u[:, SEQ + 2:U].rearrange("p (b s) -> p b s", b=DB)
        y_s = y[:, SEQ:TOK].rearrange("p (b s) -> p b s", b=DB)
        small = small_projections(nc, sh, ctx)
        block = ctx.enter_context(nc.Block())

        @block.sync
        def _(eng):
            eng.dma_start(rows[0:16, :], sh.state_conv[0].rearrange("b j c -> (b j) c")).then_inc(loaded, 16)
            eng.dma_start(rows[16:19, :], sh.conv_w[0]).then_inc(loaded, 16)
            small.load(eng)
            for c in range(4):
                load_slab(sh, eng, CONV0 + c + 2)
                eng.wait_ge(ol_ready, c + 1)
                store_branch(sh, eng, 2, slice(128 * c, 128 * c + 128), slice(0, TOK),
                             o_hi[:, c % 2, :], o_lo[:, c % 2, :], stored)
            eng.wait_ge(st_out, 4)
            eng.dma_start(sh.prompt_conv[0, 0], st_tm[0:2, :]).then_inc(stored, 16)
            eng.dma_start(sh.sample_conv[0].rearrange("b j c -> (b j) c"), st_tm[2:NS, :]).then_inc(stored, 16)
            small.store(eng)
            eng.wait_ge(stored, 16 * 10)

        @block.gpsimd
        def _(eng):
            eng.memset(u[:, 0:2], 0.0).then_inc(u_zero, 1)
            small.clear_masks(eng)

        @block.tensor
        def _(eng):
            eng.wait_ge(loaded, 32)
            for c in range(4):
                last = eng.transpose(sh.ps[:, 7, 32 * c:32 * c + 19], rows[:, 128 * c:128 * c + 128],
                                     sh.ident[0:19, 0:19])
            last.then_inc(rows_tr, 1)

            def state(c):
                eng.wait_ge(st_ready, c + 1)
                if c >= 1:
                    eng.wait_ge(st_out, c)
                eng.transpose(sh.ps[0:NS, 6, 0:128], st[:, c % 2, :], sh.ident[:, :]).then_inc(st_tr, 1)

            for c in range(4):
                project_slab(sh, eng, CONV0 + c)
                if c >= 1:
                    state(c - 1)
                if c == 1:
                    small.project(eng)
            project_slab(sh, eng, GLA0, 0, 2)
            small.transpose_logf(eng)
            state(3)

        @block.scalar
        def _(eng):
            def state(c):
                eng.wait_ge(st_tr, c + 1)
                eng.activation(st_tm[:, 128 * c:128 * c + 128], sh.ps[0:NS, 6, 0:128], ACT.Copy).then_inc(st_out, 1)

            for c in range(4):
                head_slab(sh, eng, CONV0 + c + 1)
                if c == 2:
                    small.place(eng)
                for g in range(3):
                    bank, n, free, t0, tn = fm_unit(sh, CONV0 + c, 0, g)
                    eng.wait_ge(sh.fm_ready, n)
                    eng.activation(c_sb[:, t0:t0 + tn], bank, ACT.Copy).then_inc(free, 1)
                if c == 2:
                    small.softplus(eng)
                for g in range(3):
                    bank, n, free, t0, tn = fm_unit(sh, CONV0 + c, 2, g)
                    eng.wait_ge(sh.fm_ready, n)
                    if c >= 1 and g == 0:
                        eng.wait_ge(o_whole, c)
                    eng.activation(b_sb[:, t0:t0 + tn], bank, ACT.Copy).then_inc(free, 1)
                eng.wait_ge(o_whole, c + 1)
                if c >= 2:
                    eng.wait_ge(stored, 32 * (c - 1))
                eng.activation(o_hi[:, c % 2, :], o[:, :], ACT.Copy).then_inc(oh_ready, 1)
                if c >= 1:
                    state(c - 1)
                if c == 0:
                    small.w_heads(eng)
            state(3)

        @block.vector
        def _(eng):
            ch = Chain(eng, dve_step)
            eng.wait_ge(rows_tr, 1)
            ch(eng.tensor_copy(cols[:, :, :], sh.ps[:, 7, 0:128].rearrange("p (c n) -> p c n", c=4)[:, :, 0:19]))
            eng.wait_ge(u_zero, 1)
            for c in range(4):
                tail_slab(sh, eng, CONV0 + c + 1)
                ch(eng.tensor_copy(u_s[:, :, 0:2], cols[:, c, 0:16].rearrange("p (b j) -> p b j", b=DB)))
                for g in range(3):
                    bank, n, free, t0, tn = fm_unit(sh, CONV0 + c, 1, g)
                    wait_freed(sh, eng, CONV0 + c, 0, g)
                    eng.wait_ge(sh.fm_ready, n)
                    pn = min(tn, SEQ - t0)
                    if pn < tn:
                        ch(eng.tensor_tensor(u_s[:, :, 2:], bank[:, pn:tn].rearrange("p (b t) -> p b t", b=DB),
                                             c_sb[:, SEQ:TOK].rearrange("p (b t) -> p b t", b=DB), ALU.mult))
                    eng.tensor_tensor(u[:, 2 + t0:2 + t0 + pn], bank[:, 0:pn], c_sb[:, t0:t0 + pn],
                                      ALU.mult).then_inc(free, 1)
                wait_block_freed(sh, eng, CONV0 + c, 1)
                tap = [cols[:, c, 16 + j:17 + j] for j in range(3)]
                eng.tensor_scalar(y[:, 0:SEQ], u[:, 0:SEQ], tap[0], None, ALU.mult)
                ch(eng.tensor_scalar(y_s, u_s[:, :, 0:DT], tap[0], None, ALU.mult))
                for j in (1, 2):
                    eng.scalar_tensor_tensor(out=y[:, 0:SEQ], in0=u[:, j:j + SEQ], scalar=tap[j], in1=y[:, 0:SEQ],
                                             op0=ALU.mult, op1=ALU.add)
                    ch(eng.scalar_tensor_tensor(out=y_s, in0=u_s[:, :, j:j + DT], scalar=tap[j], in1=y_s,
                                                op0=ALU.mult, op1=ALU.add))
                if c >= 2:
                    eng.wait_ge(st_tr, c - 1)
                ch(eng.tensor_copy(st[:, c % 2, 0:2], u[:, SEQ:SEQ + 2]))
                eng.tensor_copy(st[:, c % 2, 2:NS].rearrange("p (b j) -> p b j", b=DB),
                                u_s[:, :, DT:DT + 2]).then_inc(st_ready, 1)
                wait_block_freed(sh, eng, CONV0 + c, 2)
                if c >= 1:
                    eng.wait_ge(oh_ready, c)
                eng.tensor_tensor(o[:, :], b_sb[:, :], y[:, :], ALU.mult).then_inc(o_whole, 1)
                eng.wait_ge(o_whole, c + 1)
                eng.wait_ge(oh_ready, c + 1)
                eng.tensor_tensor(o_lo[:, c % 2, :], o[:, :], f32(o_hi[:, c % 2, :]),
                                  ALU.subtract).then_inc(ol_ready, 1)
                if c == 0:
                    small.w_tails(eng)
                if c == 2:
                    small.running_sums(eng)
            small.place_logf(eng)


def stage_gla(nc, sh):
    NCH = SEQ // CHUNK
    with ExitStack() as ctx:
        def sb(name, shape, dt=F32):
            return ctx.enter_context(nc.sbuf_tensor("gl_" + name, shape, dt))

        def sem(name):
            return sh.front_sem("gl_" + name)
        q = sb("q", [128, TOK])
        k = sb("k", [128, TOK])
        kz = sb("kz", [128, 2, TOK])
        T = sb("T", [128, 3, TOK])
        v = sb("v", [128, NT, 2 * DV])
        rs = sb("rs", [128, 2, TOK])
        kez = sb("kez", [128, 2, 2, 128])
        att = sb("att", [128, 2, 2, 128])
        att_s = sb("att_s", [64, 2, 64])
        mask, mask_s = sb("mask", [128, 2, 128], I32), sb("mask_s", [64, 2, 64], I32)
        S = sb("S", [128, 4, 2 * DV])
        S0 = sb("S0", [128, DB, 2 * DV])
        qz = sb("qz", [128, 9 * 64])
        decay = sb("decay", [128, NCH + DB])
        row_b = sb("row_b", [64, DB])
        ss, rstd = sb("ss", [128, 2 * NT]), sb("rstd", [128, 2 * NT])
        kez_s = k[0:64, 0:DB * 128].rearrange("p (b n) -> p b n", b=DB)
        (pool_s, act_s, dve_s, la_mm, la_free, e1, e2, e3, kend_ready, tr, tr_free, state_in,
         att_mm, att_ready, ds_mm, s_ready, o_mm, o_out, r_sig, ss_ready, sq_ready, on_ready, oT_tr, oT_ready, oh_ready,
         ol_ready, stored, kes_ready, dss_mm, s0_new, kz_ready, k_in, qin_ready, vk_ready, sq_in, z_ready, b_ready) = (
             sem(n) for n in (
             "pool", "act", "dve", "la_mm", "la_free", "e1", "e2", "e3", "kend_ready", "tr",
             "tr_free", "state_in", "att_mm", "att_ready", "ds_mm", "s_ready", "o_mm", "o_out", "r_sig", "ss_ready",
             "sq_ready", "on_ready", "oT_tr", "oT_ready", "oh_ready", "ol_ready", "stored", "kes_ready", "dss_mm",
             "s0_new", "kz_ready", "k_in", "qin_ready", "vk_ready", "sq_in", "z_ready", "b_ready"))
        block = ctx.enter_context(nc.Block())
        NOT = 6

        @block.gpsimd
        def _(eng):
            ch = Chain(eng, pool_s)
            for m, n in ((mask, 128), (mask_s, 64)):
                f = T[0:n, 0, 0:2 * n].rearrange("p (h t) -> p h t", h=2)
                ch(eng.memset(f, 1.0))
                ch(eng.affine_select(out=f, in_=f, compare_op=ALU.is_ge, fill=0.0, base=0,
                                     pattern=[[0, 2], [1, n]], channel_multiplier=-1))
                if n == 128:
                    g = f[:, :, 64:128]
                    ch(eng.affine_select(out=g, in_=g, compare_op=ALU.is_ge, fill=0.0, base=-64,
                                         pattern=[[0, 2], [0, 64]], channel_multiplier=1))
                else:
                    g = f.rearrange("p h (b t) -> p h b t", b=DB)
                    ch(eng.affine_select(out=g, in_=g, compare_op=ALU.is_ge, fill=0.0, base=0,
                                         pattern=[[0, 2], [-DT, DB], [0, DT]], channel_multiplier=1))
                ch(eng.tensor_copy(m[:, :, :], f))
            ch(eng.memset(row_b[:, :], 1.0))
            ch(eng.affine_select(out=row_b[:, :], in_=row_b[:, :], compare_op=ALU.is_ge, fill=0.0, base=0,
                                 pattern=[[-DT, DB]], channel_multiplier=1))
            ch(eng.affine_select(out=row_b[:, :], in_=row_b[:, :], compare_op=ALU.is_ge, fill=0.0, base=DT - 1,
                                 pattern=[[DT, DB]], channel_multiplier=-1))
            for buf in (kz[:, :, :], att[:, :, :, :], att_s[:, :, :], kez[:, :, :, :], S0[:, :, :], qz[:, :],
                        v[64:128, NT - 1, :]):
                ch(eng.memset(buf, 0.0))
        POOL_DONE = 8 + 3 + 7

        @block.sync
        def _(eng):
            for p in range(2):
                if p == 0:
                    eng.wait_ge(pool_s, POOL_DONE)
                else:
                    eng.wait_ge(stored, 16 * 4)
                for h in range(2):
                    eng.dma_start(S0[64 * h:64 * h + 64, :, 128 * h:128 * h + 128],
                                  sh.state_gla[0, :, 2 * p + h].rearrange("b k v -> k b v")).then_inc(state_in, 16)
                load_slab(sh, eng, GLA0 + 2 * p + 2)
                load_slab(sh, eng, GLA0 + 2 * p + 3)
                eng.wait_ge(s_ready, (NCH + 1) * (p + 1))
                for h in range(2):
                    eng.dma_start(sh.prompt_gla[0, 0, 2 * p + h],
                                  S[64 * h:64 * h + 64, NCH % 4, 128 * h:128 * h + 128]).then_inc(stored, 16)
                eng.wait_ge(s0_new, 4 * (p + 1))
                for h in range(2):
                    eng.dma_start(sh.sample_gla[0, :, 2 * p + h].rearrange("b k v -> k b v"),
                                  S0[64 * h:64 * h + 64, :, 128 * h:128 * h + 128]).then_inc(stored, 16)
                for h in range(2):
                    eng.wait_ge(ol_ready, 2 * p + h + 1)
                    r0 = 128 * (2 * p + h)
                    store_branch(sh, eng, 0, slice(r0, r0 + 128), slice(0, TOK), T[:, 1, :], T[:, 2, :], stored)
                    eng.wait_ge(stored, 128 * p + 64 + 32 * (h + 1))

        def transpose_tile(eng, p, t):
            n = 128 if t < 8 else 64
            if t >= 2:
                eng.wait_ge(tr_free, NT * p + t - 1)
            for j, src in enumerate((T[:, 1, :], T[:, 2, :], k[:, :])):
                last = eng.transpose(sh.ps[0:n, 2 + t % 2, 128 * j:128 * j + 128],
                                     src[:, 128 * t:128 * t + n], sh.ident[:, :])
            last.then_inc(tr, 1)

        def place_tile(eng, p, t):
            n = 128 if t < 8 else 64
            eng.wait_ge(tr, NT * p + t + 1)
            bank = sh.ps[0:n, 2 + t % 2, :]
            if t < 8:
                if t >= 2:
                    eng.wait_ge(ds_mm, 8 * p + t - 1)
                eng.tensor_copy(kez[0:64, t % 2, 0, :], bank[0:64, 256:384])
                eng.tensor_copy(kez[64:128, t % 2, 1, :], bank[64:128, 256:384])
            else:
                for b in range(DB):
                    last = eng.tensor_scalar(kez_s[:, b, :], bank[:, 256:384], row_b[:, b:b + 1], None, ALU.mult)
                last.then_inc(kes_ready, 1)
            eng.tensor_copy(v[0:n, t, :], bank[:, 0:256]).then_inc(tr_free, 1)

        @block.tensor
        def _(eng):
            for p in range(2):
                if p == 1:
                    eng.wait_ge(oT_ready, NOT)
                for g, (t0, tn) in enumerate(GROUPS):
                    eng.matmul(sh.ps[:, 2 + g, 0:tn], sh.wa2[:, 128 * p:128 * p + 128], sh.gaT[:, t0:t0 + tn],
                               start=True, stop=True).then_inc(la_mm, 1)
                project_slab(sh, eng, GLA0 + 2 * p, 2)
                project_slab(sh, eng, GLA0 + 2 * p + 1)
                eng.wait_ge(la_free, 3 * (p + 1))
                wait_block_freed(sh, eng, GLA0 + 2 * p, 2)
                wait_block_freed(sh, eng, GLA0 + 2 * p + 1, 0)
                eng.wait_ge(kend_ready, p + 1)
                transpose_tile(eng, p, 0)
                eng.wait_ge(qin_ready, p + 1)
                eng.wait_ge(kz_ready, p + 1)
                eng.wait_ge(state_in, 32 * (p + 1))
                for t in range(NT):
                    if t < 8:
                        transpose_tile(eng, p, t + 1)
                    eng.wait_ge(tr_free, NT * p + t + 1)
                    n = 128 if t < 8 else 64
                    i = NT * p + t
                    tok = slice(128 * t, 128 * t + n)
                    if i >= 1:
                        eng.wait_ge(att_ready, i)
                    for h in range(2):
                        last = eng.matmul(sh.ps[0:n, 4, 128 * h:128 * h + n], kz[:, h, tok], q[:, tok],
                                          start=(h == 0), stop=(h == 1), skip_group_check=True)
                    last.then_inc(att_mm, 1)
                    if t < 8:
                        if t >= 1:
                            eng.wait_ge(s_ready, (NCH + 1) * p + 2 * t + 1)
                        elif p == 1:
                            eng.wait_ge(s0_new, 4)
                        for c in range(2):
                            last = eng.matmul(sh.ps[:, 7, 256 * c:256 * c + 256], kez[:, t % 2, c, :], v[:, t, :],
                                              start=True, stop=True, skip_group_check=True)
                        last.then_inc(ds_mm, 1)
                    out = sh.ps[0:n, 5 + t % 2, 0:256]
                    if i >= 2:
                        eng.wait_ge(o_out, i - 1)
                    eng.wait_ge(att_ready, i + 1)
                    for h in range(2):
                        a = att[:, t % 2, h, :] if t < 8 else att_s[:, h, :]
                        eng.matmul(out[:, 128 * h:128 * h + 128], a, v[0:n, t, 128 * h:128 * h + 128],
                                   start=(h == 0), stop=False, skip_group_check=True)
                    if t < 8:
                        for c in range(2):
                            eng.wait_ge(s_ready, (NCH + 1) * p + 2 * t + c + 1)
                            last = eng.matmul(out[64 * c:64 * c + 64, :],
                                              q[:, 128 * t + 64 * c:128 * t + 64 * c + 64],
                                              S[:, (2 * t + c) % 4, :], start=False, stop=True, skip_group_check=True)
                    else:
                        for b in range(DB):
                            last = eng.matmul(out, qz[:, 64 * b:64 * b + 64], S0[:, b, :],
                                              start=False, stop=(b == DB - 1), skip_group_check=True)
                    last.then_inc(o_mm, 1)
                eng.wait_ge(kes_ready, p + 1)
                for b2 in range(4):
                    if b2 == 0:
                        eng.wait_ge(s_ready, (NCH + 1) * (p + 1))
                    else:
                        eng.wait_ge(s0_new, 4 * p + b2)
                    for e in range(2):
                        last = eng.matmul(sh.ps[:, 7, 256 * e:256 * e + 256], kez_s[:, 2 * b2 + e, :],
                                          v[0:64, NT - 1, :], start=True, stop=True, skip_group_check=True)
                    last.then_inc(dss_mm, 1)
                project_slab(sh, eng, GLA0 + 2 * p + 2, 0, 2)
                eng.wait_ge(on_ready, p + 1)
                for h in range(2):
                    for w in range(3):
                        i = NOT * p + 3 * h + w
                        if i % NOT >= 2:
                            eng.wait_ge(oT_ready, i - 1)
                        for t in range(4 * w, min(4 * w + 4, NT)):
                            n = 128 if t < 8 else 64
                            last = eng.transpose(sh.ps[:, 2 + i % 2, 128 * (t % 4):128 * (t % 4) + n],
                                                 v[0:n, t, 128 * h:128 * h + 128], sh.ident[0:n, 0:n])
                        last.then_inc(oT_tr, 1)

        @block.scalar
        def _(eng):
            ch = Chain(eng, act_s)
            for p in range(2):
                s0, s1 = GLA0 + 2 * p, GLA0 + 2 * p + 1
                head_slab(sh, eng, s1)
                if p == 0:
                    eng.wait_ge(pool_s, 8)
                else:
                    eng.wait_ge(stored, 128)
                for g, (t0, tn) in enumerate(GROUPS):
                    eng.wait_ge(la_mm, 3 * p + g + 1)
                    eng.activation(T[:, 0, t0:t0 + tn], sh.ps[:, 2 + g, 0:tn], ACT.Identity,
                                   bias=sh.bga[:, p:p + 1]).then_inc(la_free, 1)
                eng.wait_ge(la_free, 3 * (p + 1))
                ch(eng.activation(T[:, 1, :], T[:, 0, :], ACT.Abs))
                ch(eng.activation(T[:, 1, :], T[:, 1, :], ACT.Exp, scale=-1.0))
                eng.activation(T[:, 1, :], T[:, 1, :], ACT.Ln, bias=1.0).then_inc(z_ready, 1)
                for g in range(3):
                    bank, n, free, t0, tn = fm_unit(sh, s0, 0, g)
                    eng.wait_ge(sh.fm_ready, n)
                    eng.activation(q[:, t0:t0 + tn], bank, ACT.Copy, scale=DK ** -0.5).then_inc(free, 1)
                eng.wait_ge(b_ready, p + 1)
                eng.activation(T[:, 1, :], T[:, 0, :], ACT.Exp).then_inc(e1, 1)
                eng.activation(T[:, 2, :], T[:, 0, :], ACT.Exp, scale=-1.0).then_inc(e2, 1)
                for g in range(3):
                    bank, n, free, t0, tn = fm_unit(sh, s0, 1, g)
                    eng.wait_ge(sh.fm_ready, n)
                    eng.activation(k[:, t0:t0 + tn], bank, ACT.Copy).then_inc(free, 1)
                eng.wait_ge(e3, p + 1)
                ch(eng.activation(T[:, 0, :], T[:, 0, :], ACT.Exp, scale=-1.0))
                eng.wait_ge(kz_ready, p + 1)
                eng.wait_ge(qin_ready, p + 1)
                for n0, b, dst in ((s0, 2, 1), (s1, 0, 2)):
                    for g in range(3):
                        bank, n, free, t0, tn = fm_unit(sh, n0, b, g)
                        eng.wait_ge(sh.fm_ready, n)
                        eng.activation(T[:, dst, t0:t0 + tn], bank, ACT.Copy).then_inc(free, 1)
                    if b == 2:
                        head_slab(sh, eng, s1 + 1)
                eng.wait_ge(kend_ready, p + 1)
                for b in (1, 2):
                    for g in range(3):
                        bank, n, free, t0, tn = fm_unit(sh, s1, b, g)
                        eng.wait_ge(sh.fm_ready, n)
                        if b == 2:
                            wait_freed(sh, eng, s1, 1, g)
                        eng.activation(T[:, 0, t0:t0 + tn], bank, ACT.Sigmoid).then_inc(r_sig, 1)
                for t in range(NT):
                    n = 128 if t < 8 else 64
                    eng.wait_ge(o_mm, NT * p + t + 1)
                    if t == NT - 1:
                        eng.wait_ge(dss_mm, 4 * (p + 1))
                    eng.activation(v[0:n, t, :], sh.ps[0:n, 5 + t % 2, 0:256], ACT.Copy).then_inc(o_out, 1)
                eng.wait_ge(ss_ready, p + 1)
                eng.activation(ss[:, :], ss[:, :], ACT.Sqrt).then_inc(sq_ready, 1)
                for h in range(2):
                    eng.wait_ge(oT_ready, NOT * p + 3 * h + 3)
                    if h == 1:
                        eng.wait_ge(stored, 128 * p + 64 + 32)
                    eng.activation(T[:, 1, :].bitcast(F32R), T[:, 0, :], ACT.Copy).then_inc(oh_ready, 1)

        @block.vector
        def _(eng):
            ch = Chain(eng, dve_s)
            for p in range(2):
                s0, s1 = GLA0 + 2 * p, GLA0 + 2 * p + 1
                tail_slab(sh, eng, s1)
                eng.wait_ge(z_ready, p + 1)
                ch(eng.scalar_tensor_tensor(out=T[:, 2, :], in0=T[:, 0, :], scalar=0.0, in1=T[:, 1, :],
                                            op0=ALU.min, op1=ALU.subtract))
                ch(eng.tensor_scalar(T[:, 2, :], T[:, 2, :], 1.0 / 16.0, None, ALU.mult))
                eng.tensor_tensor_scan(T[:, 0, :], sh.restart[:, :], T[:, 2, :], 0.0, ALU.mult,
                                       ALU.add).then_inc(b_ready, 1)
                if p == 0:
                    eng.wait_ge(pool_s, POOL_DONE)
                eng.wait_ge(e1, p + 1)
                wait_block_freed(sh, eng, s0, 0)
                ch(eng.tensor_copy(decay[:, 0:NCH], T[:, 1, CHUNK - 1:SEQ:CHUNK]))
                ch(eng.tensor_copy(decay[:, NCH:], T[:, 1, SEQ + DT - 1:TOK:DT]))
                eng.tensor_tensor(q[:, :], q[:, :], T[:, 1, :], ALU.mult).then_inc(qin_ready, 1)
                eng.wait_ge(qin_ready, p + 1)
                ch(eng.tensor_copy(qz[:, :].rearrange("p (b s) -> p b s", s=72)[:, :, 0:DT],
                                   q[:, SEQ:TOK].rearrange("p (b t) -> p b t", b=DB)))
                eng.wait_ge(e2, p + 1)
                wait_block_freed(sh, eng, s0, 1)
                ch(eng.tensor_tensor(kz[0:64, 0, :], k[0:64, :], T[0:64, 2, :], ALU.mult))
                eng.tensor_tensor(kz[64:128, 1, :], k[64:128, :], T[64:128, 2, :], ALU.mult).then_inc(kz_ready, 1)
                bp = T[:, 0, 0:SEQ].rearrange("p (c s) -> p c s", s=CHUNK)
                bs = T[:, 0, SEQ:TOK].rearrange("p (c s) -> p c s", s=DT)
                ch(eng.tensor_copy(ss[:, 0:NCH], T[:, 0, CHUNK - 1:SEQ:CHUNK]))
                ch(eng.tensor_copy(rstd[:, 0:DB], T[:, 0, SEQ + DT - 1:TOK:DT]))
                ch(eng.tensor_tensor(bp, bp, ss[:, 0:NCH].unsqueeze(2).broadcast_to([128, NCH, CHUNK]), ALU.subtract))
                eng.tensor_tensor(bs, bs, rstd[:, 0:DB].unsqueeze(2).broadcast_to([128, DB, DT]),
                                  ALU.subtract).then_inc(e3, 1)
                eng.wait_ge(act_s, 3 * (p + 1))
                eng.tensor_tensor(k[:, :], k[:, :], T[:, 0, :], ALU.mult).then_inc(kend_ready, 1)
                tail_slab(sh, eng, s1 + 1)
                if p == 1:
                    eng.wait_ge(stored, 32)
                eng.memset(S[:, :, :], 0.0).then_inc(s_ready, 1)
                for b in (1, 2):
                    for g in range(3):
                        bank, n, free, t0, tn = fm_unit(sh, s1, b, g)
                        out = rs[:, b - 1, t0:t0 + tn]
                        eng.wait_ge(r_sig, 6 * p + 3 * (b - 1) + g + 1)
                        eng.tensor_tensor(out, bank, T[:, 0, t0:t0 + tn], ALU.mult).then_inc(free, 1)
                place_tile(eng, p, 0)
                for t in range(NT):
                    if t < 8:
                        place_tile(eng, p, t + 1)
                    n = 128 if t < 8 else 64
                    i = NT * p + t
                    eng.wait_ge(att_mm, i + 1)
                    if t < 8:
                        if t >= 2:
                            eng.wait_ge(o_mm, i - 1)
                        eng.copy_predicated(att[:, t % 2, :, :], mask[:, :, :],
                                            sh.ps[:, 4, 0:256].rearrange("p (h t) -> p h t", h=2)).then_inc(att_ready, 1)
                        for c in range(2):
                            m = 2 * t + c
                            eng.wait_ge(ds_mm, 8 * p + t + 1)
                            eng.wait_ge(s_ready, (NCH + 1) * p + m + 1)
                            if m >= 3 and c == 1:
                                eng.wait_ge(o_mm, i)
                            new, old = S[:, (m + 1) % 4], S[:, m % 4]
                            ds = sh.ps[:, 7, 256 * c:256 * c + 256]
                            d = decay[:, m:m + 1]
                            eng.scalar_tensor_tensor(out=new[0:64, 0:128], in0=old[0:64, 0:128], scalar=d[0:64],
                                                     in1=ds[0:64, 0:128], op0=ALU.mult, op1=ALU.add)
                            eng.scalar_tensor_tensor(out=new[64:128, 128:256], in0=old[64:128, 128:256],
                                                     scalar=d[64:128], in1=ds[64:128, 128:256], op0=ALU.mult,
                                                     op1=ALU.add).then_inc(s_ready, 1)
                    else:
                        eng.copy_predicated(att_s[:, :, :], mask_s[:, :, :],
                                            sh.ps[0:64, 4, 0:256].rearrange("p (h t) -> p h t", h=2)[:, :, 0:64]
                                            ).then_inc(att_ready, 1)
                eng.wait_ge(o_mm, NT * (p + 1))
                for b2 in range(4):
                    eng.wait_ge(dss_mm, 4 * p + b2 + 1)
                    for e in range(2):
                        b = 2 * b2 + e
                        ds = sh.ps[:, 7, 256 * e:256 * e + 256]
                        d = decay[:, NCH + b:NCH + b + 1]
                        for h in range(2):
                            r, cc = slice(64 * h, 64 * h + 64), slice(128 * h, 128 * h + 128)
                            last = eng.scalar_tensor_tensor(out=S0[r, b, cc], in0=S0[r, b, cc], scalar=d[r],
                                                            in1=ds[r, cc], op0=ALU.mult, op1=ALU.add)
                    last.then_inc(s0_new, 1)
                eng.wait_ge(o_out, NT * (p + 1))
                ov = v[:, :, :].rearrange("p t (h n) -> p (t h) n", h=2)
                sq = T[:, :, :].rearrange("p a n -> p (a n)")[:, 0:NT * 256].rearrange("p (i n) -> p i n", n=DV)
                ch(eng.tensor_tensor(sq, ov, ov, ALU.mult))
                ch(eng.reduce_sum(ss[:, :], sq, axis=X))
                eng.tensor_scalar(ss[:, :], ss[:, :], 1.0 / DV, EPS, ALU.mult, ALU.add).then_inc(ss_ready, 1)
                eng.wait_ge(sq_ready, p + 1)
                ch(eng.reciprocal(rstd[:, :], ss[:, :]))
                eng.tensor_tensor(ov, ov, rstd[:, :].unsqueeze(2).broadcast_to([128, 2 * NT, DV]),
                                  ALU.mult).then_inc(on_ready, 1)
                for h in range(2):
                    if 2 * p + h:
                        eng.wait_ge(ol_ready, 2 * p + h)
                    for w in range(3):
                        i = NOT * p + 3 * h + w
                        t0, tn = 512 * w, min(512, TOK - 512 * w)
                        eng.wait_ge(oT_tr, i + 1)
                        eng.scalar_tensor_tensor(out=T[:, 0, t0:t0 + tn], in0=sh.ps[:, 2 + i % 2, 0:tn],
                                                 scalar=sh.gnorm[:, 2 * p + h:2 * p + h + 1],
                                                 in1=rs[:, h, t0:t0 + tn], op0=ALU.mult, op1=ALU.mult).then_inc(oT_ready, 1)
                    eng.wait_ge(oh_ready, 2 * p + h + 1)
                    eng.tensor_tensor(T[:, 2, :].bitcast(F32R), T[:, 0, :], T[:, 1, :], ALU.subtract).then_inc(ol_ready, 1)



def stage_fox(nc, sh):
    UN = 16
    chunks = [i // 2 // 4 + 1 for i in range(UN)]
    NCHK = sum(chunks)
    with ExitStack() as ctx:
        def sb(name, shape, dt=F32):
            return ctx.enter_context(nc.sbuf_tensor("fx_" + name, shape, dt))

        def sem(name):
            return sh.front_sem("fx_" + name)
        qh, ql, kh, kl = (sb(n, [HD + 2, 2, SEQ], F32R) for n in ("qh", "ql", "kh", "kl"))
        kT, vT = sb("kT", [128, TOK]), sb("vT", [128, TOK])
        kv = sb("kv", [128, NT, 2 * 128])
        P = sb("P", [128, 2, SEQ])
        PT = sb("PT", [128, 2, 8, 128])
        o_tm = sb("o_tm", [128, 2, 2, HD])
        oh, ol = kT[:, 0:SEQ].bitcast(F32R), vT[:, 0:SEQ].bitcast(F32R)
        mx, nm, rsum = sb("mx", [128, UN]), sb("nm", [128, UN]), sb("rsum", [128, UN])
        rinv = sb("rinv", [128, 2, 2])
        mneg, ident16 = sb("mneg", [128, 128], BF16), sb("ident16", [128, 128], BF16)
        mf = kv[:, 0, 0:128]
        qk_head, cs_in, cs_head, cs_tail, cs_out = (sem(n) for n in ("qk_head", "cs_in", "cs_head", "cs_tail", "cs_out"))
        c_all = P[0:H_FOX].rearrange("p a n -> p (a n)")[:, 0:TOK]
        c_hi = PT[0:H_FOX].rearrange("p a t n -> p (a t n)")[:, 0:TOK].bitcast(F32R)
        c_lo = c_all.bitcast(F32R)
        (pool_s, dve_s, c_in, kv_tr, kv_out, kv_stored, s_ready, nm_ready, exp_done, p_tr, pt_out, pv_done,
         o_out, oT_tr, oT_hi, oT_lo, stored) = (sem(n) for n in (
             "pool", "dve", "c_in", "kv_tr", "kv_out", "kv_stored", "s_ready", "nm_ready", "exp_done", "p_tr",
             "pt_out", "pv_done", "o_out", "oT_tr", "oT_hi", "oT_lo", "stored"))
        block = ctx.enter_context(nc.Block())

        def first_chunk(p, i):
            return NCHK * p + sum(chunks[:i])

        @block.gpsimd
        def _(eng):
            ch = Chain(eng, pool_s)
            for m, ones in ((qh, -1.0), (ql, 0.0), (kh, 1.0), (kl, 0.0)):
                ch(eng.memset(f32(m[HD:HD + 2, :, :]), ones))
            ch(eng.memset(mf[:, :], 0.0))
            ch(eng.affine_select(out=mf[:, :], in_=mf[:, :], compare_op=ALU.is_ge, fill=-BIG, base=0,
                                 pattern=[[-1, 128]], channel_multiplier=1))
            ch(eng.tensor_copy(mneg[:, :], mf[:, :]))
            ch(eng.tensor_copy(ident16[:, :], sh.ident[:, :]))
            ch(eng.memset(sh.qbd[:, :, :, :], 0.0))

        @block.sync
        def _(eng):
            eng.dma_start(c_all, sh.c_dram[0]).then_inc(cs_in, 16)
            eng.wait_ge(cs_tail, 1)
            eng.dma_start(sh.c_dram[2], f32(c_hi)).then_inc(cs_out, 16)
            eng.dma_start(sh.c_dram[3], f32(c_lo)).then_inc(cs_out, 16)
            eng.wait_ge(cs_out, 32)
            eng.wait_ge(pool_s, 4)
            for p in range(4):
                load_slab(sh, eng, FOX0 + p + 2)
                if p >= 1:
                    eng.wait_ge(s_ready, UN * p)
                for j, dst, row in ((2, qh, HD), (2, kh, HD + 1), (3, ql, HD), (3, kl, HD + 1)):
                    eng.dma_start(f32(dst[row:row + 1, :, :]), sh.c_dram[j, 2 * p:2 * p + 2, 0:SEQ].unsqueeze(0)).then_inc(c_in, 16)
                eng.wait_ge(kv_out, NT * (p + 1))
                cols = slice(128 * p, 128 * p + 128)
                for j, (po, so) in enumerate(((sh.prompt_fox_k, sh.sample_fox_k), (sh.prompt_fox_v, sh.sample_fox_v))):
                    part = slice(128 * j, 128 * j + 128)
                    eng.dma_start(po[0, 0].rearrange("(t p) h d -> p t (h d)", p=128)[:, :, cols],
                                  kv[:, 0:8, part]).then_inc(kv_stored, 16)
                    eng.dma_start(so[0].rearrange("b t h d -> (b t) (h d)")[:, cols],
                                  kv[0:64, 8, part]).then_inc(kv_stored, 16)
                eng.wait_ge(oT_lo, 8 * (p + 1))
                store_branch(sh, eng, 1, cols, slice(0, SEQ), oh[:, :], ol[:, :], stored)
            eng.wait_ge(kv_stored, 64 * 4)
            eng.wait_ge(stored, 32 * 4)

        @block.tensor
        def _(eng):
            def scores(p, i):
                qt, h = divmod(i, 2)
                I, kn = UN * p + i, 128 * (qt + 1)
                if I >= 2:
                    eng.wait_ge(exp_done, I - 1)
                bank0 = 2 + 2 * (i % 2)
                for k0 in range(0, kn, 512):
                    n = min(512, kn - k0)
                    out = sh.ps[:, bank0 + k0 // 512, 0:n]
                    diag = k0 + n == kn
                    for j, (q, k) in enumerate(((qh, kh), (qh, kl), (ql, kh))):
                        last = eng.matmul(out, q[:, h, 128 * qt:128 * qt + 128], k[:, h, k0:k0 + n],
                                          start=(j == 0), stop=(j == 2 and not diag), skip_group_check=True)
                    if diag:
                        last = eng.matmul(out[:, n - 128:n], ident16[:, :], mneg[:, :], start=False, stop=True,
                                          skip_group_check=True)
                last.then_inc(s_ready, 1)

            def transpose_probs(p, i):
                qt = i // 2
                eng.wait_ge(exp_done, UN * p + i + 1)
                for c in range(chunks[i]):
                    C = first_chunk(p, i) + c
                    if C >= 2:
                        eng.wait_ge(pt_out, C - 1)
                    for t in range(4 * c, min(4 * c + 4, qt + 1)):
                        last = eng.transpose(sh.ps[:, 6 + C % 2, 128 * (t % 4):128 * (t % 4) + 128],
                                             P[:, i % 2, 128 * t:128 * t + 128], sh.ident[:, :])
                    last.then_inc(p_tr, 1)

            def weigh_values(p, i):
                qt, h = divmod(i, 2)
                eng.wait_ge(pt_out, first_chunk(p, i) + chunks[i])
                if h == 0 and qt >= 2:
                    eng.wait_ge(oT_lo, 8 * p + qt - 1)
                for t in range(qt + 1):
                    last = eng.matmul(sh.ps[:, qt % 2, 64 * h:64 * h + 64], PT[:, i % 2, t, :],
                                      kv[:, t, 128 + 64 * h:128 + 64 * h + 64],
                                      start=(h == 0 and t == 0), stop=(t == qt), skip_group_check=True)
                last.then_inc(pv_done, 1)

            def transpose_out(p, qt):
                eng.wait_ge(o_out, 8 * p + qt + 1)
                eng.transpose(sh.ps[:, qt % 2, 128:256], o_tm[:, qt % 2, :, :].rearrange("p h d -> p (h d)"),
                              sh.ident[:, :]).then_inc(oT_tr, 1)

            for p in range(4):
                n = FOX0 + p
                if p >= 1:
                    eng.wait_ge(oT_lo, 8 * p)
                project_slab(sh, eng, n, 2 if p == 0 else 0)
                for b in range(3):
                    wait_block_freed(sh, eng, n, b)
                eng.wait_ge(c_in, 64 * (p + 1))
                if p == 0:
                    eng.wait_ge(pool_s, 9)
                for t in range(NT):
                    m = 128 if t < 8 else 64
                    if t >= 2:
                        eng.wait_ge(kv_out, NT * p + t - 1)
                    else:
                        eng.wait_ge(pt_out, NCHK * p)
                    tok = slice(128 * t, 128 * t + m)
                    bank = sh.ps[0:m, 6 + t % 2, :]
                    eng.transpose(bank[:, 0:128], kT[:, tok], sh.ident[:, :])
                    eng.transpose(bank[:, 128:256], vT[:, tok], sh.ident[:, :]).then_inc(kv_tr, 1)
                eng.wait_ge(kv_out, NT * (p + 1))
                scores(p, 0)
                for i in range(UN + 2):
                    if i + 1 < UN:
                        scores(p, i + 1)
                    if i < UN:
                        transpose_probs(p, i)
                    if 1 <= i <= UN:
                        weigh_values(p, i - 1)
                    if i >= 3 and i % 2:
                        transpose_out(p, (i - 3) // 2)

        @block.scalar
        def _(eng):
            eng.wait_ge(cs_in, 16)
            eng.activation(c_hi, c_all, ACT.Copy).then_inc(cs_head, 1)
            for p in range(4):
                n0 = FOX0 + p
                head_slab(sh, eng, n0 + 1)
                for g in range(3):
                    bank, n, free, t0, tn = fm_unit(sh, n0, 0, g)
                    eng.wait_ge(sh.fm_ready, n)
                    if g == 2:
                        if p == 0:
                            eng.wait_ge(pool_s, 9)
                        for h in range(2):
                            at = 16 * p + 8 * h
                            eng.activation(sh.qbd[64 * h:64 * h + 64, p, :, at:at + 8],
                                           bank[64 * h:64 * h + 64, SEQ - t0:].rearrange("p (b t) -> p b t", b=DB),
                                           ACT.Copy, scale=HD ** -0.5)
                    pn = min(tn, SEQ - t0)
                    for h in range(2):
                        last = eng.activation(qh[0:HD, h, t0:t0 + pn], bank[64 * h:64 * h + 64, 0:pn], ACT.Copy,
                                              scale=HD ** -0.5)
                    last.then_inc(qk_head, 1)
                for g in range(3):
                    bank, n, free, t0, tn = fm_unit(sh, n0, 1, g)
                    eng.wait_ge(sh.fm_ready, n)
                    pn = min(tn, SEQ - t0)
                    for h in range(2):
                        last = eng.activation(kh[0:HD, h, t0:t0 + pn], bank[64 * h:64 * h + 64, 0:pn], ACT.Copy)
                    last.then_inc(qk_head, 1)
                for g in range(3):
                    bank, n, free, t0, tn = fm_unit(sh, n0, 2, g)
                    eng.wait_ge(sh.fm_ready, n)
                    if p >= 1 and g == 0:
                        eng.wait_ge(stored, 32 * p)
                    eng.activation(vT[:, t0:t0 + tn], bank, ACT.Copy).then_inc(free, 1)
                for i in range(-1, UN + 2):
                    if i + 1 < UN:
                        I = UN * p + i + 1
                        eng.wait_ge(nm_ready, I + 1)
                        if i + 1 >= 2:
                            eng.wait_ge(p_tr, first_chunk(p, i - 1) + chunks[i - 1])
                        kn = 128 * ((i + 1) // 2 + 1)
                        s = sh.ps[:, 2 + 2 * ((i + 1) % 2):4 + 2 * ((i + 1) % 2), :].rearrange("p a n -> p (a n)")
                        eng.activation(P[:, (i + 1) % 2, 0:kn], s[:, 0:kn], ACT.Exp, bias=nm[:, i + 1:i + 2],
                                       accum_out=rsum[:, i + 1:i + 2]).then_inc(exp_done, 1)
                    if i >= 3 and i % 2:
                        qt = (i - 3) // 2
                        eng.wait_ge(oT_tr, 8 * p + qt + 1)
                        eng.activation(oh[:, 128 * qt:128 * qt + 128], sh.ps[:, qt % 2, 128:256],
                                       ACT.Copy).then_inc(oT_hi, 1)

        @block.vector
        def _(eng):
            ch = Chain(eng, dve_s)
            eng.wait_ge(cs_head, 1)
            eng.tensor_tensor(c_lo, c_all, f32(c_hi), ALU.subtract).then_inc(cs_tail, 1)
            for p in range(4):
                n0 = FOX0 + p
                tail_slab(sh, eng, n0 + 1)
                for g in range(3):
                    bank, n, free, t0, tn = fm_unit(sh, n0, 0, g)
                    eng.wait_ge(qk_head, 6 * p + g + 1)
                    pn = min(tn, SEQ - t0)
                    for h in range(2):
                        last = eng.scalar_tensor_tensor(out=ql[0:HD, h, t0:t0 + pn], in0=bank[64 * h:64 * h + 64, 0:pn],
                                                        scalar=HD ** -0.5, in1=f32(qh[0:HD, h, t0:t0 + pn]),
                                                        op0=ALU.mult, op1=ALU.subtract)
                    last.then_inc(free, 1)
                for g in range(3):
                    bank, n, free, t0, tn = fm_unit(sh, n0, 1, g)
                    eng.wait_ge(qk_head, 6 * p + g + 4)
                    if p >= 1 and g == 0:
                        eng.wait_ge(stored, 32 * p)
                    if g == 2:
                        eng.tensor_copy(sh.kTs[:, p, :], bank[:, SEQ - t0:])
                    eng.tensor_copy(kT[:, t0:t0 + tn], bank)
                    pn = min(tn, SEQ - t0)
                    for h in range(2):
                        last = eng.tensor_tensor(kl[0:HD, h, t0:t0 + pn], bank[64 * h:64 * h + 64, 0:pn],
                                                 f32(kh[0:HD, h, t0:t0 + pn]), ALU.subtract)
                    last.then_inc(free, 1)
                if p >= 1:
                    eng.wait_ge(kv_stored, 64 * p)
                    eng.wait_ge(pv_done, UN * p)
                for t in range(NT):
                    m = 128 if t < 8 else 64
                    eng.wait_ge(kv_tr, NT * p + t + 1)
                    if t == 8:
                        ch(eng.tensor_copy(sh.vs[:, 128 * p:128 * p + 128], sh.ps[0:m, 6 + t % 2, 128:256]))
                    eng.tensor_copy(kv[0:m, t, :], sh.ps[0:m, 6 + t % 2, 0:256]).then_inc(kv_out, 1)
                for i in range(-1, UN + 2):
                    if i + 1 < UN:
                        I = UN * p + i + 1
                        eng.wait_ge(s_ready, I + 1)
                        kn = 128 * ((i + 1) // 2 + 1)
                        s = sh.ps[:, 2 + 2 * ((i + 1) % 2):4 + 2 * ((i + 1) % 2), :].rearrange("p a n -> p (a n)")
                        if I >= UN:
                            eng.wait_ge(exp_done, I + 1 - UN)
                        ch(eng.reduce_max(mx[:, i + 1:i + 2], s[:, 0:kn], axis=X))
                        eng.tensor_scalar(nm[:, i + 1:i + 2], mx[:, i + 1:i + 2], -1.0, None,
                                          ALU.mult).then_inc(nm_ready, 1)
                    if 0 <= i < UN:
                        qt = i // 2
                        if UN * p + i >= 2:
                            eng.wait_ge(pv_done, UN * p + i - 1)
                        for c in range(chunks[i]):
                            C = first_chunk(p, i) + c
                            eng.wait_ge(p_tr, C + 1)
                            nt = min(4, qt + 1 - 4 * c)
                            eng.tensor_copy(PT[:, i % 2, 4 * c:4 * c + nt, :].rearrange("p t n -> p (t n)"),
                                            sh.ps[:, 6 + C % 2, 0:128 * nt]).then_inc(pt_out, 1)
                    if i >= 2 and i % 2 == 0:
                        qt = (i - 2) // 2
                        eng.wait_ge(pv_done, UN * p + i)
                        if 8 * p + qt >= 2:
                            eng.wait_ge(oT_tr, 8 * p + qt - 1)
                        ch(eng.reciprocal(rinv[:, qt % 2, :], rsum[:, 2 * qt:2 * qt + 2]))
                        eng.tensor_tensor(o_tm[:, qt % 2, :, :],
                                          sh.ps[:, qt % 2, 0:128].rearrange("p (h d) -> p h d", h=2),
                                          rinv[:, qt % 2, :].unsqueeze(2).broadcast_to([128, 2, HD]),
                                          ALU.mult).then_inc(o_out, 1)
                    if i >= 3 and i % 2:
                        qt = (i - 3) // 2
                        eng.wait_ge(oT_hi, 8 * p + qt + 1)
                        eng.tensor_tensor(ol[:, 128 * qt:128 * qt + 128], sh.ps[:, qt % 2, 128:256],
                                          f32(oh[:, 128 * qt:128 * qt + 128]), ALU.subtract).then_inc(oT_lo, 1)


def stage_fox_sample(nc, sh):
    R = H_FOX * DT
    KN = NPAGE * PAGE + DB * DT
    PAST = NPAGE * PAGE
    RP = 4
    with ExitStack() as ctx:
        def sb(name, shape, dt=F32):
            return ctx.enter_context(nc.sbuf_tensor("fs_" + name, shape, dt))

        def sem(name):
            return sh.front_sem("fs_" + name)
        pages = sb("pages", [1, DB * NPAGE], I32)
        kp, vp = sb("kp", [128, RP, NPAGE, BW]), sb("vp", [128, RP, NPAGE, BW])
        lf = sb("lf", [128, RP, NPAGE, H_FOX])
        KT = sb("KT", [128, 2, 4, PAST])
        bias = sb("bias", [H_FOX, 2, KN])
        cs, cneg = sb("cs", [H_FOX, DB * DT]), sb("cneg", [H_FOX, DB * DT])
        head = sb("head", [H_FOX, R])
        headc = sb("headc", [H_FOX, 2, R])
        tsel = sb("tsel", [DT, R])
        base, window = sb("base", [DT, 128]), sb("window", [R, 128])
        after, ones = sb("after", [128, 128]), sb("ones", [128, KN])
        P, PT = sb("P", [R, 2, KN]), sb("PT", [128, 2, 3, R])
        mx, nm, rsum, rinv = (sb(n, [R, DB]) for n in ("mx", "nm", "rsum", "rinv"))
        oT = sb("oT", [128, 4, DB * DT])
        oh, ol = sb("oh", [128, 4, DB * DT], F32R), sb("ol", [128, 4, DB * DT], F32R)
        (pool_s, dve_s, small_in, k_tr, k_out, b_mm, b_out, w_mm, w_out, s_mm, nm_ready, exp_done, p_ready,
         p_tr, pt_out, pv_mm, o_out, oT_hi, oT_lo, stored) = (sem(n) for n in (
             "pool", "dve", "small_in", "k_tr", "k_out", "b_mm", "b_out", "w_mm", "w_out", "s_mm",
             "nm_ready", "exp_done", "p_ready", "p_tr", "pt_out", "pv_mm", "o_out", "oT_hi", "oT_lo", "stored"))
        k_in, v_in = ([sem(f"{n}_in{i}") for i in range(RP)] for n in "kv")
        block = ctx.enter_context(nc.Block())

        @block.gpsimd
        def _(eng):
            ch = Chain(eng, pool_s)
            for m in (head, tsel):
                ch(eng.memset(m[:, :], 0.0))
            hv = head[:, :].rearrange("p (h t) -> p h t", h=H_FOX)
            tv = tsel[:, :].rearrange("p (h t) -> p h t", h=H_FOX)
            ch(eng.affine_select(out=hv, in_=hv, compare_op=ALU.not_equal, fill=1.0, base=0,
                                 pattern=[[-1, H_FOX], [0, DT]], channel_multiplier=1))
            ch(eng.affine_select(out=tv, in_=tv, compare_op=ALU.not_equal, fill=1.0, base=0,
                                 pattern=[[0, H_FOX], [-1, DT]], channel_multiplier=1))
            off = (DB - 1) * DT
            ch(eng.memset(base[:, :], 0.0))
            ch(eng.affine_select(out=base[:, :], in_=base[:, :], compare_op=ALU.is_ge, fill=-BIG, base=-off,
                                 pattern=[[1, 128]], channel_multiplier=0))
            ch(eng.affine_select(out=base[:, :], in_=base[:, :], compare_op=ALU.is_ge, fill=-BIG, base=off,
                                 pattern=[[-1, 128]], channel_multiplier=1))
            ch(eng.memset(after[:, :], 1.0))
            ch(eng.affine_select(out=after[:, :], in_=after[:, :], compare_op=ALU.is_gt, fill=0.0, base=0,
                                 pattern=[[-1, 128]], channel_multiplier=1))
            ch(eng.memset(ones[:, :], 1.0))
            for s in range(2):
                tail_gates(sh, eng, s, s)
        POOL_DONE = 10

        @block.sync
        def _(eng):
            eng.dma_start(pages[:, :], sh.page_table.rearrange("b p -> (b p)").unsqueeze(0)).then_inc(small_in, 16)
            eng.wait_ge(small_in, 16)
            for b in range(DB):
                if b >= RP:
                    eng.wait_ge(b_mm, b - RP + 1)
                page = [eng.value_load(pages[0:1, NPAGE * b + g:NPAGE * b + g + 1], min_val=0,
                                       max_val=sh.cache_fox_k.shape[1] - 1) for g in range(NPAGE)]
                for g in range(NPAGE):
                    eng.dma_start(kp[:, b % RP, g, :], sh.cache_fox_k[0, bass.ds(page[g], 1)].rearrange("o s h d -> (o s) (h d)")
                                  ).then_inc(k_in[b % RP], 16)
                    eng.dma_start(lf[:, b % RP, g, :], sh.cache_fox_logf[0, bass.ds(page[g], 1)].rearrange("o s h -> (o s) h")
                                  ).then_inc(k_in[b % RP], 16)
                if b >= RP:
                    eng.wait_ge(pv_mm, b - RP + 1)
                for g in range(NPAGE):
                    eng.dma_start(vp[:, b % RP, g, :], sh.cache_fox_v[0, bass.ds(page[g], 1)].rearrange("o s h d -> (o s) (h d)")
                                  ).then_inc(v_in[b % RP], 16)
                if b == 0:
                    eng.dma_start(cs[:, :], sh.c_dram[0, :, SEQ:TOK]).then_inc(small_in, 16)
                    eng.dma_start(cneg[:, :], sh.c_dram[1, :, SEQ:TOK]).then_inc(small_in, 16)
                if b == RP - 1:
                    load_gates(sh, eng, 0, 0, 0)
            load_gates(sh, eng, 0, 1, 1)
            eng.wait_ge(oT_lo, 1)
            for dst, src in ((sh.oT_hi, oh), (sh.oT_lo, ol)):
                eng.dma_start(dst[1, :, SEQ:TOK].rearrange("(c p) n -> p c n", p=128), f32(src[:, :, :])).then_inc(stored, 16)
            eng.wait_ge(stored, 32)

        @block.tensor
        def _(eng):
            eng.wait_ge(pool_s, POOL_DONE)
            eng.matmul(sh.ps[0:R, 7, 0:128], tsel[:, :], base[:, :], start=True, stop=True).then_inc(w_mm, 1)
            eng.wait_ge(w_out, 1)

            def transpose_keys(b):
                r = b % RP
                eng.wait_ge(k_in[r], 64 * (b // RP + 1))
                if b >= 1:
                    eng.wait_ge(k_out, 2 * b)
                for g in range(NPAGE):
                    for c in range(4):
                        last = eng.transpose(sh.ps[:, g, 128 * c:128 * c + 128], kp[:, r, g, 128 * c:128 * c + 128],
                                             sh.ident[:, :])
                    last.then_inc(k_tr, 1)
                if b >= 1:
                    eng.wait_ge(b_out, b)
                eng.matmul(sh.ps[0:H_FOX, 2, 0:128], lf[:, r, 0, :], after[:, :], start=True, stop=False)
                eng.matmul(sh.ps[0:H_FOX, 2, 0:128], lf[:, r, 1, :], ones[:, 0:128], start=False, stop=True)
                eng.matmul(sh.ps[0:H_FOX, 2, 128:256], lf[:, r, 1, :], after[:, :], start=True,
                           stop=True, skip_group_check=True).then_inc(b_mm, 1)

            def scores(b):
                r = b % 2
                eng.wait_ge(b_out, b + 1)
                eng.wait_ge(k_out, 2 * b + 2)
                if b >= 2:
                    eng.wait_ge(exp_done, b - 1)
                out = sh.ps[0:R, 3 + r, 0:KN]
                eng.matmul(out, head[:, :], bias[:, r, :], start=True, stop=False, skip_group_check=True)
                eng.matmul(out, headc[:, r, :], ones[0:H_FOX, :], start=False, stop=False, skip_group_check=True)
                for c in range(4):
                    eng.matmul(out[:, 0:PAST], sh.qbd[:, c, b, :], KT[:, r, c, :], start=False, stop=False,
                               skip_group_check=True)
                    eng.matmul(out[:, PAST:], sh.qbd[:, c, b, :], sh.kTs[:, c, :], start=False, stop=False,
                               skip_group_check=True)
                w0 = (DB - 1 - b) * DT
                eng.matmul(out[:, PAST:], sh.ident[0:R, 0:R], window[:, w0:w0 + DB * DT], start=False, stop=True,
                           skip_group_check=True).then_inc(s_mm, 1)

            def transpose_probs(b):
                r = b % 2
                eng.wait_ge(p_ready, b + 1)
                if b >= 1:
                    eng.wait_ge(pt_out, b)
                for g, n in enumerate((128, 128, 64)):
                    last = eng.transpose(sh.ps[0:n, 5, R * g:R * g + R], P[:, r, 128 * g:128 * g + n],
                                         sh.ident[0:R, 0:R])
                last.then_inc(p_tr, 1)

            def weigh_values(b):
                r, rp = b % 2, b % RP
                eng.wait_ge(pt_out, b + 1)
                eng.wait_ge(v_in[rp], 32 * (b // RP + 1))
                if b >= 1:
                    eng.wait_ge(o_out, b)
                for c in range(4):
                    out, cc = sh.ps[:, 6, R * c:R * c + R], slice(128 * c, 128 * c + 128)
                    eng.matmul(out, vp[:, rp, 0, cc], PT[:, r, 0, :], start=(c == 0), stop=False, skip_group_check=True)
                    eng.matmul(out, vp[:, rp, 1, cc], PT[:, r, 1, :], start=False, stop=False, skip_group_check=True)
                    last = eng.matmul(out, sh.vs[:, cc], PT[0:64, r, 2, :], start=False, stop=True, skip_group_check=True)
                last.then_inc(pv_mm, 1)

            for i in range(DB + 3):
                for step, b in ((transpose_keys, i), (transpose_probs, i - 2), (scores, i - 1), (weigh_values, i - 3)):
                    if 0 <= b < DB:
                        step(b)

        @block.scalar
        def _(eng):
            for b in range(DB):
                r = b % 2
                eng.wait_ge(nm_ready, b + 1)
                if b >= 2:
                    eng.wait_ge(p_tr, b - 1)
                eng.activation(P[:, r, :], sh.ps[0:R, 3 + r, 0:KN], ACT.Exp, bias=nm[:, b:b + 1],
                               accum_out=rsum[:, b:b + 1]).then_inc(exp_done, 1)
                if b == RP:
                    head_gates(sh, eng, 0, 0)
            head_gates(sh, eng, 1, 1)
            eng.wait_ge(o_out, DB)
            eng.activation(oh[:, :, :], oT[:, :, :], ACT.Copy).then_inc(oT_hi, 1)

        @block.vector
        def _(eng):
            ch = Chain(eng, dve_s)
            eng.wait_ge(w_mm, 1)
            eng.tensor_copy(window[:, :], sh.ps[0:R, 7, 0:128]).then_inc(w_out, 1)
            eng.wait_ge(small_in, 48)
            eng.wait_ge(pool_s, POOL_DONE)

            def place_keys(b):
                r = b % 2
                for g in range(NPAGE):
                    eng.wait_ge(k_tr, 2 * b + g + 1)
                    if b >= 2:
                        eng.wait_ge(s_mm, b - 1)
                    eng.tensor_copy(KT[:, r, :, 128 * g:128 * g + 128],
                                    sh.ps[:, g, :].rearrange("p (c n) -> p c n", c=4)).then_inc(k_out, 1)
                ch(eng.tensor_tensor(headc[:, r, :].rearrange("p (h t) -> p h t", h=H_FOX),
                                     head[:, :].rearrange("p (h t) -> p h t", h=H_FOX),
                                     cs[:, DT * b:DT * b + DT].unsqueeze(1).broadcast_to([H_FOX, H_FOX, DT]), ALU.mult))
                ch(eng.tensor_copy(bias[:, r, PAST:], cneg[:, :]))
                eng.wait_ge(b_mm, b + 1)
                eng.tensor_copy(bias[:, r, 0:PAST], sh.ps[0:H_FOX, 2, 0:PAST]).then_inc(b_out, 1)

            def maximum(b):
                eng.wait_ge(s_mm, b + 1)
                ch(eng.reduce_max(mx[:, b:b + 1], sh.ps[0:R, 3 + b % 2, 0:KN], axis=X))
                eng.tensor_scalar(nm[:, b:b + 1], mx[:, b:b + 1], -1.0, None, ALU.mult).then_inc(nm_ready, 1)

            def normalise(b):
                eng.wait_ge(exp_done, b + 1)
                ch(eng.reciprocal(rinv[:, b:b + 1], rsum[:, b:b + 1]))
                eng.tensor_scalar(P[:, b % 2, :], P[:, b % 2, :], rinv[:, b:b + 1], None, ALU.mult).then_inc(p_ready, 1)

            def place_probs(b):
                r = b % 2
                eng.wait_ge(p_tr, b + 1)
                if b >= 2:
                    eng.wait_ge(pv_mm, b - 1)
                ch(eng.tensor_copy(PT[0:64, r, 2, :], sh.ps[0:64, 5, 2 * R:3 * R]))
                eng.tensor_copy(PT[:, r, 0:2, :], sh.ps[:, 5, 0:2 * R].rearrange("p (g n) -> p g n", g=2)).then_inc(pt_out, 1)

            def place_output(b):
                eng.wait_ge(pv_mm, b + 1)
                o = sh.ps[:, 6, 0:4 * 80].rearrange("p (c n) -> p c n", c=4)
                eng.tensor_copy(oT[0:64, :, DT * b:DT * b + DT], o[0:64, :, 0:DT])
                eng.tensor_copy(oT[64:128, :, DT * b:DT * b + DT], o[64:128, :, DT:2 * DT]).then_inc(o_out, 1)

            for i in range(DB + 3):
                for step, b in ((normalise, i - 2), (place_keys, i), (place_probs, i - 2), (maximum, i - 1),
                                (place_output, i - 3)):
                    if 0 <= b < DB:
                        step(b)
            eng.wait_ge(oT_hi, 1)
            eng.tensor_tensor(ol[:, :, :], oT[:, :, :], f32(oh[:, :, :]), ALU.subtract).then_inc(oT_lo, 1)


def load_gates(sh, eng, j, cp, n):
    raw = weight_views(sh, 2, 12)[0]
    if not isinstance(n, int) or n > 0:
        eng.wait_ge(sh.g_split, n)
    for c in range(2):
        col = (2 * cp + c) * 128
        eng.dma_start(raw[:, c, 0:8, :],
                      sh.w_in[0, :, bass.ds(GATE + col + j * D, 128)].rearrange("(k p) n -> p k n", p=128)
                      ).then_inc(sh.g_loaded, 16)
        eng.dma_start(raw[:, c, 8:12, :],
                      sh.w_branch[0, bass.ds(j, 1), :, col:col + 128].rearrange("o (k p) n -> p (o k) n", p=128)
                      ).then_inc(sh.g_loaded, 16)


def head_gates(sh, eng, n, s):
    raw, hi, _lo = weight_views(sh, 2, 12)
    eng.wait_ge(sh.g_loaded, 64 * (n + 1))
    eng.activation(hi[:, s % 2], raw, ACT.Copy).then_inc(sh.g_head, 1)


def tail_gates(sh, eng, n, s):
    raw, hi, lo = weight_views(sh, 2, 12)
    eng.wait_ge(sh.g_head, n + 1)
    eng.tensor_tensor(lo[:, s % 2], raw, f32(hi[:, s % 2]), ALU.subtract).then_inc(sh.g_split, 1)


def stage_gates(nc, sh):
    UJ = 24
    with ExitStack() as ctx:
        def sb(name, shape, dt=F32):
            return ctx.enter_context(nc.sbuf_tensor("gt_" + name, shape, dt))

        def sem(name):
            return sh.front_sem("gt_" + name)
        _w_raw, w_hi, w_lo = weight_views(sh, 2, 12)
        oh, ol = sb("oh", [128, 4, TOK], F32R), sb("ol", [128, 4, TOK], F32R)
        sg = sb("sg", [128, 4, 384])
        first = sb("first", [1, 1])
        m_clear = sem("m_clear")
        split = sh.g_split
        (o_in, gate_mm, br_mm, sg_ready, mul_done, m_done) = (sem(n) for n in (
            "o_in", "gate_mm", "br_mm", "sg_ready", "mul_done", "m_done"))
        block = ctx.enter_context(nc.Block())

        @block.gpsimd
        def _(eng):
            eng.memset(first[:, :], 0.0).then_inc(m_done, 1)
            eng.memset(sh.m[:, :, :], 0.0).then_inc(m_clear, 1)

        @block.sync
        def _(eng):
            def branch(j, last):
                eng.wait_ge(m_done, UJ * j + 1)
                for dst, src in ((oh, sh.oT_hi), (ol, sh.oT_lo)):
                    eng.dma_start(f32(dst[:, :, :]), src[bass.ds(j, 1)].rearrange("o (k p) n -> p (o k) n", p=128)
                                  ).then_inc(o_in, 16)
                for s in range(2 if last else 4):
                    load_gates(sh, eng, j if s < 2 else j + 1, (s + 2) % 4, 4 * j + s + 2)
            with eng.Fori(0, 2) as j:
                branch(j, False)
            branch(2, True)

        @block.tensor
        def _(eng):
            def branch(j):
                eng.wait_ge(m_done, UJ * j + 1)
                for s in range(4):
                    eng.wait_ge(split, 4 * j + s + 1)
                    for c in range(2):
                        for kind, bank0, ks, hi, lo, done in (("gate", 0, range(8), sh.xh, sh.xl, gate_mm),
                                                              ("branch", 4, range(4), oh, ol, br_mm)):
                            if kind == "branch" and s == 0 and c == 0:
                                eng.wait_ge(o_in, 32 * j + 32)
                            for g, (t0, tn) in enumerate(GROUPS):
                                v = 3 * (2 * s + c) + g
                                if v >= 4:
                                    eng.wait_ge(m_done, UJ * j + v - 2)
                                out = sh.ps[:, bank0 + v % 4, 0:tn]
                                for k in ks:
                                    wk = k + (8 if bank0 else 0)
                                    for i, (w, x) in enumerate(((w_hi, hi), (w_hi, lo), (w_lo, hi))):
                                        last = eng.matmul(out, w[:, s % 2, c, wk, :], x[:, k, t0:t0 + tn],
                                                          start=(k == 0 and i == 0), stop=(k == ks[-1] and i == 2))
                                last.then_inc(done, 1)
            with eng.Fori(0, 2) as j:
                branch(j)
            branch(2)

        @block.scalar
        def _(eng):
            def branch(j, last):
                for s in range(4):
                    for u in range(6):
                        v = 6 * s + u
                        t0, tn = GROUPS[u % 3]
                        eng.wait_ge(gate_mm, UJ * j + v + 1)
                        eng.activation(sg[:, v % 4, 0:tn], sh.ps[:, v % 4, 0:tn], ACT.Sigmoid).then_inc(sg_ready, 1)
                    if not last or s < 2:
                        eng.wait_ge(br_mm, UJ * j + 6 * s + 6)
                        head_gates(sh, eng, 4 * j + s + 2, s)
            with eng.Fori(0, 2) as j:
                branch(j, False)
            branch(2, True)

        @block.vector
        def _(eng):
            eng.wait_ge(m_clear, 1)

            def branch(j, last):
                for s in range(4):
                    for u in range(6):
                        v = 6 * s + u
                        t0, tn = GROUPS[u % 3]
                        fb = 2 * s + u // 3
                        eng.wait_ge(sg_ready, UJ * j + v + 1)
                        eng.wait_ge(br_mm, UJ * j + v + 1)
                        eng.tensor_tensor(sg[:, v % 4, 0:tn], sh.ps[:, 4 + v % 4, 0:tn], sg[:, v % 4, 0:tn],
                                          ALU.mult).then_inc(mul_done, 1)
                        eng.wait_ge(mul_done, UJ * j + v + 1)
                        eng.tensor_tensor(sh.m[:, fb, t0:t0 + tn], sh.m[:, fb, t0:t0 + tn], sg[:, v % 4, 0:tn],
                                          ALU.add).then_inc(m_done, 1)
                    if not last or s < 2:
                        tail_gates(sh, eng, 4 * j + s + 2, s)
            with eng.Fori(0, 2) as j:
                branch(j, False)
            branch(2, True)


def tile_rows(t):
    return (128 * t, 0) if t < 8 else (TOK - 128, 64)


def stage_out(nc, sh):
    with ExitStack() as ctx:
        def sb(name, shape, dt=F32):
            return ctx.enter_context(nc.sbuf_tensor("wo_" + name, shape, dt))

        def sem(name):
            return sh.front_sem("wo_" + name)
        w_raw = sb("w_raw", [128, 2, D])
        KS = 2 * SLAB // D
        part = [t[:, :].rearrange("p (k n) -> p k n", k=KS) for t in (sh.slab_hi, sh.slab_lo)]
        rest = [sb(n, [128, KC - KS, D], F32R) for n in ("w_hi", "w_lo")]
        w_hi, w_lo = ([a[:, k, :] for k in range(KS)] + [b[:, k, :] for k in range(KC - KS)] for a, b in zip(part, rest))
        x1 = sh.slab_raw[:, :].rearrange("p (b n) -> p b n", b=3)
        r, gb, bb = (sb(n, [128, D]) for n in ("r", "gb", "bb"))
        x = w_raw
        x1T = sb("x1T", [128, KC, 128])
        wr, brb = sb("wr", [128, KC, NE]), sb("brb", [128, NE])
        st, mv = sb("st", [128, 2, 6]), sb("mv", [128, 2])
        std, rstd = sb("std", [128, 1]), sb("rstd", [128, 1])
        (c_in, w_in0, w_in1, w_head, w_tail, m_head, m_tail, x_in0, x_in1, mix_mm, dve_s, var_ready, std_ready, x1_ready, x1_tr,
         x1T_out, lg_mm, lg_out, r_ready) = (sem(n) for n in (
             "c_in", "w_in0", "w_in1", "w_head", "w_tail", "m_head", "m_tail", "x_in0", "x_in1", "mix_mm", "dve", "var_ready",
             "std_ready", "x1_ready", "x1_tr", "x1T_out", "lg_mm", "lg_out", "r_ready"))
        x_in, w_in = [x_in0, x_in1], [w_in0, w_in1]
        stored = [sh.dma_sem(f"wo_stored{i}") for i in range(3)]
        block = ctx.enter_context(nc.Block())

        @block.sync
        def _(eng):
            for k in range(KC):
                if k >= 2:
                    eng.wait_ge(w_tail, k - 1)
                eng.dma_start(w_raw[:, k % 2, :], sh.w_out[0, 128 * k:128 * k + 128, :]).then_inc(w_in[k % 2], 16)
                if k == 1:
                    for dst, src in ((gb, sh.ln1_g), (bb, sh.ln1_b)):
                        eng.dma_start(dst[:, :], src.broadcast_to([128, D])).then_inc(c_in, 16)
                    eng.dma_start(brb[:, :], sh.b_router.unsqueeze(0).broadcast_to([128, NE])).then_inc(c_in, 16)
                    eng.dma_start(wr[:, :, :], sh.w_router.rearrange("(k p) n -> p k n", p=128)).then_inc(c_in, 16)
            for t in range(NT):
                if t >= 2:
                    eng.wait_ge(r_ready, t - 1)
                else:
                    eng.wait_ge(w_tail, KC - 1 + t)
                if t < 8:
                    eng.dma_start(x[:, t % 2, :], sh.x_prompt[0, 128 * t:128 * t + 128, :]).then_inc(x_in[t % 2], 16)
                else:
                    eng.dma_start(x[0:64, t % 2, :], sh.x_prompt[0, SEQ - 64:SEQ, :]).then_inc(x_in[t % 2], 16)
                    eng.dma_start(x[64:128, t % 2, :], sh.x_sample.rearrange("b t d -> (b t) d")).then_inc(x_in[t % 2], 16)

        @block.gpsimd
        def _(eng):
            for t in range(NT):
                t0, p0 = tile_rows(t)
                eng.wait_ge(x1_ready, t + 1)
                eng.dma_start(sh.x1_dram[t0 + p0:t0 + 128, :], x1[p0:128, t % 3, :]).then_inc(stored[t % 3], 16)
            for i in range(3):
                eng.wait_ge(stored[i], 16 * 3)

        @block.tensor
        def _(eng):
            def transpose_x1(t):
                eng.wait_ge(x1_ready, t + 1)
                for half in range(2):
                    u = 2 * t + half
                    if u >= 2:
                        eng.wait_ge(x1T_out, u - 1)
                    for k in range(4):
                        c0 = 128 * (4 * half + k)
                        last = eng.transpose(sh.ps[:, 4 + half, 128 * k:128 * k + 128], x1[:, t % 3, c0:c0 + 128],
                                             sh.ident[:, :])
                    last.then_inc(x1_tr, 1)

            def router(t):
                eng.wait_ge(x1T_out, 2 * t + 2)
                if t >= 2:
                    eng.wait_ge(lg_out, t - 1)
                for k in range(KC):
                    last = eng.matmul(sh.ps[:, 6 + t % 2, 0:NE], x1T[:, k, :], wr[:, k, :], start=(k == 0), stop=(k == KC - 1))
                last.then_inc(lg_mm, 1)

            def mix(t, half, k):
                t0, _p0 = tile_rows(t)
                for i, (m, w) in enumerate(((sh.xh, w_hi), (sh.xl, w_hi), (sh.xh, w_lo))):
                    last = eng.matmul(sh.ps[:, 2 * (t % 2) + half, :], m[:, k, t0:t0 + 128],
                                      w[k][:, 512 * half:512 * half + 512],
                                      start=(k == 0 and i == 0), stop=(k == KC - 1 and i == 2))
                return last

            eng.wait_ge(c_in, 64)
            eng.wait_ge(m_tail, 1)
            for k in range(KC):
                eng.wait_ge(w_tail, k + 1)
                for half in range(2):
                    last = mix(0, half, k)
            last.then_inc(mix_mm, 1)
            for t in range(1, NT + 2):
                for half in range(2):
                    if t < NT:
                        if half == 0:
                            eng.wait_ge(m_tail, t + 1)
                            if t >= 2:
                                eng.wait_ge(r_ready, t - 1)
                        for k in range(KC):
                            last = mix(t, half, k)
                        if half == 1:
                            last.then_inc(mix_mm, 1)
                    if t >= 2:
                        transpose_x1(t - 2) if half == 0 else router(t - 2)

        @block.scalar
        def _(eng):
            def m_heads(t):
                at = slice(128 * t, min(128 * t + 128, TOK))
                eng.activation(sh.xh[:, :, at], sh.m[:, :, at], ACT.Copy).then_inc(m_head, 1)

            m_heads(0)
            for k in range(KC):
                eng.wait_ge(w_in[k % 2], 16 * (k // 2 + 1))
                eng.activation(w_hi[k], w_raw[:, k % 2, :], ACT.Copy).then_inc(w_head, 1)
            m_heads(1)
            for t in range(NT + 2):
                if t >= 2:
                    for half in range(2):
                        eng.wait_ge(x1_tr, 2 * (t - 2) + half + 1)
                        if t >= 3 and half == 0:
                            eng.wait_ge(lg_mm, t - 2)
                        eng.activation(x1T[:, 4 * half:4 * half + 4, :],
                                       sh.ps[:, 4 + half, :].rearrange("p (k n) -> p k n", k=4), ACT.Copy).then_inc(x1T_out, 1)
                if t < NT:
                    eng.wait_ge(var_ready, t + 1)
                    eng.activation(std[:, :], mv[:, 1:2], ACT.Sqrt).then_inc(std_ready, 1)
                if t + 2 < NT:
                    m_heads(t + 2)

        @block.vector
        def _(eng):
            def m_tails(t):
                at = slice(128 * t, min(128 * t + 128, TOK))
                eng.wait_ge(m_head, t + 1)
                eng.tensor_tensor(sh.xl[:, :, at], sh.m[:, :, at], f32(sh.xh[:, :, at]), ALU.subtract).then_inc(m_tail, 1)

            m_tails(0)
            for k in range(KC):
                eng.wait_ge(w_head, k + 1)
                eng.tensor_tensor(w_lo[k], w_raw[:, k % 2, :], f32(w_hi[k]), ALU.subtract).then_inc(w_tail, 1)
            m_tails(1)
            eng.wait_ge(c_in, 64)
            ch = Chain(eng, dve_s)
            for t in range(NT + 3):
                if t < NT:
                    eng.wait_ge(mix_mm, t + 1)
                    eng.wait_ge(x_in[t % 2], 16 * (t // 2 + 1) if t < 8 else 16 * 6)
                    eng.scalar_tensor_tensor(out=r[:, :], in0=x[:, t % 2, :], scalar=ALPHA,
                                             in1=sh.ps[:, 2 * (t % 2):2 * (t % 2) + 2, :].rearrange("p a n -> p (a n)"),
                                             op0=ALU.mult, op1=ALU.add).then_inc(r_ready, 1)
                    eng.wait_ge(r_ready, t + 1)
                    for half in range(2):
                        ch(eng.bn_stats(st[:, half, :], r[:, 512 * half:512 * half + 512]))
                    ch(eng.bn_aggr(mv[:, :], st[:, :, :].rearrange("p a n -> p (a n)")))
                    eng.tensor_scalar(mv[:, 1:2], mv[:, 1:2], EPS, None, ALU.add).then_inc(var_ready, 1)
                if t >= 3:
                    eng.wait_ge(lg_mm, t - 2)
                    eng.tensor_tensor(sh.lg[:, t - 3, :], sh.ps[:, 6 + (t - 3) % 2, 0:NE], brb[:, :], ALU.add).then_inc(lg_out, 1)
                if t < NT:
                    eng.wait_ge(std_ready, t + 1)
                    ch(eng.reciprocal(rstd[:, :], std[:, :]))
                    ch(eng.tensor_scalar(r[:, :], r[:, :], mv[:, 0:1], rstd[:, :], ALU.subtract, ALU.mult))
                    ch(eng.tensor_tensor(r[:, :], r[:, :], gb[:, :], ALU.mult))
                    if t >= 3:
                        eng.wait_ge(stored[t % 3], 16 * (t // 3))
                        eng.wait_ge(x1_tr, 2 * (t - 2))
                    eng.tensor_tensor(x1[:, t % 3, :], r[:, :], bb[:, :], ALU.add).then_inc(x1_ready, 1)
                    eng.wait_ge(x1_ready, t + 1)
                    if t + 2 < NT:
                        m_tails(t + 2)


TILE = 256
NTILE = (2 * TOK - NE) // TILE + NE
NSLOT = NTILE * TILE
NB = NSLOT // 128


def wait_count(eng, sem, value):
    if not isinstance(value, int) or value > 0:
        eng.wait_ge(sem, value)


def expert_buffers(nc, sh, ctx):
    def sb(name, shape, dt=F32):
        return ctx.enter_context(nc.sbuf_tensor("ex_" + name, shape, dt))
    sh.e_raw = [sb(f"raw{m}", [128, 2048]) for m in "gud"]
    sh.e_hi = [sb(f"hi{m}", [128, 2, 2048], F32R) for m in "gud"]
    sh.e_lo = [sb(f"lo{m}", [128, 2, 2048], F32R) for m in "gud"]
    sh.e_in, sh.e_head, sh.e_tail = ([ctx.enter_context(nc.semaphore(f"ex_{n}{m}")) for m in "gud"]
                                     for n in ("in", "head", "tail"))


def load_expert(sh, eng, i):
    ex = eng.value_load(sh.eid[0:1, bass.ds(i, 1)], min_val=0, max_val=NE - 1)
    for m, w in enumerate((sh.w_e_gate, sh.w_e_up, sh.w_e_down)):
        wait_count(eng, sh.e_tail[m], i)
        k = w.shape[2] // 128
        eng.dma_start(sh.e_raw[m][:, :].rearrange("p (k n) -> p k n", k=k),
                      w[0, bass.ds(ex, 1)].rearrange("o (k p) n -> p (o k) n", p=128)).then_inc(sh.e_in[m], 16)


def head_expert(sh, eng, i, r, m):
    eng.wait_ge(sh.e_in[m], 16 * i + 16)
    eng.activation(sh.e_hi[m][:, r, :], sh.e_raw[m][:, :], ACT.Copy).then_inc(sh.e_head[m], 1)


def tail_expert(sh, eng, i, r, m):
    eng.wait_ge(sh.e_head[m], i + 1)
    eng.tensor_tensor(sh.e_lo[m][:, r, :], sh.e_raw[m][:, :], f32(sh.e_hi[m][:, r, :]),
                      ALU.subtract).then_inc(sh.e_tail[m], 1)


def stage_route(nc, sh):
    with ExitStack() as ctx:
        def sb(name, shape, dt=F32):
            return ctx.enter_context(nc.sbuf_tensor("rt_" + name, shape, dt))

        def sem(name):
            return ctx.enter_context(nc.semaphore("rt_" + name))
        N4 = NT * NG
        e, p, pm, eq, oh1, oh2, ohc, rank, slot = (sb(n, [128, NT, NE]) for n in (
            "e", "p", "pm", "eq", "oh1", "oh2", "ohc", "rank", "slot"))
        s6, gs, geq, gsel = sb("s6", [128, N4, 6]), sb("gs", [128, NT, NG]), sb("geq", [128, NT, NG]), sb("gsel", [128, NT, NG])
        a, b, v1, v2 = (sb(n, [128, NT]) for n in ("a", "b", "v1", "v2"))
        desc = sb("desc", [128, NE])
        cnt, nt, incl, off, one16 = (sb(n, [128, NE]) for n in ("cnt", "nt", "incl", "off", "one16"))
        tot = sb("tot", [128, NT, NE])
        before_, ones = sb("before", [128, 128]), sb("ones", [128, 128])
        sloti, blk, pos = (sb(n, [128, 2, NT], I32) for n in ("sloti", "blk", "pos"))
        addr = sb("addr", [128, 2, NT], U32)
        dummy = sb("dummy", [64, 2], I32)
        tokid = sb("tokid", [128, NT], U32)
        tokf = sb("tokf", [128, NT], I32)
        zeros = sb("zeros", [128, NB + 1], U32)
        ti = sb("ti", [1, NTILE])
        eid_ready = sem("eid_ready")
        tcmp, tsum = sb("tcmp", [1, NTILE, NE]), sb("tsum", [1, NTILE])
        (pool_s, dve_s, act_s, exp_in, oh_ready, r_mm, a_ready, cleared, scattered, idx_in) = (sem(n) for n in (
            "pool", "dve", "act", "exp_in", "oh_ready", "r_mm", "a_ready", "cleared", "scattered", "idx_in"))
        block = ctx.enter_context(nc.Block())

        @block.gpsimd
        def _(eng):
            ch = Chain(eng, pool_s)
            ch(eng.memset(zeros[:, :], 0))
            eng.dma_start(sh.slot_tok[0:128 * (NB + 1), :].rearrange("(p b) o -> p (b o)", p=128), zeros[:, :]
                          ).then_inc(cleared, 16)
            ch(eng.iota(desc[:, :], pattern=[[-1, NE]], base=NE, channel_multiplier=0,
                        allow_small_or_imprecise_dtypes=True))
            ch(eng.iota(ti[:, :], pattern=[[1, NTILE]], base=0, channel_multiplier=0,
                        allow_small_or_imprecise_dtypes=True))
            ch(eng.memset(ones[:, :], 1.0))
            ch(eng.memset(one16[:, :], 1.0))
            ch(eng.memset(before_[:, :], 1.0))
            ch(eng.affine_select(out=before_[:, :], in_=before_[:, :], compare_op=ALU.is_gt, fill=0.0, base=0,
                                 pattern=[[1, 128]], channel_multiplier=-1))
            ch(eng.iota(tokf[:, 0:8], pattern=[[128, 8]], base=0, channel_multiplier=1))
            ch(eng.iota(tokf[:, 8:9], pattern=[[0, 1]], base=TOK - 128, channel_multiplier=1))
            ch(eng.tensor_copy(tokid[:, :], tokf[:, :]))
            ch(eng.iota(dummy[:, :], pattern=[[64, 2]], base=NSLOT, channel_multiplier=1))
            eng.wait_ge(a_ready, 1)
            eng.wait_ge(cleared, 16)
            for c in range(2):
                for t in range(NT):
                    eng.indirect_dma_start(out=sh.slot_tok[:, :],
                                           out_offset=bass.IndirectOffsetOnAxis(ap=addr[:, c, t:t + 1], axis=0),
                                           in_=tokid[:, t:t + 1], in_offset=None).then_inc(scattered, 16)
            eng.wait_ge(scattered, 16 * 2 * NT)
            eng.dma_start(sh.slot_idx[:, :], sh.slot_tok[0:NSLOT, :].rearrange("(p b) o -> p (b o)", p=128)
                          ).then_inc(idx_in, 16)
            eng.wait_ge(idx_in, 16)
        POOL_DONE = 11

        @block.scalar
        def _(eng):
            eng.wait_ge(exp_in, 1)
            eng.activation(e[:, :, :], e[:, :, :], ACT.Exp).then_inc(act_s, 1)
            for i in range(2):
                for m in range(3):
                    head_expert(sh, eng, i, i, m)

        @block.sync
        def _(eng):
            eng.wait_ge(eid_ready, 1)
            for i in range(2):
                load_expert(sh, eng, i)

        @block.tensor
        def _(eng):
            eng.wait_ge(pool_s, POOL_DONE)
            eng.wait_ge(oh_ready, 1)
            rhs = ohc[:, :, :].rearrange("p t e -> p (t e)")
            eng.matmul(sh.ps[:, 0, 0:NT * NE], before_[:, :], rhs, start=True, stop=True)
            eng.matmul(sh.ps[:, 1, 0:NT * NE], ones[:, :], rhs, start=True, stop=True).then_inc(r_mm, 1)

        @block.vector
        def _(eng):
            ch = Chain(eng, dve_s)
            tt, ts = eng.tensor_tensor, eng.tensor_scalar

            def wide(ap, n=NE):
                return ap.unsqueeze(2).broadcast_to([128, ap.shape[1], n])

            def first_max(value, best, out, k):
                ch(eng.reduce_max(best, value, axis=X))
                ch(tt(out, value, wide(best, k), ALU.is_equal))
                ch(tt(out, out, desc[:, NE - k:].unsqueeze(1).broadcast_to([128, NT, k]), ALU.mult))
                ch(eng.reduce_max(b[:, :], out, axis=X))
                ch(tt(out, out, wide(b[:, :], k), ALU.is_equal))

            eng.wait_ge(pool_s, POOL_DONE)
            ch(eng.reduce_max(a[:, :], sh.lg[:, :, :], axis=X))
            tt(e[:, :, :], sh.lg[:, :, :], wide(a[:, :]), ALU.subtract).then_inc(exp_in, 1)
            eng.wait_ge(act_s, 1)
            ch(eng.reduce_sum(a[:, :], e[:, :, :], axis=X))
            ch(eng.reciprocal(a[:, :], a[:, :]))
            ch(tt(p[:, :, :], e[:, :, :], wide(a[:, :]), ALU.mult))
            pg = p[:, :, :].rearrange("p t (g n) -> p (t g) n", g=NG)
            at = 0
            for d in (1, 2, 3):
                ch(tt(s6[:, :, at:at + 4 - d], pg[:, :, 0:4 - d], pg[:, :, d:4], ALU.add))
                at += 4 - d
            ch(eng.reduce_max(gs[:, :, :].rearrange("p t g -> p (t g)"), s6[:, :, :], axis=X))
            first_max(gs[:, :, :], a[:, :], gsel[:, :, :], NG)
            ch(ts(geq[:, :, :], gsel[:, :, :], -1.0, None, ALU.add))
            g4 = lambda ap: ap.rearrange("p t g -> p (t g)").unsqueeze(2).broadcast_to([128, N4, EPG])
            pmg = pm[:, :, :].rearrange("p t (g n) -> p (t g) n", g=NG)
            ch(tt(pmg, pg, g4(gsel[:, :, :]), ALU.mult))
            ch(tt(pmg, pmg, g4(geq[:, :, :]), ALU.add))
            first_max(pm[:, :, :], v1[:, :], oh1[:, :, :], NE)
            ch(eng.scalar_tensor_tensor(out=pm[:, :, :], in0=oh1[:, :, :], scalar=-4.0, in1=pm[:, :, :],
                                        op0=ALU.mult, op1=ALU.add))
            first_max(pm[:, :, :], v2[:, :], oh2[:, :, :], NE)
            ch(tt(a[:, :], v1[:, :], v2[:, :], ALU.add))
            ch(eng.reciprocal(a[:, :], a[:, :]))
            ch(tt(sh.wt[:, 0, :], v1[:, :], a[:, :], ALU.mult))
            ch(tt(sh.wt[:, 1, :], v2[:, :], a[:, :], ALU.mult))
            ch(tt(ohc[:, :, :], oh1[:, :, :], oh2[:, :, :], ALU.add))
            eng.memset(ohc[0:64, NT - 1, :], 0.0).then_inc(oh_ready, 1)
            eng.wait_ge(r_mm, 1)
            ch(eng.tensor_copy(rank[:, :, :], sh.ps[:, 0, 0:NT * NE].rearrange("p (t e) -> p t e", t=NT)))
            ch(eng.tensor_copy(tot[:, :, :], sh.ps[:, 1, 0:NT * NE].rearrange("p (t e) -> p t e", t=NT)))
            ch(eng.tensor_copy(cnt[:, :], tot[:, 0, :]))
            for t in range(1, NT):
                ch(tt(rank[:, t, :], rank[:, t, :], cnt[:, :], ALU.add))
                ch(tt(cnt[:, :], cnt[:, :], tot[:, t, :], ALU.add))
            ch(ts(nt[:, :], cnt[:, :], 0.0, None, ALU.is_gt))
            for k in range(1, -(-TOK // TILE)):
                ch(eng.scalar_tensor_tensor(out=nt[:, :], in0=cnt[:, :], scalar=float(TILE * k), in1=nt[:, :],
                                            op0=ALU.is_gt, op1=ALU.add))
            ch(eng.tensor_tensor_scan(incl[:, :], one16[:, :], nt[:, :], 0.0, ALU.mult, ALU.add))
            ch(tt(off[:, :], incl[:, :], nt[:, :], ALU.subtract))
            ch(ts(off[:, :], off[:, :], float(TILE), None, ALU.mult))
            ch(tt(rank[:, :, :], rank[:, :, :], off[:, :].unsqueeze(1).broadcast_to([128, NT, NE]), ALU.add))
            for c, oh in enumerate((oh1, oh2)):
                ch(tt(slot[:, :, :], rank[:, :, :], oh[:, :, :], ALU.mult))
                ch(eng.reduce_sum(a[:, :], slot[:, :, :], axis=X))
                ch(eng.memset(a[0:64, NT - 1:NT], 0.0))
                ch(eng.tensor_copy(sloti[:, c, :], a[:, :]))
            ch(eng.tensor_copy(sh.slots[:, :, :], sloti[:, :, :]))
            ch(ts(blk[:, :, :], sloti[:, :, :], 7, None, ALU.arith_shift_right))
            ch(ts(pos[:, :, :], sloti[:, :, :], 127, None, ALU.bitwise_and))
            ch(eng.scalar_tensor_tensor(out=pos[:, :, :], in0=pos[:, :, :], scalar=float(NB), in1=blk[:, :, :],
                                        op0=ALU.mult, op1=ALU.add))
            ch(eng.tensor_copy(pos[0:64, :, NT - 1], dummy[:, :]))
            eng.tensor_copy(addr[:, :, :], pos[:, :, :]).then_inc(a_ready, 1)
            ch(tt(tcmp[:, :, :], incl[0:1, :].unsqueeze(1).broadcast_to([1, NTILE, NE]),
                  ti[:, :].unsqueeze(2).broadcast_to([1, NTILE, NE]), ALU.is_le))
            ch(eng.reduce_sum(tsum[:, :], tcmp[:, :, :], axis=X))
            ch(ts(tsum[:, :], tsum[:, :], float(NE - 1), None, ALU.min))
            eng.tensor_copy(sh.eid[:, :], tsum[:, :]).then_inc(eid_ready, 1)
            for i in range(2):
                for m in range(3):
                    tail_expert(sh, eng, i, i, m)


def stage_moe(nc, sh):
    with ExitStack() as ctx:
        def sb(name, shape, dt=F32):
            return ctx.enter_context(nc.sbuf_tensor("mo_" + name, shape, dt))

        def sem(name):
            return ctx.enter_context(nc.semaphore("mo_" + name))
        hi, lo, w_tail = sh.e_hi, sh.e_lo, sh.e_tail
        idx = sb("idx", [128, 2, 2], U32)
        probe = sb("probe", [128, 2])
        xg = sb("xg", [128, 2, 2, D])
        xh, xl = sb("xh", [128, 2, KC, TILE], F32R), sb("xl", [128, 2, KC, TILE], F32R)
        sg, t_, h = (sb(n, [128, 2 * TILE]) for n in ("sg", "t", "h"))
        hh, hl = sb("hh", [128, 2, 2, TILE], F32R), sb("hl", [128, 2, 2, TILE], F32R)
        y = sb("y", [128, 2, D])
        (idx_ready, x_in0, x_in1, x_tr, x_head, x_tail, g_mm, u_mm, sg_ready, t_ready, h_ready, hh_ready, hl_ready, y_mm,
         y_out, y_st0, y_st1) = (sem(n) for n in (
             "idx_ready", "x_in0", "x_in1", "x_tr", "x_head", "x_tail", "g_mm", "u_mm", "sg_ready", "t_ready", "h_ready",
             "hh_ready", "hl_ready", "y_mm", "y_out", "y_st0", "y_st1"))
        x_in, y_st = [x_in0, x_in1], [y_st0, y_st1]
        y_rows = sh.y_dram.rearrange("(i j p) n -> i j p n", j=2, p=128)
        LAST = NTILE // 2 - 1
        block = ctx.enter_context(nc.Block())

        wait = wait_count
        @block.sync
        def _(eng):
            def body(i, r, more):
                if more:
                    load_expert(sh, eng, i + 2)
                for j in range(2):
                    eng.wait_ge(y_out, 4 * i + 2 * j + 2)
                    eng.dma_start(y_rows[bass.ds(i, 1), j].rearrange("o p n -> (o p) n"), y[:, j, :]).then_inc(y_st[j], 16)
            for r in range(2):
                eng.wait_ge(x_in[r], 32)
            body(0, 0, True)
            body(1, 1, True)
            with eng.Fori(1, LAST) as q:
                body(2 * q, 0, True)
                body(2 * q + 1, 1, True)
            body(NTILE - 2, 0, False)
            body(NTILE - 1, 1, False)
            for j in range(2):
                eng.wait_ge(y_st[j], 16 * NTILE)

        @block.gpsimd
        def _(eng):
            def gather(i, r, tiles_done):
                if tiles_done is not None:
                    eng.wait_ge(x_tr, tiles_done)
                eng.tensor_copy(idx[:, r, :], sh.slot_idx[:, bass.ds(2 * i, 2)]).then_inc(idx_ready, 1)
                eng.wait_ge(idx_ready, i + 1)
                eng.tensor_tensor(probe[:, 1:2], probe[:, 0:1], probe[:, 0:1], ALU.add)
                for j in range(2):
                    eng.indirect_dma_start(out=xg[:, r, j, :], out_offset=None, in_=sh.x1_dram[:, :],
                                           in_offset=bass.IndirectOffsetOnAxis(ap=idx[:, r, j:j + 1], axis=0)
                                           ).then_inc(x_in[r], 16)
            eng.memset(probe[:, :], 0.0)
            gather(0, 0, None)
            gather(1, 1, None)
            with eng.Fori(0, LAST) as q:
                for r in range(2):
                    i = 2 * q + r
                    gather(i + 2, r, 4 * i + 4)

        @block.tensor
        def _(eng):
            def transpose(i, r, pair, quarters, first=False):
                if quarters[0] == 0:
                    eng.wait_ge(x_in[r], 32 * pair + 32)
                for q in quarters:
                    if not (first and q < 2):
                        eng.wait_ge(x_tail, 4 * i + q - 1)
                    for k in range(2):
                        for j in range(2):
                            c0 = 128 * (2 * q + k)
                            last = eng.transpose(sh.ps[:, q % 2, TILE * k + 128 * j:TILE * k + 128 * j + 128],
                                                 xg[:, r, j, c0:c0 + 128], sh.ident[:, :])
                    last.then_inc(x_tr, 1)

            def in_product(i, r, m, done):
                eng.wait_ge(w_tail[m], i + 1)
                if m == 0:
                    eng.wait_ge(x_tail, 4 * i + 4)
                    wait(eng, h_ready, i - 1)
                for f in range(2):
                    out = sh.ps[:, 2 + 2 * r + m, TILE * f:TILE * f + TILE]
                    for k in range(KC):
                        w0 = DE * k + 128 * f
                        for a, (w, x) in enumerate(((hi, xh), (hi, xl), (lo, xh))):
                            last = eng.matmul(out, w[m][:, r, w0:w0 + 128], x[:, r, k, :],
                                              start=(k == 0 and a == 0), stop=(k == KC - 1 and a == 2),
                                              skip_group_check=True)
                last.then_inc(done, 1)

            def down(i, r):
                eng.wait_ge(hl_ready, i + 1)
                eng.wait_ge(w_tail[2], i + 1)
                for j in range(2):
                    for half in range(2):
                        u = 2 * j + half
                        wait(eng, y_out, 4 * i + (u - 1 if u >= 2 else 0))
                        for f in range(2):
                            w0 = D * f + 512 * half
                            for a, (hx, w) in enumerate(((hh, hi), (hl, hi), (hh, lo))):
                                last = eng.matmul(sh.ps[:, 6 + half, :], hx[:, r, f, 128 * j:128 * j + 128],
                                                  w[2][:, r, w0:w0 + 512],
                                                  start=(f == 0 and a == 0), stop=(f == 1 and a == 2))
                        last.then_inc(y_mm, 1)

            def body(i, r, pair, more, most):
                if most:
                    transpose(i + 2, r, pair + 1, (0, 1))
                if more:
                    in_product(i + 1, 1 - r, 0, g_mm)
                if most:
                    transpose(i + 2, r, pair + 1, (2, 3))
                if more:
                    in_product(i + 1, 1 - r, 1, u_mm)
                down(i, r)

            transpose(0, 0, 0, (0, 1, 2, 3), True)
            transpose(1, 1, 0, (0, 1))
            in_product(0, 0, 0, g_mm)
            transpose(1, 1, 0, (2, 3))
            in_product(0, 0, 1, u_mm)
            body(0, 0, 0, True, True)
            body(1, 1, 0, True, True)
            with eng.Fori(1, LAST) as q:
                body(2 * q, 0, q, True, True)
                body(2 * q + 1, 1, q, True, True)
            body(NTILE - 2, 0, LAST, True, False)
            body(NTILE - 1, 1, LAST, False, False)

        @block.scalar
        def _(eng):
            def head(i, r, m):
                head_expert(sh, eng, i, r, m)

            def x_heads(i, r, quarters):
                for q in quarters:
                    eng.wait_ge(x_tr, 4 * i + q + 1)
                    eng.activation(xh[:, r, 2 * q:2 * q + 2, :],
                                   sh.ps[:, q % 2, :].rearrange("p (k n) -> p k n", k=2), ACT.Copy).then_inc(x_head, 1)

            def sigmoid(i, r):
                eng.wait_ge(g_mm, i + 1)
                wait(eng, t_ready, i)
                eng.activation(sg[:, :], sh.ps[:, 2 + 2 * r, :], ACT.Sigmoid).then_inc(sg_ready, 1)

            def h_head(i, r):
                eng.wait_ge(h_ready, i + 1)
                eng.activation(hh[:, r].rearrange("p f n -> p (f n)"), h[:, :], ACT.Copy).then_inc(hh_ready, 1)

            def body(i, r, more, most):
                if most:
                    x_heads(i + 2, r, (0, 1))
                    eng.wait_ge(g_mm, i + 1)
                    head(i + 2, r, 0)
                if more:
                    sigmoid(i + 1, 1 - r)
                if most:
                    x_heads(i + 2, r, (2, 3))
                if more:
                    wait(eng, y_mm, 4 * i)
                    h_head(i + 1, 1 - r)
                for u in range(4):
                    if most and u == 2:
                        eng.wait_ge(u_mm, i + 1)
                        head(i + 2, r, 1)
                    j, half = divmod(u, 2)
                    eng.wait_ge(y_mm, 4 * i + u + 1)
                    if half == 0:
                        wait(eng, y_st[j], 16 * i)
                    eng.activation(y[:, j, 512 * half:512 * half + 512], sh.ps[:, 6 + half, :], ACT.Copy).then_inc(y_out, 1)
                if most:
                    head(i + 2, r, 2)

            for i in range(2):
                x_heads(i, i, (0, 1, 2, 3))
            sigmoid(0, 0)
            h_head(0, 0)
            body(0, 0, True, True)
            body(1, 1, True, True)
            with eng.Fori(1, LAST) as q:
                body(2 * q, 0, True, True)
                body(2 * q + 1, 1, True, True)
            body(NTILE - 2, 0, True, False)
            body(NTILE - 1, 1, False, False)

        @block.vector
        def _(eng):
            def tail(i, r, m):
                tail_expert(sh, eng, i, r, m)

            def x_tails(i, r, quarters):
                for q in quarters:
                    eng.wait_ge(x_head, 4 * i + q + 1)
                    eng.tensor_tensor(xl[:, r, 2 * q:2 * q + 2, :], sh.ps[:, q % 2, :].rearrange("p (k n) -> p k n", k=2),
                                      f32(xh[:, r, 2 * q:2 * q + 2, :]), ALU.subtract).then_inc(x_tail, 1)

            def gate(i, r):
                eng.wait_ge(sg_ready, i + 1)
                wait(eng, h_ready, i)
                eng.tensor_tensor(t_[:, :], sh.ps[:, 2 + 2 * r, :], sg[:, :], ALU.mult).then_inc(t_ready, 1)

            def hidden(i, r):
                eng.wait_ge(u_mm, i + 1)
                eng.wait_ge(t_ready, i + 1)
                wait(eng, hl_ready, i)
                eng.tensor_tensor(h[:, :], sh.ps[:, 3 + 2 * r, :], t_[:, :], ALU.mult).then_inc(h_ready, 1)
                eng.wait_ge(hh_ready, i + 1)
                eng.tensor_tensor(hl[:, r].rearrange("p f n -> p (f n)"), h[:, :],
                                  f32(hh[:, r]).rearrange("p f n -> p (f n)"), ALU.subtract).then_inc(hl_ready, 1)

            def body(i, r, more, most):
                if most:
                    x_tails(i + 2, r, (0, 1))
                    tail(i + 2, r, 0)
                if more:
                    gate(i + 1, 1 - r)
                if most:
                    x_tails(i + 2, r, (2, 3))
                if more:
                    hidden(i + 1, 1 - r)
                if most:
                    tail(i + 2, r, 1)
                    tail(i + 2, r, 2)

            for i in range(2):
                x_tails(i, i, (0, 1, 2, 3))
            gate(0, 0)
            hidden(0, 0)
            body(0, 0, True, True)
            body(1, 1, True, True)
            with eng.Fori(1, LAST) as q:
                body(2 * q, 0, True, True)
                body(2 * q + 1, 1, True, True)
            body(NTILE - 2, 0, True, False)


def stage_combine(nc, sh):
    with ExitStack() as ctx:
        def sb(name, shape, dt=F32):
            return ctx.enter_context(nc.sbuf_tensor("co_" + name, shape, dt))

        def sem(name):
            return ctx.enter_context(nc.semaphore("co_" + name))
        RB = 5
        x1, y1, y2, a, r, o = (sb(n, [128, RB, D]) for n in ("x1", "y1", "y2", "a", "r", "o"))
        gb, bb = sb("gb", [128, D]), sb("bb", [128, D])
        st, mv = sb("st", [128, RB, 2, 6]), sb("mv", [128, RB, 2])
        std, rstd, nmr = sb("std", [128, RB]), sb("rstd", [128, RB]), sb("nmr", [128, RB])
        (c_in, a_ready, dve_s, var_ready, std_ready, rstd_ready, n_ready, g_ready, o_ready, r_ready) = (sem(n) for n in (
            "c_in", "a_ready", "dve", "var_ready", "std_ready", "rstd_ready", "n_ready", "g_ready", "o_ready", "r_ready"))
        t_in = [sem(f"t_in{i}") for i in range(RB)]
        x_in = [sem(f"x_in{i}") for i in range(RB)]
        stored = [sem(f"stored{i}") for i in range(RB)]
        block = ctx.enter_context(nc.Block())

        @block.sync
        def _(eng):
            for t in range(NT + 3):
                if t < NT:
                    if t >= RB:
                        eng.wait_ge(r_ready, t - RB + 1)
                    eng.dma_start(x1[:, t % RB, :], sh.x1_dram[tile_rows(t)[0]:tile_rows(t)[0] + 128, :]).then_inc(x_in[t % RB], 16)
                if t == 0:
                    for dst, src in ((gb, sh.ln2_g), (bb, sh.ln2_b)):
                        eng.dma_start(dst[:, :], src.broadcast_to([128, D])).then_inc(c_in, 16)
                u = t - 3
                if u >= 0:
                    eng.wait_ge(o_ready, u + 1)
                    if u < 8:
                        eng.dma_start(sh.y_prompt[0, 128 * u:128 * u + 128, :], o[:, u % RB, :]).then_inc(stored[u % RB], 16)
                    else:
                        eng.dma_start(sh.y_sample.rearrange("b t d -> (b t) d"), o[64:128, u % RB, :]).then_inc(stored[u % RB], 16)
            for i in range(RB):
                eng.wait_ge(stored[i], 16 * len(range(i, NT, RB)))

        @block.gpsimd
        def _(eng):
            def fetch(t):
                if t >= RB:
                    eng.wait_ge(r_ready, t - RB + 1)
                for c, dst in enumerate((y1, y2)):
                    eng.indirect_dma_start(out=dst[:, t % RB, :], out_offset=None, in_=sh.y_dram[:, :],
                                           in_offset=bass.IndirectOffsetOnAxis(ap=sh.slots[:, c, t:t + 1], axis=0)
                                           ).then_inc(t_in[t % RB], 16)
            for t in range(RB):
                fetch(t)
            eng.wait_ge(c_in, 32)
            for t in range(NT):
                if t + RB < NT:
                    fetch(t + RB)
                eng.wait_ge(g_ready, t + 1)
                if t >= RB:
                    eng.wait_ge(stored[t % RB], 16 * (t // RB))
                eng.tensor_tensor(o[:, t % RB, :], r[:, t % RB, :], bb[:, :], ALU.add).then_inc(o_ready, 1)

        @block.scalar
        def _(eng):
            def weigh_first(t):
                b = t % RB
                eng.wait_ge(t_in[b], 32 * (t // RB + 1))
                if t >= RB:
                    eng.wait_ge(r_ready, t - RB + 1)
                eng.activation(a[:, b, :], y1[:, b, :], ACT.Copy, scale=sh.wt[:, 0, t:t + 1]).then_inc(a_ready, 1)

            weigh_first(0)
            weigh_first(1)
            for t in range(NT):
                b = t % RB
                if t + 2 < NT:
                    weigh_first(t + 2)
                eng.wait_ge(var_ready, t + 1)
                eng.activation(std[:, b:b + 1], mv[:, b, 1:2], ACT.Sqrt).then_inc(std_ready, 1)
                eng.wait_ge(rstd_ready, t + 1)
                eng.activation(r[:, b, :], r[:, b, :], ACT.Identity, scale=rstd[:, b:b + 1],
                               bias=nmr[:, b:b + 1]).then_inc(n_ready, 1)

        @block.vector
        def _(eng):
            ch = Chain(eng, dve_s)

            def add_up(t):
                b = t % RB
                eng.wait_ge(a_ready, t + 1)
                eng.wait_ge(x_in[b], 16 * (t // RB + 1))
                ch(eng.scalar_tensor_tensor(out=a[:, b, :], in0=y2[:, b, :], scalar=sh.wt[:, 1, t:t + 1], in1=a[:, b, :],
                                            op0=ALU.mult, op1=ALU.add))
                if t >= RB:
                    eng.wait_ge(o_ready, t - RB + 1)
                eng.scalar_tensor_tensor(out=r[:, b, :], in0=x1[:, b, :], scalar=ALPHA, in1=a[:, b, :],
                                         op0=ALU.mult, op1=ALU.add).then_inc(r_ready, 1)
                eng.wait_ge(r_ready, t + 1)
                for half in range(2):
                    ch(eng.bn_stats(st[:, b, half, :], r[:, b, 512 * half:512 * half + 512]))
                ch(eng.bn_aggr(mv[:, b, :], st[:, b, :, :].rearrange("p a n -> p (a n)")))
                eng.tensor_scalar(mv[:, b, 1:2], mv[:, b, 1:2], EPS, None, ALU.add).then_inc(var_ready, 1)

            def scales(t):
                b = t % RB
                eng.wait_ge(std_ready, t + 1)
                ch(eng.reciprocal(rstd[:, b:b + 1], std[:, b:b + 1]))
                eng.scalar_tensor_tensor(out=nmr[:, b:b + 1], in0=mv[:, b, 0:1], scalar=-1.0, in1=rstd[:, b:b + 1],
                                         op0=ALU.mult, op1=ALU.mult).then_inc(rstd_ready, 1)

            def gain(t):
                b = t % RB
                eng.wait_ge(n_ready, t + 1)
                eng.tensor_tensor(r[:, b, :], r[:, b, :], gb[:, :], ALU.mult).then_inc(g_ready, 1)

            eng.wait_ge(c_in, 32)
            for t in range(NT + 2):
                if t < NT:
                    add_up(t)
                if 1 <= t <= NT:
                    scales(t - 1)
                if t >= 2:
                    gain(t - 2)




def build(nc, ins, outs, upto=99):
    sh = Shared()
    sh.x_prompt = ins["x_prompt"]
    sh.x_sample = ins["x_sample"]
    sh.cache_fox_k = ins["cache_fox_k"]
    sh.cache_fox_v = ins["cache_fox_v"]
    sh.cache_fox_logf = ins["cache_fox_logf"]
    sh.state_gla = ins["state_gla"]
    sh.state_conv = ins["state_conv"]
    sh.page_table = ins["page_table"]
    sh.w_in = ins["w_in"]
    sh.w_gla_a2 = ins["w_gla_a2"]
    sh.b_gla_a = ins["b_gla_a"]
    sh.gla_norm_g = ins["gla_norm_g"]
    sh.b_fox_f = ins["b_fox_f"]
    sh.conv_w = ins["conv_w"]
    sh.w_branch = ins["w_branch"]
    sh.w_out = ins["w_out"]
    sh.ln1_g = ins["ln1_g"]
    sh.ln1_b = ins["ln1_b"]
    sh.w_router = ins["w_router"]
    sh.b_router = ins["b_router"]
    sh.w_e_gate = ins["w_e_gate"]
    sh.w_e_up = ins["w_e_up"]
    sh.w_e_down = ins["w_e_down"]
    sh.ln2_g = ins["ln2_g"]
    sh.ln2_b = ins["ln2_b"]
    sh.y_prompt = outs["y_prompt"]
    sh.y_sample = outs["y_sample"]
    sh.prompt_fox_k = outs["prompt_fox_k"]
    sh.prompt_fox_v = outs["prompt_fox_v"]
    sh.prompt_fox_logf = outs["prompt_fox_logf"]
    sh.prompt_gla = outs["prompt_gla"]
    sh.prompt_conv = outs["prompt_conv"]
    sh.sample_fox_k = outs["sample_fox_k"]
    sh.sample_fox_v = outs["sample_fox_v"]
    sh.sample_fox_logf = outs["sample_fox_logf"]
    sh.sample_gla = outs["sample_gla"]
    sh.sample_conv = outs["sample_conv"]
    sh.oT_hi = nc.dram_tensor("oT_hi", [3, BW, TOK], F32, kind="Internal").ap()
    sh.oT_lo = nc.dram_tensor("oT_lo", [3, BW, TOK], F32, kind="Internal").ap()
    sh.slot_tok = nc.dram_tensor("slot_tok", [NSLOT + 128, 1], U32, kind="Internal").ap()
    sh.y_dram = nc.dram_tensor("y_dram", [NSLOT, D], F32, kind="Internal").ap()
    sh.x1_dram = nc.dram_tensor("x1_dram", [TOK, D], F32, kind="Internal").ap()
    sh.c_dram = nc.dram_tensor("c_dram", [4, H_FOX, TOK], F32, kind="Internal").ap()
    with ExitStack() as ctx:
        def sb(name, shape, dt=F32):
            return ctx.enter_context(nc.sbuf_tensor(name, shape, dt))

        sems, used = ctx.enter_context(ExitStack()), []

        def sem(name):
            used.append(sems.enter_context(nc.semaphore(name)))
            return used[-1]
        sh.front_sem = sem
        sh.dma_sem = lambda name: ctx.enter_context(nc.semaphore(name))
        sh.ps = ctx.enter_context(nc.psum_tensor("ps", [128, 8, 512], F32))
        sh.ident = sb("ident", [128, 128])
        sh.w_loaded, sh.w_head, sh.w_split = sem("w_loaded"), sem("w_head"), sem("w_split")
        sh.fm_ready = sem("fm_ready")
        sh.g_loaded, sh.g_head, sh.g_split = sem("g_loaded"), sem("g_head"), sem("g_split")
        sh.fm_free = [sem("fm_free0"), sem("fm_free1")]
        sh.lg = sb("lg", [128, NT, NE])
        sh.wt = sb("wt", [128, 2, NT])
        sh.slots = sb("slots", [128, 2, NT], U32)
        sh.slot_idx = sb("slot_idx", [128, NB], U32)
        sh.eid = sb("eid", [1, NTILE], I32)
        with ExitStack() as dense:
            sh.xh = dense.enter_context(nc.sbuf_tensor("xh", [128, KC, TOK], F32R))
            sh.xl = dense.enter_context(nc.sbuf_tensor("xl", [128, KC, TOK], F32R))
            sh.slab_raw = dense.enter_context(nc.sbuf_tensor("slab_raw", [128, SLAB], F32))
            sh.slab_hi = dense.enter_context(nc.sbuf_tensor("slab_hi", [128, 2 * SLAB], F32R))
            sh.slab_lo = dense.enter_context(nc.sbuf_tensor("slab_lo", [128, 2 * SLAB], F32R))
            with ExitStack() as front:
                def fsb(name, shape, dt=F32):
                    return front.enter_context(nc.sbuf_tensor(name, shape, dt))
                sh.w_raw, sh.w_hi, sh.w_lo = weight_views(sh, 3, KC)
                stage_x(nc, sh)
                with ExitStack() as gla:
                    def gsb(name, shape, dt=F32):
                        return gla.enter_context(nc.sbuf_tensor(name, shape, dt))
                    sh.gaT = gsb("gaT", [LR, TOK])
                    sh.wa2 = gsb("wa2", [LR, 256])
                    sh.bga = gsb("bga", [128, 2])
                    sh.gnorm = gsb("gnorm", [128, 4])
                    sh.restart = gsb("restart", [128, TOK], BF16)
                    stage_conv(nc, sh)
                    stage_gla(nc, sh)
                sh.qbd = fsb("qbd", [128, 4, DB, H_FOX * DT])
                sh.kTs = fsb("kTs", [128, 4, DB * DT])
                sh.vs = fsb("vs", [DB * DT, BW])
                stage_fox(nc, sh)
                stage_fox_sample(nc, sh)
            if upto < 1:
                return
            sh.m = dense.enter_context(nc.sbuf_tensor("m", [128, KC, TOK], F32))
            stage_gates(nc, sh)
            stage_out(nc, sh)
        if upto < 2:
            return
        clear(nc, used)
        sems.close()
        with ExitStack() as experts:
            expert_buffers(nc, sh, experts)
            stage_route(nc, sh)
            stage_moe(nc, sh)
        stage_combine(nc, sh)


_INS = ['x_prompt', 'x_sample', 'cache_fox_k', 'cache_fox_v', 'cache_fox_logf', 'state_gla', 'state_conv',
        'page_table', 'w_in', 'w_gla_a2', 'b_gla_a', 'gla_norm_g', 'b_fox_f', 'conv_w', 'w_branch', 'w_out',
        'ln1_g', 'ln1_b', 'w_router', 'b_router', 'w_e_gate', 'w_e_up', 'w_e_down', 'ln2_g', 'ln2_b']
_OUTS = [('y_prompt', (1, 1024, 1024)), ('y_sample', (8, 8, 1024)),
         ('prompt_fox_k', (1, 1, 1024, 8, 64)), ('prompt_fox_v', (1, 1, 1024, 8, 64)),
         ('prompt_fox_logf', (1, 1, 1024, 8)), ('prompt_gla', (1, 1, 4, 64, 128)), ('prompt_conv', (1, 1, 2, 512)),
         ('sample_fox_k', (1, 8, 8, 8, 64)), ('sample_fox_v', (1, 8, 8, 8, 64)), ('sample_fox_logf', (1, 8, 8, 8)),
         ('sample_gla', (1, 8, 4, 64, 128)), ('sample_conv', (1, 8, 2, 512))]


def kernel(**inputs):
    import numpy as _np
    import concourse.bacc as _bacc
    from concourse import mybir as _mybir
    from concourse.bass_utils import run_bass_kernel_spmd as _run

    nc = _bacc.Bacc("TRN2", target_bir_lowering=False, num_devices=1)
    arrays, ins, outs = {}, {}, {}
    for name in _INS:
        a = _np.ascontiguousarray(inputs[name])
        arrays[f"in_{name}"] = a
        ins[name] = nc.dram_tensor(f"in_{name}", a.shape, _mybir.dt.from_np(a.dtype), kind="ExternalInput").ap()
    for name, shape in _OUTS:
        outs[name] = nc.dram_tensor(f"out_{name}", shape, _mybir.dt.float32, kind="ExternalOutput").ap()
    build(nc, ins, outs)
    r = _run(nc, [arrays], core_ids=[0])
    return tuple(r.results[0][f"out_{name}"] for name, _ in _OUTS)
```
